# Optimizing a Trainium2 kernel written in Bass

```python
import functools
import jax, jax.numpy as jnp
from jax import lax
import numpy as np

D_MODEL = 1024
BATCH = 1
SEQ = 512
DEPTH = 1
DEC_BATCH = 1
DEC_SEQ = 32
PAST_LEN = 1024

CHUNK = 64
Q_BLOCK = 128
EPS = 1e-6
ROPE_THETA = 10000.0
A_WIDTH = D_MODEL // 2
A_HD = 64
A_HEADS = A_WIDTH // A_HD
A_KV = 2
IDX_HEADS = 4
IDX_DIM = 64
INDEX_TOPK = 256
B_WIDTH = D_MODEL - A_WIDTH
B_HEADS = 4
B_DV = B_WIDTH // B_HEADS
B_DK = B_DV // 2
GATE_RANK = 16
GATE_TAU = 16.0
N_EXPERTS = 32
TOP_K = 4
D_FF = D_MODEL
SWIGLU_LIMIT = 7.0
SWIGLU_ALPHA = 1.702
MOE_BLOCK = 128
IN_WIDTHS = (A_HEADS * A_HD, A_KV * A_HD, A_KV * A_HD, IDX_HEADS * IDX_DIM, IDX_DIM, IDX_HEADS,
             B_HEADS * B_DK, B_HEADS * B_DK, B_HEADS * B_DV, GATE_RANK, B_WIDTH)
D_IN = sum(IN_WIDTHS)

kernel_name = 'hybrid_dsa_gla_moe_stream_step'

def rms_norm(x, g):
    xf = x.astype(jnp.float32)
    y = xf * lax.rsqrt(jnp.mean(xf * xf, axis=-1, keepdims=True) + EPS)
    return (y * g.astype(jnp.float32)).astype(x.dtype)

def adaln_params(c, w, b, n):
    mod = jax.nn.silu(c) @ w + b
    return jnp.split(mod[:, None, :], n, axis=-1)

def modulate(h, shift, scale):
    return h * (1 + scale) + shift

def rope(x, pos):
    half = x.shape[-1] // 2
    inv_freq = ROPE_THETA ** (-jnp.arange(half, dtype=jnp.float32) / half)
    ang = pos.astype(jnp.float32)[:, None] * inv_freq[None, :]
    cos = jnp.cos(ang)[None, :, None, :]
    sin = jnp.sin(ang)[None, :, None, :]
    xf = x.astype(jnp.float32)
    x1, x2 = xf[..., :half], xf[..., half:]
    return jnp.concatenate([x1 * cos - x2 * sin, x2 * cos + x1 * sin], axis=-1).astype(x.dtype)

def project_mixer_inputs(h, w_in, w_gate, b_gate, pos):
    b, t, _ = h.shape
    offs, acc = [], 0
    for w in IN_WIDTHS[:-1]:
        acc += w
        offs.append(acc)
    qa, ka, va, qi, ki, wi, qg, kg, vg, lr, rg = jnp.split(h @ w_in, offs, axis=-1)
    qa = rope(qa.reshape(b, t, A_HEADS, A_HD), pos)
    ka = rope(ka.reshape(b, t, A_KV, A_HD), pos)
    va = va.reshape(b, t, A_KV, A_HD)
    qi = rope(qi.reshape(b, t, IDX_HEADS, IDX_DIM), pos)
    ki = rope(ki.reshape(b, t, 1, IDX_DIM), pos)[:, :, 0]
    wi = wi * IDX_HEADS ** -0.5
    qg = qg.reshape(b, t, B_HEADS, B_DK) * B_DK ** -0.5
    kg = kg.reshape(b, t, B_HEADS, B_DK)
    vg = vg.reshape(b, t, B_HEADS, B_DV)
    gg = (jax.nn.log_sigmoid((lr @ w_gate + b_gate).astype(jnp.float32)) / GATE_TAU).reshape(b, t, B_HEADS, B_DK)
    return qa, ka, va, qi, ki, wi, qg, kg, vg, gg, rg

def dsa_attend(q, qi, wi, key_lim, k_all, v_all, ki_all, top_k):
    b, nq, nh, hd = q.shape
    n_keys = k_all.shape[1]
    rel = jax.nn.relu(jnp.einsum('bqhd,bld->bqhl', qi, ki_all).astype(jnp.float32))
    iscore = jnp.einsum('bqh,bqhl->bql', wi.astype(jnp.float32), rel)
    admissible = jnp.arange(n_keys)[None, :] < key_lim[:, None]
    iscore = jnp.where(admissible[None], iscore, -jnp.inf)
    _, sel = lax.top_k(iscore, top_k)
    valid = sel < key_lim[None, :, None]
    bidx = jnp.arange(b)[:, None, None]
    k_sel = k_all[bidx, sel]
    v_sel = v_all[bidx, sel]
    qh = q.reshape(b, nq, A_KV, nh // A_KV, hd)
    logits = jnp.einsum('bqgrd,bqkgd->bqgrk', qh, k_sel).astype(jnp.float32) * hd ** -0.5
    logits = jnp.where(valid[:, :, None, None, :], logits, -jnp.inf)
    p = jax.nn.softmax(logits, axis=-1)
    o = jnp.einsum('bqgrk,bqkgd->bqgrd', p.astype(v_sel.dtype), v_sel)
    return o.reshape(b, nq, nh, hd)

def gla_chunk(state, q, k, v, g):
    c = q.shape[1]
    qf, kf, vf = q.astype(jnp.float32), k.astype(jnp.float32), v.astype(jnp.float32)
    bcum = jnp.cumsum(g, axis=1)
    causal = jnp.arange(c)[:, None] >= jnp.arange(c)[None, :]
    diff = bcum[:, :, None] - bcum[:, None, :]
    decay = jnp.exp(jnp.where(causal[None, :, :, None, None], diff, -jnp.inf))
    scores = jnp.einsum('bthd,bshd,btshd->bhts', qf, kf, decay)
    o = (jnp.einsum('bhts,bshv->bthv', scores, vf)
         + jnp.einsum('bthd,bhdv->bthv', qf * jnp.exp(bcum), state))
    b_last = bcum[:, -1]
    new_state = (jnp.exp(b_last)[..., None] * state
                 + jnp.einsum('bshd,bshv->bhdv', kf * jnp.exp(b_last[:, None] - bcum), vf))
    return new_state, o

def merge_groups(oa, ob, rg, g_out, w_out):
    b, t = oa.shape[:2]
    ob = rms_norm(ob, g_out).reshape(b, t, B_WIDTH).astype(rg.dtype) * jax.nn.silu(rg)
    return jnp.concatenate([oa.reshape(b, t, A_WIDTH).astype(rg.dtype), ob], axis=-1) @ w_out

def mix_prompt(w_in, w_gate, b_gate, g_out, w_out, h):
    b, s, _ = h.shape
    pos = jnp.arange(s)
    qa, ka, va, qi, ki, wi, qg, kg, vg, gg, rg = project_mixer_inputs(h, w_in, w_gate, b_gate, pos)
    n_qb = s // Q_BLOCK
    key_lim = (pos // CHUNK + 1) * CHUNK
    top_k = min(INDEX_TOPK, s // 4)

    def qblocks(a):
        return a.reshape(b, n_qb, Q_BLOCK, *a.shape[2:]).swapaxes(0, 1)

    oa = lax.map(lambda args: dsa_attend(*args, ka, va, ki, top_k),
                 (qblocks(qa), qblocks(qi), qblocks(wi), key_lim.reshape(n_qb, Q_BLOCK)))
    oa = oa.swapaxes(0, 1).reshape(b, s, A_HEADS, A_HD)
    n_c = s // CHUNK

    def chunks(a):
        return a.reshape(b, n_c, CHUNK, *a.shape[2:]).swapaxes(0, 1)

    state0 = jnp.zeros((b, B_HEADS, B_DK, B_DV), jnp.float32)
    state, ob = lax.scan(lambda st, xs_: gla_chunk(st, *xs_), state0,
                         (chunks(qg), chunks(kg), chunks(vg), chunks(gg)))
    ob = ob.swapaxes(0, 1).reshape(b, s, B_HEADS, B_DV)
    y = merge_groups(oa, ob, rg, g_out, w_out)
    return y, (ka, va, ki, state.astype(h.dtype))

def mix_sample(cache_k, cache_v, cache_kidx, state, w_in, w_gate, b_gate, g_out, w_out, h):
    b, t, _ = h.shape
    past = cache_k.shape[1]
    pos = past + jnp.arange(t)
    qa, ka, va, qi, ki, wi, qg, kg, vg, gg, rg = project_mixer_inputs(h, w_in, w_gate, b_gate, pos)
    k_all = jnp.concatenate([cache_k.astype(ka.dtype), ka], axis=1)
    v_all = jnp.concatenate([cache_v.astype(va.dtype), va], axis=1)
    ki_all = jnp.concatenate([cache_kidx.astype(ki.dtype), ki], axis=1)
    n_keys = past + t
    key_lim = jnp.full((t,), n_keys, jnp.int32)
    oa = dsa_attend(qa, qi, wi, key_lim, k_all, v_all, ki_all, min(INDEX_TOPK, n_keys // 4))
    new_state, ob = gla_chunk(state.astype(jnp.float32), qg, kg, vg, gg)
    y = merge_groups(oa, ob, rg, g_out, w_out)
    return y, (ka, va, ki, new_state.astype(state.dtype))

def expert_ffn(xb, w_gu, b_gu, w_dn, b_dn):
    gu = xb @ w_gu + b_gu
    gate = jnp.minimum(gu[..., :D_FF], SWIGLU_LIMIT)
    up = jnp.clip(gu[..., D_FF:], -SWIGLU_LIMIT, SWIGLU_LIMIT)
    glu = gate * jax.nn.sigmoid(gate * SWIGLU_ALPHA)
    return ((up + 1) * glu) @ w_dn + b_dn

def moe_ffn(h, w_router, b_router, w_gu, b_gu, w_dn, b_dn):
    b, t, d = h.shape
    hf = h.reshape(-1, d)
    n_tok = hf.shape[0]
    logits = (hf @ w_router + b_router).astype(jnp.float32)
    top_v, top_e = lax.top_k(logits, TOP_K)
    gates = jax.nn.softmax(top_v, axis=-1)
    n_asg = n_tok * TOP_K
    n_blocks = -(-n_asg // MOE_BLOCK) + N_EXPERTS
    n_slots = n_blocks * MOE_BLOCK
    flat_e = top_e.reshape(-1)
    order = jnp.argsort(flat_e)
    e_sorted = flat_e[order]
    tok_sorted = order // TOP_K
    g_sorted = gates.reshape(-1)[order]
    counts = jnp.bincount(flat_e, length=N_EXPERTS)
    padded = (counts + MOE_BLOCK - 1) // MOE_BLOCK * MOE_BLOCK
    pad_end = jnp.cumsum(padded)
    pad_start = pad_end - padded
    start = jnp.cumsum(counts) - counts
    dest = pad_start[e_sorted] + jnp.arange(n_asg) - start[e_sorted]
    slot_tok = jnp.full((n_slots,), n_tok, jnp.int32).at[dest].set(tok_sorted.astype(jnp.int32))
    slot_gate = jnp.zeros((n_slots,), jnp.float32).at[dest].set(g_sorted)
    block_expert = jnp.minimum(
        jnp.searchsorted(pad_end, jnp.arange(n_blocks) * MOE_BLOCK, side='right'), N_EXPERTS - 1)
    h_pad = jnp.concatenate([hf, jnp.zeros((1, d), hf.dtype)], axis=0)
    xs = h_pad[slot_tok].reshape(n_blocks, MOE_BLOCK, d)
    ys = lax.map(lambda args: expert_ffn(args[0], w_gu[args[1]], b_gu[args[1]], w_dn[args[1]], b_dn[args[1]]),
                 (xs, block_expert)).reshape(n_slots, d)
    out = jax.ops.segment_sum(ys * slot_gate[:, None].astype(ys.dtype), slot_tok,
                              num_segments=n_tok + 1)[:n_tok]
    return out.reshape(b, t, d)

def trunk_layer(x, c, mixer, w_mod, b_mod, g_mix, g_ffn, w_router, b_router, w_gu, b_gu, w_dn, b_dn):
    sh1, sc1, gt1, sh2, sc2, gt2 = adaln_params(c, w_mod, b_mod, 6)
    y, new_state = mixer(modulate(rms_norm(x, g_mix), sh1, sc1))
    x = x + gt1 * y
    x = x + gt2 * moe_ffn(modulate(rms_norm(x, g_ffn), sh2, sc2), w_router, b_router, w_gu, b_gu, w_dn, b_dn)
    return x, new_state

def final_norm(x, c, w_mod_final, b_mod_final, g_final):
    shift, scale = adaln_params(c, w_mod_final, b_mod_final, 2)
    return modulate(rms_norm(x, g_final), shift, scale)

def setup_inputs(seed: int = 0) -> dict:
    key = jax.random.key(seed)
    ks = jax.random.split(key, 32)

    def nrm(k, shape, scale):
        return jax.random.normal(k, shape, jnp.float32) * scale

    d_mix = A_WIDTH + B_WIDTH
    return {
        'x_prompt': nrm(ks[0], (BATCH, SEQ, D_MODEL), 1.0),
        'x_sample': nrm(ks[1], (DEC_BATCH, DEC_SEQ, D_MODEL), 1.0),
        'cache_k': nrm(ks[2], (DEPTH, DEC_BATCH, PAST_LEN, A_KV, A_HD), 1.0),
        'cache_v': nrm(ks[3], (DEPTH, DEC_BATCH, PAST_LEN, A_KV, A_HD), 1.0),
        'cache_kidx': nrm(ks[4], (DEPTH, DEC_BATCH, PAST_LEN, IDX_DIM), 1.0),
        'state_gla': nrm(ks[5], (DEPTH, DEC_BATCH, B_HEADS, B_DK, B_DV), 0.3),
        'c_prompt': nrm(ks[6], (BATCH, D_MODEL), 1.0),
        'c_sample': nrm(ks[7], (DEC_BATCH, D_MODEL), 1.0),
        'w_mod': nrm(ks[8], (DEPTH, D_MODEL, 6 * D_MODEL), 0.5 * D_MODEL ** -0.5),
        'b_mod': nrm(ks[9], (DEPTH, 6 * D_MODEL), 0.02),
        'g_mix': 1.0 + nrm(ks[10], (DEPTH, D_MODEL), 0.02),
        'g_ffn': 1.0 + nrm(ks[11], (DEPTH, D_MODEL), 0.02),
        'w_in': nrm(ks[12], (DEPTH, D_MODEL, D_IN), D_MODEL ** -0.5),
        'gla_w_gate': nrm(ks[13], (DEPTH, GATE_RANK, B_HEADS * B_DK), GATE_RANK ** -0.5),
        'gla_b_gate': nrm(ks[14], (DEPTH, B_HEADS * B_DK), 0.1),
        'gla_g_out': 1.0 + nrm(ks[15], (DEPTH, B_DV), 0.02),
        'w_out': nrm(ks[16], (DEPTH, d_mix, D_MODEL), d_mix ** -0.5),
        'w_router': nrm(ks[17], (DEPTH, D_MODEL, N_EXPERTS), D_MODEL ** -0.5),
        'b_router': nrm(ks[18], (DEPTH, N_EXPERTS), 0.01),
        'w_gate_up': nrm(ks[19], (DEPTH, N_EXPERTS, D_MODEL, 2 * D_FF), D_MODEL ** -0.5),
        'b_gate_up': nrm(ks[20], (DEPTH, N_EXPERTS, 2 * D_FF), 0.01),
        'w_down': nrm(ks[21], (DEPTH, N_EXPERTS, D_FF, D_MODEL), D_FF ** -0.5),
        'b_down': nrm(ks[22], (DEPTH, N_EXPERTS, D_MODEL), 0.01),
        'w_mod_final': nrm(ks[23], (D_MODEL, 2 * D_MODEL), 0.5 * D_MODEL ** -0.5),
        'b_mod_final': nrm(ks[24], (2 * D_MODEL,), 0.02),
        'g_final': 1.0 + nrm(ks[25], (D_MODEL,), 0.02),
    }

def reference(x_prompt, x_sample, cache_k, cache_v, cache_kidx, state_gla, c_prompt, c_sample,
              w_mod, b_mod, g_mix, g_ffn, w_in, gla_w_gate, gla_b_gate, gla_g_out, w_out,
              w_router, b_router, w_gate_up, b_gate_up, w_down, b_down,
              w_mod_final, b_mod_final, g_final):
    xp, xs = x_prompt, x_sample
    kp_l, vp_l, kip_l, sp_l = [], [], [], []
    ks_l, vs_l, kis_l, ss_l = [], [], [], []
    for l in range(DEPTH):
        mix_w = (w_in[l], gla_w_gate[l], gla_b_gate[l], gla_g_out[l], w_out[l])
        blk_w = (w_mod[l], b_mod[l], g_mix[l], g_ffn[l], w_router[l], b_router[l],
                 w_gate_up[l], b_gate_up[l], w_down[l], b_down[l])
        xp, (kp, vp, kip, sp) = trunk_layer(xp, c_prompt, functools.partial(mix_prompt, *mix_w), *blk_w)
        xs, (kn, vn, kin, sn) = trunk_layer(
            xs, c_sample,
            functools.partial(mix_sample, cache_k[l], cache_v[l], cache_kidx[l], state_gla[l], *mix_w),
            *blk_w)
        kp_l.append(kp); vp_l.append(vp); kip_l.append(kip); sp_l.append(sp)
        ks_l.append(kn); vs_l.append(vn); kis_l.append(kin); ss_l.append(sn)
    y_prompt = final_norm(xp, c_prompt, w_mod_final, b_mod_final, g_final)
    y_sample = final_norm(xs, c_sample, w_mod_final, b_mod_final, g_final)
    return (y_prompt, y_sample,
            jnp.stack(kp_l), jnp.stack(vp_l), jnp.stack(kip_l), jnp.stack(sp_l),
            jnp.stack(ks_l), jnp.stack(vs_l), jnp.stack(kis_l), jnp.stack(ss_l))


_drawn_inputs = setup_inputs


def setup_inputs(seed=0):
    import zlib

    import numpy as np

    out = dict(_drawn_inputs(seed))
    spreads = {}
    factors = {'state_gla': 3.443,
     'g_ffn': 3.746,
     'gla_g_out': 8.0,
     'b_router': 6.035,
     'b_gate_up': 8.0,
     'b_down': 64.0,
     'g_final': 8.437,
     'b_mod_final': 2.897}
    for name, (base, spread) in spreads.items():
        noise = np.random.default_rng([zlib.crc32(name.encode()), seed]).standard_normal(out[name].shape)
        drawn = base * np.exp(spread * noise) if base else spread * noise
        out[name] = __import__('jax').numpy.asarray(drawn.astype(out[name].dtype))
    for name, factor in factors.items():
        out[name] = (out[name] * factor).astype(out[name].dtype)
    return out
```

```python
from contextlib import ExitStack

import concourse.bass as bass
from concourse import mybir

F32 = mybir.dt.float32
I32 = mybir.dt.int32
U32 = mybir.dt.uint32
ALU = mybir.AluOpType
ACT = mybir.ActivationFunctionType
AX = mybir.AxisListType

P = 128
D = 1024
KD = D // P
SEQ, DEC, PAST = 512, 32, 1024
NTOK = SEQ + DEC
T = 5
ROWS = [P, P, P, P, DEC]
TOK = [0, 128, 256, 384, 512]
SAMPLE = 4
HD = 64
NH, NIH, NBH, DV = 8, 4, 4, 128
NKEYS = [128, 256, 384, 512, PAST + DEC]
TOPK_PROMPT, TOPK_SAMPLE = min(256, SEQ // 4), min(256, (PAST + DEC) // 4)
CHUNK = 64
NE, TOPE = 32, 4
NOV = NTOK * TOPE // P - 1
NBLK = NE + NOV + 1
EPS = 1e-6
NEG = -3.0e38
MASKED = -1.0e30
CW = 512
SLOT = KD * CW
RING, FRONT_RING = 6, 3
LIMIT, ALPHA = 7.0, 1.702

QA, KA, VA, QI, KI, WI, QG, KG, VG, LR, RG = 0, 512, 640, 768, 1024, 1088, 1092, 1348, 1604, 2116, 2132
ORDER = [SAMPLE, 0, 1, 2, 3]
UNITS = [(SAMPLE, 0), (SAMPLE, 1)] + [(t, h) for t in range(4) for h in range(NH)]
LAST = [NH - 1] * 4 + [1]
UNIT = {x: u for u, x in enumerate(UNITS)}


def front_chunks():
    c, m = [("mod", n) for n in range(4)], 4
    for x, more in (("qi", 2), ("kv", 3), ("qa", 3), ("qkg", 2), ("vg", 2), ("rg", 0)):
        c += [(x, 0)] + [("mod", m + n) for n in range(more)]
        m += more
    return c + [("out", 0), ("out", 1)]


def steps():
    s = [("c",)]
    for n in range(4):
        s += [("mod", n), ("modT", n)]
    s += [("xT", k) for k in range(KD)]
    s += [("qi", t) for t in ORDER]
    s += [("qiT", t) for t in ORDER]
    s += [("cacheT", i) for i in range(PAST // P)]
    s += [("mod", 4), ("mod", 5)]
    for t in ORDER:
        for h in range(NIH):
            s.append(("idx", t, h))
            if t == SAMPLE:
                s.append(("idxnew", t, h))
    s += [("kv", t) for t in ORDER] + [("lr",), ("mod", 6), ("mod", 7), ("mod", 8)]
    s += [("qa", t) for t in ORDER] + [("mod", 9), ("mod", 10), ("mod", 11)]
    s += [("qaT", t) for t in ORDER]
    s += [("qkg", j) for j in range(4)] + [("mod", 12), ("mod", 13)]
    s += [("vg", t) for t in ORDER] + [("mod", 14), ("mod", 15)]
    s += [("z", j) for j in range(2)]
    s += [("rg", t) for t in ORDER]
    s += [("kd", t) for t in range(T)]
    gla = []
    for t in range(T):
        gla += [("gs", t), ("gst", t, 0)]
        if t != SAMPLE:
            gla += [("gst", t, 1)]
        gla += [("gi", t), ("go", t)]
    for u in range(len(UNITS) + 3):
        if u < len(UNITS):
            s.append(("sc", *UNITS[u]))
            if UNITS[u][0] == SAMPLE:
                s.append(("scnew", *UNITS[u]))
        if 2 <= u < len(UNITS) + 2:
            s.append(("pT", *UNITS[u - 2]))
            if UNITS[u - 2][0] == SAMPLE:
                s.append(("pTnew", *UNITS[u - 2]))
        s += gla[:1]
        gla = gla[1:]
        if u >= 3:
            s.append(("pv", *UNITS[u - 3]))
    assert not gla
    s += [("catT", t) for t in range(T)]
    s.append(("y", 0))
    for t in range(T):
        if t + 1 < T:
            s.append(("y", t + 1))
        s += [("hT", t), ("rt", t)]
    s += [("rank",)]
    return s


STEPS = steps()
JOB = {s: j for j, s in enumerate(STEPS)}
NJOBS = len(STEPS)


class Carver:

    def __init__(self, ap, words):
        self.ap, self.at, self.words = ap, 0, words

    def take(self, words):
        assert self.at + words <= self.words, (self.at, words, self.words)
        self.at += words
        return self.ap[:, self.at - words:self.at]


def build(nc, a, outs):
    (y_prompt, y_sample, k_prompt, v_prompt, ki_prompt, gla_prompt, k_sample, v_sample, ki_sample,
     gla_sample) = outs
    ctx = ExitStack()
    with ctx:
        def sem(name):
            return ctx.enter_context(nc.semaphore(name))

        def dram(name, shape, dt=F32):
            return nc.dram_tensor(name, shape, dt, kind="Internal").ap()

        mod_dram = dram("mod_dram", [2, 8 * D])
        x2_dram = dram("x2_dram", [NTOK, D])
        h_dram = dram("h_dram", [NTOK, D])
        slot_dram = dram("slot_dram", [P * NBLK, 1], I32)
        ys_dram = dram("ys_dram", [(NE + NOV) * P, D])

        ring = ctx.enter_context(nc.sbuf_tensor("ring", [P, RING * SLOT], F32))
        KEEP, WORK = 1362, 27200
        keep_t = ctx.enter_context(nc.sbuf_tensor("keep", [P, KEEP], F32))
        work_t = ctx.enter_context(nc.sbuf_tensor("work", [P, WORK], F32))
        psum = ctx.enter_context(nc.psum_tensor("psum", [P, 8, 512], F32))

        def slot(n):
            return ring[:, n * SLOT:(n + 1) * SLOT]

        def wslot(n):
            return slot(n).rearrange("p (k n) -> p k n", k=KD)

        keep = Carver(keep_t, KEEP)
        ident = keep.take(P)
        before = keep.take(P)
        ones = keep.take(P)
        gates = keep.take(T * TOPE)
        chosen = keep.take(T * TOPE)
        ys_row = keep.take(T * TOPE).bitcast(I32)
        tab_pos = keep.take(T * TOPE).bitcast(I32)
        tok_id = keep.take(8).bitcast(I32)
        slot_tok = keep.take(NBLK).bitcast(I32)
        over = keep.take(NOV + 1).bitcast(I32)
        small = keep.take(300)
        sel = keep.take(T * NE)
        iota_e = keep.take(NE)
        idx_now = keep.take(1).bitcast(I32)
        pick2 = keep.take(2)
        zero_i = keep.take(NBLK).bitcast(I32)

        hi = Carver(ring[:, FRONT_RING * SLOT:RING * SLOT], (RING - FRONT_RING) * SLOT)
        lo = Carver(work_t, WORK)
        hT = lo.take(KD * NTOK).rearrange("p (k n) -> p k n", k=KD)
        qiT = lo.take(2 * NTOK).rearrange("p (k n) -> p k n", k=2)
        kiT = lo.take(NTOK)
        qaT = lo.take(4 * NTOK).rearrange("p (k n) -> p k n", k=4)
        kaT = lo.take(NTOK)
        va = lo.take(T * P).rearrange("p (t n) -> p t n", t=T)
        score = [lo.take(n) for n in NKEYS]
        kiTs = lo.take(PAST + DEC)
        kTs = lo.take(PAST + DEC)
        Vs = lo.take(9 * P).rearrange("p (t n) -> p t n", t=9)
        cs = lo.take(T * 128).rearrange("p (t n) -> p t n", t=T)
        gmask = lo.take(256).bitcast(I32)
        gout_b = lo.take(P)
        wgate = lo.take(256)
        vT = lo.take(16)
        cT = lo.take(16)
        colT = lo.take(32)
        a1 = lo.take(16)
        cc = lo.take(P)
        csg = lo.take(P)
        vecs = lo.take(P)
        wis = lo.take(T * 4).rearrange("p (t n) -> p t n", t=T)
        m8 = lo.take(8)
        lrT = lo.take(NTOK)
        gT2 = lo.take(NTOK)
        vg = hi.take(T * 512).rearrange("p (t n) -> p t n", t=T)
        rg = hi.take(T * 512).rearrange("p (t n) -> p t n", t=T)
        xs5 = ring[:, FRONT_RING * SLOT:FRONT_RING * SLOT + T * D].rearrange("p (t n) -> p t n", t=T)
        catA = hi.take(T * 512).rearrange("p (t n) -> p t n", t=T)
        qaro = catA
        catA_flat = catA.rearrange("p t n -> p (t n)")
        qgT = hi.take(2 * NTOK).rearrange("p (k n) -> p k n", k=2)
        kgT = hi.take(2 * NTOK).rearrange("p (k n) -> p k n", k=2)
        STAGE = 9280
        pr = Carver(lo.take(STAGE), STAGE)
        qro = pr.take(T * 320).rearrange("p (t n) -> p t n", t=T)
        qiraw = [pr.take(324), pr.take(324)]
        raw = [pr.take(512), pr.take(512)]
        kro = pr.take(T * P).rearrange("p (t n) -> p t n", t=T)
        prefix = pr.take(2048)
        rel = [prefix[:, 0:1024], prefix[:, 1024:2048]]
        rope_p = pr.take(512)
        ckidx = pr.take(8 * 64).rearrange("p (t n) -> p t n", t=8)
        ck = pr.take(8 * 128).rearrange("p (t n) -> p t n", t=8)
        modrow = [pr.take(CW), pr.take(CW)]
        cache_flat = pr.ap[:, pr.at - 2 * CW - 1536:pr.at - 2 * CW]
        bmod = [catA_flat[:, n * CW:(n + 1) * CW] for n in range(FRONT_RING)]
        bmod2 = [cache_flat[:, n * CW:(n + 1) * CW] for n in range(FRONT_RING)]
        twork = hi.take(PAST + DEC)
        gl = Carver(pr.ap, STAGE)
        bT = gl.take(2 * NTOK).rearrange("p (k n) -> p k n", k=2)
        gqA = gl.take(2 * NTOK).rearrange("p (k n) -> p k n", k=2)
        gk0 = gl.take(2 * NTOK).rearrange("p (k n) -> p k n", k=2)
        gk1 = gl.take(2 * SEQ).rearrange("p (k n) -> p k n", k=2)
        gqe = gl.take(2 * NTOK).rearrange("p (k n) -> p k n", k=2)
        gkd = gl.take(2 * NTOK).rearrange("p (k n) -> p k n", k=2)
        kdn = gl.take(T * 256).rearrange("p (t n) -> p t n", t=T)
        states = [gl.take(256).rearrange("p (j n) -> p j n", j=2) for _ in range(6)]
        scT = [hi.take(256), hi.take(256)]
        ot = hi.take(512)
        eL = lo.take(18).rearrange("p (j n) -> p j n", j=2)
        at = Carver(hT.rearrange("p k n -> p (k n)"), KD * NTOK)
        prob = [at.take(PAST + DEC) for _ in range(3)]
        gT1 = [qiT[:, 0, :], qiT[:, 1, :]]
        graw = [kiTs[:, 0:512], kiTs[:, 512:1024]]
        pTs = [(qiT.rearrange("p k n -> p (k n)")[:, 0:1024], kiT[:, 0:P]), (kiTs[:, 0:1024], kiT[:, P:2 * P])]
        qaTs = csg
        osum = [cc[:, 0:64], cc[:, 64:128]]
        pT = [at.take(512), at.take(512)]
        amx = at.take(16)
        ars = at.take(16)
        op = Carver(work_t, WORK)
        catT = op.take(KD * NTOK).rearrange("p (k n) -> p k n", k=KD)
        rowP = [op.take(D) for _ in range(3)]
        rowS = [op.take(D) for _ in range(3)]
        gffn_b = op.take(D)
        xin = [op.take(D), op.take(D)]
        x2b = [op.take(D), op.take(D)]
        h2b = [op.take(D), op.take(D)]
        junk = op.take(D)
        h2T = op.take(D)
        wr = op.take(KD * NE).rearrange("p (k n) -> p k n", k=KD)
        br_b = op.take(NE)
        oneh = op.take(T * TOPE * NE)
        rank = op.take(T * NE + NE)
        tmpn = op.take(NOV * NE)
        iota_j = op.take(NOV * NE)
        xb_, xe_, xst = op.take(NE), op.take(NE), op.take(NE)
        rj = op.take(NE)
        pick_t = op.take(T * TOPE * NE)
        ex = Carver(work_t, WORK)
        xg = ex.take(D)
        xgT = ex.take(D).rearrange("p (k n) -> p k n", k=KD)
        act = ex.take(D)
        actT = ex.take(D).rearrange("p (k n) -> p k n", k=KD)
        eg, eu, es = ex.take(512), ex.take(512), ex.take(512)
        ysb = ex.take(D)
        brow = ex.take(3 * D)
        bias_b = ex.take(3 * D)
        fi = Carver(ring, RING * SLOT)
        yg = [fi.take(4 * D), fi.take(4 * D)]
        xf = [fi.take(D), fi.take(D)]
        fo = [fi.take(D), fi.take(D)]
        facc = fi.take(D)
        fP = [fi.take(D) for _ in range(3)]
        fS = [fi.take(D) for _ in range(3)]
        gfin_b = fi.take(D)

        sm = Carver(small, 300)
        ss, vv, rr, r2, r3 = (sm.take(8) for _ in range(5))
        ss4, vv4, rr4 = (sm.take(4) for _ in range(3))
        cgt, thr8, ngate = sm.take(1), sm.take(8), sm.take(1)
        v8 = sm.take(8)
        i8 = sm.take(8).bitcast(U32)
        e4 = sm.take(4)
        gs1, gr1 = sm.take(1), sm.take(1)
        nR = T * TOPE
        f1, f2, f3, f4, f5, f6, f7 = (sm.take(nR) for _ in range(7))
        negm = sm.take(16)
        rinv = sm.take(16)
        two = sm.take(2)
        ovf = sm.take(NOV + 1)

        psum_filled = sem("psum_filled")
        psum_drained = [sem(f"psum_drained{g}") for g in range(4)]
        loaded = [sem(f"loaded{n}") for n in range(RING)]
        consts = sem("consts")
        c_in, x_in, cache_in, tabs_in = sem("c_in"), sem("x_in"), sem("cache_in"), sem("tabs_in")
        c_sig, c_silu = sem("c_sig"), sem("c_silu")
        x_sq, x_var, x_sqrt, x_norm = sem("x_sq"), sem("x_var"), sem("x_sqrt"), sem("x_norm")
        mod_copied, bias_clear = sem("mod_copied"), sem("bias_clear")
        mod_stored = [sem("mod_stored0"), sem("mod_stored1")]
        a1_made = sem("a1_made")
        qi_roped, raw_used = sem("qi_roped"), sem("raw_used")
        rel_used = sem("rel_used")
        masks_made, mask_spread = sem("masks_made"), sem("mask_spread")
        act_s = sem("act_order")
        dve_s = sem("dve_order")
        pool_s = sem("pool_order")
        new_keys = sem("new_keys")
        out_kv, out_ki, out_state = sem("out_kv"), sem("out_ki"), sem("out_state")
        rg_gated = sem("rg_gated")
        gate_z, gate_l = sem("gate_z"), sem("gate_l")
        gla_in, gla_exp, gla_made = sem("gla_in"), sem("gla_exp"), sem("gla_made")
        state_in = sem("state_in")
        o_sum, o_sq, o_var, o_sqrt, o_done = (sem(n) for n in ("o_sum", "o_sq", "o_var", "o_sqrt", "o_done"))
        logits_max, probs_made = sem("logits_max"), sem("probs_made")
        rows_in, x_again = sem("rows_in"), [sem("x_again0"), sem("x_again1")]
        rows_made = sem("rows_made")
        x2_made, x2_sq, x2_var, x2_sqrt, h2_made = (sem(n) for n in ("x2_made", "x2_sq", "x2_var", "x2_sqrt", "h2_made"))
        x2_stored = [sem("x2_stored0"), sem("x2_stored1")]
        h2_stored = [sem("h2_stored0"), sem("h2_stored1")]
        top_ready, gate_exp, sel_made = sem("top_ready"), sem("gate_exp"), sem("sel_made")
        routed, tab_zero, tab_written, tab_in = sem("routed"), sem("tab_zero"), sem("tab_written"), sem("tab_in")
        chunk_done = sem("chunk_done")
        bias_in, bias_ready, bias_gu_used, bias_dn_used = (sem(n) for n in ("bias_in", "bias_ready", "bias_gu_used", "bias_dn_used"))
        gathered, xg_turned, xgT_ready = sem("gathered"), sem("xg_turned"), sem("xgT_ready")
        gate_added, gate_sig, act_ready = sem("gate_added"), sem("gate_sig"), sem("act_ready")
        act_turned, actT_ready = sem("act_turned"), sem("actT_ready")
        ys_ready, ys_stored = sem("ys_ready"), sem("ys_stored")
        xgT_half = sem("xgT_half")
        gu_added = sem("gu_added")
        fin_rows, fin_rows_made = sem("fin_rows"), sem("fin_rows_made")
        fin_x = [sem("fin_x0"), sem("fin_x1")]
        fin_y = [sem("fin_y0"), sem("fin_y1")]
        f_made, f_sq, f_var, f_sqrt, f_out = (sem(n) for n in ("f_made", "f_sq", "f_var", "f_sqrt", "f_out"))
        f_stored = [sem("f_stored0"), sem("f_stored1")]
        idx_copied = sem("idx_copied")
        ys_cleared = sem("ys_cleared")
        pool_settled = sem("pool_settled")
        ss_clear, gate_mask, iota_made = sem("ss_clear"), sem("gate_mask"), sem("iota_made")

        def note(eng, s):
            eng.sem_inc(s, 1)

        ROW_DMAS = 9

        class Order:

            def __init__(self, eng, s):
                self.eng, self.s, self.n = eng, s, 0

            def __call__(self, ins):
                self.n = self.n + 1
                ins.then_inc(self.s, 1)
                self.eng.wait_ge(self.s, self.n)

        def bank(j, b=0):
            return psum[:, 2 * (j % 4) + b, :]

        def group(j):
            return psum[:, 2 * (j % 4):2 * (j % 4) + 2, :].rearrange("p b n -> p (b n)")

        SPAN = {"qi": 81, "kv": 64, "qa": P, "vg": P, "rg": P, "y": P}

        def halves(ap):
            return ap.rearrange("p (b n) -> p b n", b=2)

        def turned(j):
            return psum[:, 2 * (j % 4):2 * (j % 4) + 2, 0:NTOK // 2]

        def filled(eng, j):
            eng.wait_ge(psum_filled, j + 1)

        def in_sbuf(eng, step):
            j = JOB[step]
            eng.wait_ge(psum_drained[j % 4], j // 4 + 1)

        def free_group(eng, j):
            if j >= 4:
                eng.wait_ge(psum_drained[j % 4], j // 4)

        chunks = front_chunks()
        CH = {c: n for n, c in enumerate(chunks)}
        NCH = len(chunks)
        assert NCH % FRONT_RING == 0
        last_step = {}
        for s in STEPS:
            key = {"mod": ("mod", s[1] if len(s) > 1 else 0), "lr": ("kv", 0), "qi": ("qi", 0), "kv": ("kv", 0),
                   "qa": ("qa", 0), "qkg": ("qkg", 0), "vg": ("vg", 0), "rg": ("rg", 0)}.get(s[0])
            if key:
                last_step[key] = s
            if s[0] == "y":
                last_step[("out", 0)] = last_step[("out", 1)] = s
        parts = [2 if c[0] in ("mod", "kv") else 1 for c in chunks]
        need = []
        tot = [0] * FRONT_RING
        for n in range(NCH):
            tot[n % FRONT_RING] += 16 * parts[n]
            need.append(tot[n % FRONT_RING])
        FRONT_TOTAL = tot + [0] * (RING - FRONT_RING)

        def chunk_in(eng, c):
            eng.wait_ge(loaded[CH[c] % FRONT_RING], need[CH[c]])

        w_in = a["w_in"][0].rearrange("(k p) n -> p k n", p=P)
        w_mod = a["w_mod"][0].rearrange("(k p) n -> p k n", p=P)
        w_modf = a["w_mod_final"].rearrange("(k p) n -> p k n", p=P)
        w_out = a["w_out"][0].rearrange("(k p) n -> p k n", p=P)
        w_gu = a["w_gate_up"][0].rearrange("e (k p) n -> e p k n", p=P)
        w_dn = a["w_down"][0].rearrange("e (k p) n -> e p k n", p=P)
        x_p, x_s = a["x_prompt"][0], a["x_sample"][0]

        def x_rows(t):
            return x_s if t == SAMPLE else x_p[TOK[t]:TOK[t] + P, :]

        def chunk_cols(c):
            kind, n = c
            if kind == "mod":
                w = w_mod[:, :, n * CW:(n + 1) * CW] if n < 12 else w_modf[:, :, (n - 12) * CW:(n - 11) * CW]
                return [(0, CW, w)]
            if kind == "qi":
                return [(0, 324, w_in[:, :, QI:QI + 324])]
            if kind == "kv":
                return [(0, 256, w_in[:, :, KA:KA + 256]), (256, 16, w_in[:, :, LR:LR + 16])]
            if kind == "out":
                return [(0, CW, w_out[:, :, n * CW:(n + 1) * CW])]
            at_ = {"qa": QA, "qkg": QG, "vg": VG, "rg": RG}[kind]
            return [(0, CW, w_in[:, :, at_:at_ + CW])]

        block = ctx.enter_context(nc.Block())

        @block.sync
        def _(sp):
            for n, c in enumerate(chunks):
                if n >= FRONT_RING:
                    old = chunks[n - FRONT_RING]
                    filled(sp, JOB[last_step[old]])
                s = n % FRONT_RING
                for at_, w, src in chunk_cols(c):
                    sp.dma_start(wslot(s)[:, :, at_:at_ + w], src).then_inc(loaded[s], 16)
                if c[0] == "mod":
                    m = c[1]
                    b = a["b_mod"][0, m * CW:(m + 1) * CW] if m < 12 else a["b_mod_final"][(m - 12) * CW:(m - 11) * CW]
                    if m == 0:
                        sp.wait_ge(bias_clear, 1)
                    if m == 4:
                        filled(sp, JOB[("cacheT", 7)])
                    sp.dma_start((bmod if m < 4 else bmod2)[s][0:1, :], b.unsqueeze(0)).then_inc(loaded[s], 16)

            def expert_weights(i, e, first=False):
                for c in range(RING):
                    if not first:
                        sp.wait_ge(chunk_done, (i - 1) * RING + c + 1)
                    if c < 4:
                        n = (c // 2) + 2 * (c % 2)
                        src = w_gu[bass.ds(e, 1), :, :, n * CW:(n + 1) * CW].rearrange("e p k n -> p (e k) n")
                        sp.dma_start(wslot(c), src).then_inc(loaded[c], 16)
                    else:
                        src = w_dn[bass.ds(e, 1), :, (c - 4) * 4:(c - 3) * 4, :].rearrange("e p k n -> p (e k) n")
                        sp.dma_start(slot(c).rearrange("p (k n) -> p k n", k=4), src).then_inc(loaded[c], 16)
                    if c == 0:
                        if not first:
                            sp.wait_ge(bias_ready, i)
                        else:
                            sp.wait_ge(routed, 1)
                        sp.dma_start(brow[0:1, 0:2 * D], a["b_gate_up"][0][bass.ds(e, 1), :]).then_inc(bias_in, 16)
                        sp.dma_start(brow[0:1, 2 * D:3 * D], a["b_down"][0][bass.ds(e, 1), :]).then_inc(bias_in, 16)

            filled(sp, JOB[("y", T - 1)])
            expert_weights(0, 0, first=True)
            with sp.Fori(1, NE) as e:
                expert_weights(e, e)
            sp.wait_ge(routed, 1)
            n_over = sp.value_load(over[0:1, NOV:NOV + 1], min_val=0, max_val=NOV)
            with sp.If(n_over > 0):
                with sp.Fori(0, n_over) as j:
                    e = sp.value_load(over[0:1, bass.ds(j, 1)], min_val=0, max_val=NE - 1)
                    expert_weights(j + NE, e)

            sp.wait_ge(ys_stored, (n_over + NE + 1) * 16)
            for n, m in enumerate((5, 6, 7)):
                sp.dma_start(fP[n], mod_dram[0:1, m * D:(m + 1) * D].to_broadcast([P, D])).then_inc(fin_rows, 16)
                sp.dma_start(fS[n][0:DEC, :], mod_dram[1:2, m * D:(m + 1) * D].to_broadcast([DEC, D])).then_inc(fin_rows, 16)
            sp.dma_start(gfin_b, a["g_final"].unsqueeze(0).to_broadcast([P, D])).then_inc(fin_rows, 16)

            def load_x2(t):
                sp.dma_start(xf[t % 2][0:ROWS[t], :], x2_dram[TOK[t]:TOK[t] + ROWS[t], :]).then_inc(fin_x[t % 2], 16)

            load_x2(0)
            load_x2(1)
            for t in range(T):
                R = ROWS[t]
                sp.wait_ge(f_out, t + 1)
                dst = y_sample[0] if t == SAMPLE else y_prompt[0, TOK[t]:TOK[t] + P, :]
                sp.dma_start(dst, fo[t % 2][0:R, :]).then_inc(f_stored[t % 2], 16)
                if t + 2 < T:
                    load_x2(t + 2)
            sp.wait_ge(f_stored[0], 48)
            sp.wait_ge(f_stored[1], 32)

        @block.scalar
        def _(act_e):
            order = Order(act_e, act_s)
            sc = nc.scalar

            def leave(dst, j, t, lo_, n, fn=ACT.Copy):
                if t != SAMPLE:
                    return sc.activation(dst, bank(j)[0:ROWS[t], lo_:lo_ + n], fn)
                w = SPAN[STEPS[j][0]]
                for q in range(4):
                    x, y = max(lo_, q * w), min(lo_ + n, (q + 1) * w)
                    if x < y:
                        ins = sc.activation(dst[:, x - lo_:y - lo_], bank(j)[32 * q:32 * q + DEC, x - q * w:y - q * w], fn)
                return ins

            act_e.dma_start(cc[0:8, :], a["c_prompt"].rearrange("o (k p) -> (o k) p", p=P)).then_inc(c_in, 16)
            act_e.dma_start(cc[8:16, :], a["c_sample"].rearrange("o (k p) -> (o k) p", p=P)).then_inc(c_in, 16)
            act_e.dma_start(vecs[0:8, :], a["g_mix"].rearrange("o (k p) -> (o k) p", p=P)).then_inc(c_in, 16)
            act_e.dma_start(vecs[8:10, :], a["gla_b_gate"].rearrange("o (k p) -> (o k) p", p=P)).then_inc(c_in, 16)
            for t in range(T):
                act_e.dma_start(xs5[0:ROWS[t], t, :], x_rows(t)).then_inc(x_in, 16)
            act_e.wait_ge(c_in, 64)
            sc.activation(csg[0:16, :], cc[0:16, :], ACT.Sigmoid).then_inc(c_sig, 1)
            act_e.wait_ge(x_in, 16 * T)
            act_e.wait_ge(ss_clear, 1)
            for t in range(T):
                order(sc.activation(rel[0][0:ROWS[t], :], xs5[0:ROWS[t], t, :], ACT.Square,
                                    accum_out=ss[0:ROWS[t], t:t + 1]))
            note(act_e, x_sq)
            act_e.wait_ge(x_var, 1)
            sc.activation(rr[:, 0:T], vv[:, 0:T], ACT.Sqrt).then_inc(x_sqrt, 1)
            act_e.wait_ge(loaded[1], need[1])
            act_e.dma_start(cs[:, 0:4, :], a["rope"][0:SEQ].rearrange("(t p) n -> p t n", p=P)).then_inc(tabs_in, 16)
            act_e.dma_start(cs[0:DEC, 4, :], a["rope"][SEQ:NTOK]).then_inc(tabs_in, 16)
            act_e.dma_start(wgate[0:16, :], a["gla_w_gate"][0]).then_inc(tabs_in, 16)
            act_e.dma_start(gout_b, a["gla_g_out"].to_broadcast([P, DV])).then_inc(tabs_in, 16)
            act_e.dma_start(ckidx, a["cache_kidx"][0, 0].rearrange("(t p) n -> p t n", p=P)).then_inc(cache_in, 16)
            act_e.dma_start(ck, a["cache_k"][0, 0].rearrange("(t p) g n -> p t (g n)", p=P)).then_inc(cache_in, 16)
            act_e.dma_start(Vs[:, 0:8, :], a["cache_v"][0, 0].rearrange("(t p) g n -> p t (g n)", p=P)).then_inc(cache_in, 16)
            kt = 0
            for j, s in enumerate(STEPS):
                kind = s[0]
                done = psum_drained[j % 4]
                t = s[1] if len(s) > 1 else 0
                R = ROWS[t] if t < T else 0
                tok = slice(TOK[t], TOK[t] + R) if t < T else None
                if kind == "mod":
                    filled(act_e, j)
                    if t >= 2:
                        act_e.wait_ge(mod_stored[t % 2], 16 * (t // 2))
                        if t - 2 < 4:
                            filled(act_e, JOB[("modT", t - 2)])
                    for q in range(4):
                        ins = sc.activation(modrow[t % 2][0:2, q * P:(q + 1) * P], bank(j)[32 * q:32 * q + 2, 0:P], ACT.Copy)
                    order(ins)
                    note(act_e, done)
                    note(act_e, mod_copied)
                    act_e.dma_start(mod_dram[:, t * CW:(t + 1) * CW], modrow[t % 2][0:2, :]).then_inc(mod_stored[t % 2], 16)
                elif kind == "qi":
                    i = ORDER.index(t)
                    filled(act_e, j)
                    if i >= 2:
                        act_e.wait_ge(qi_roped, i - 1)
                    leave(qiraw[i % 2][0:R, :], j, t, 0, 324).then_inc(done, 1)
                elif kind == "qiT":
                    filled(act_e, j)
                    sc.activation(qiT[:, :, tok], bank(j)[:, 0:2 * R].rearrange("p (k n) -> p k n", k=2), ACT.Copy)
                    dst = ki_sample[0, 0] if t == SAMPLE else ki_prompt[0, 0, tok, :]
                    act_e.dma_start(dst, qro[0:R, t, 256:320]).then_inc(out_ki, 16)
                    if t == SAMPLE:
                        sc.activation(kiTs[:, PAST:PAST + DEC], bank(j)[:, 2 * R:3 * R], ACT.Copy)
                    sc.activation(kiT[:, tok], bank(j)[:, 2 * R:3 * R], ACT.Copy).then_inc(done, 1)
                elif kind == "cacheT":
                    filled(act_e, j)
                    sc.activation(kiTs[:, t * P:(t + 1) * P], bank(j)[:, 0:P], ACT.Copy)
                    sc.activation(kTs[:, t * P:(t + 1) * P], bank(j, 1)[:, 0:P], ACT.Copy).then_inc(done, 1)
                elif kind in ("idx", "idxnew"):
                    filled(act_e, j)
                    if kt >= 2:
                        act_e.wait_ge(rel_used, kt - 1)
                    n = min(NKEYS[t], 1024) if kind == "idx" else DEC
                    sc.activation(rel[kt % 2][0:R, 0:n], group(j)[0:R, 0:n], ACT.Relu).then_inc(done, 1)
                    kt += 1
                elif kind == "kv":
                    i = ORDER.index(t)
                    filled(act_e, j)
                    if i >= 2:
                        act_e.wait_ge(raw_used, i - 1)
                    if t == SAMPLE:
                        act_e.wait_ge(cache_in, 48)
                        leave(Vs[0:R, 8, :], j, t, 128, 128)
                    leave(va[0:R, t, :], j, t, 128, 128)
                    leave(raw[i % 2][0:R, 0:128], j, t, 0, 128).then_inc(done, 1)
                elif kind == "lr":
                    filled(act_e, j)
                    sc.activation(halves(lrT)[0:16], turned(j)[0:16], ACT.Copy).then_inc(done, 1)
                elif kind == "qa":
                    i = ORDER.index(t)
                    filled(act_e, j)
                    act_e.wait_ge(raw_used, T + i - 1)
                    leave(raw[(T + i) % 2][0:R, :], j, t, 0, 512).then_inc(done, 1)
                elif kind == "qaT":
                    filled(act_e, j)
                    if t == SAMPLE:
                        sc.activation(qaTs, bank(j)[:, 0:4 * R], ACT.Copy)
                    else:
                        sc.activation(qaT[:, :, tok], bank(j)[:, 0:4 * R].rearrange("p (k n) -> p k n", k=4), ACT.Copy)
                    if t == SAMPLE:
                        sc.activation(kTs[:, PAST:PAST + DEC], bank(j, 1)[:, 0:R], ACT.Copy)
                    sc.activation(kaT[:, tok], bank(j, 1)[:, 0:R], ACT.Copy).then_inc(done, 1)
                elif kind == "qkg":
                    filled(act_e, j)
                    dst, f = (qgT, HD ** -0.5) if t < 2 else (kgT, 1.0)
                    sc.activation(halves(dst[:, t % 2, :]), turned(j), ACT.Copy, scale=f).then_inc(done, 1)
                elif kind == "vg":
                    filled(act_e, j)
                    leave(vg[0:R, t, :], j, t, 0, 512).then_inc(done, 1)
                elif kind == "rg":
                    i = ORDER.index(t)
                    filled(act_e, j)
                    if i >= 2:
                        act_e.wait_ge(raw_used, 2 * T + i - 1)
                    if t == SAMPLE:
                        act_e.wait_ge(masks_made, 1)
                        for q in range(1, 4):
                            ins = sc.activation(score[t][32 * q:32 * q + DEC, :], score[t][0:DEC, :], ACT.Copy)
                        ins.then_inc(mask_spread, 1)
                    leave(graw[i % 2][0:R, :], j, t, 0, 512, ACT.Sigmoid)
                    leave(rg[0:R, t, :], j, t, 0, 512).then_inc(done, 1)
                elif kind == "z":
                    act_e.wait_ge(gate_z, t + 1)
                    order(sc.activation(gT1[1], gT1[1], ACT.Exp, scale=-1.0))
                    sc.activation(gT1[1], gT1[1], ACT.Ln, bias=1.0).then_inc(gate_l, 1)
                    if t == 1:
                        for n, x in enumerate((gqA, gk0, gk1, gqe, gkd, eL)):
                            act_e.wait_ge(gla_in, n + 1)
                            sc.activation(x, x, ACT.Exp).then_inc(gla_exp, 1)
                elif kind == "kd":
                    filled(act_e, j)
                    sc.activation(kdn[0:R, t, :], bank(j)[0:R, 0:256], ACT.Copy).then_inc(done, 1)
                elif kind == "gi":
                    filled(act_e, j)
                    act_e.wait_ge(o_done, t)
                    sc.activation(ot[0:R, :].rearrange("p (j b n) -> p b j n", b=2, j=2),
                                  group(j)[0:R, :].rearrange("p (b j n) -> p b j n", b=2, j=4)[:, :, 0:2, :],
                                  ACT.Copy).then_inc(done, 1)
                elif kind == "go":
                    act_e.wait_ge(o_sum, t + 1)
                    for h in range(NBH):
                        order(sc.activation(gT2[0:R, 0:DV], ot[0:R, h * DV:(h + 1) * DV], ACT.Square,
                                            accum_out=ss4[0:R, h:h + 1]))
                    note(act_e, o_sq)
                    act_e.wait_ge(o_var, t + 1)
                    sc.activation(rr4[0:R, :], vv4[0:R, :], ACT.Sqrt).then_inc(o_sqrt, 1)
                elif kind in ("pT", "pTnew") and t == SAMPLE:
                    filled(act_e, j)
                    if kind == "pT":
                        act_e.wait_ge(raw_used, 3 * T)
                        sc.activation(pTs[s[2]][0], group(j), ACT.Copy).then_inc(done, 1)
                    else:
                        sc.activation(pTs[s[2]][1][0:DEC, :], bank(j)[0:DEC, 0:P], ACT.Copy).then_inc(done, 1)
                elif kind == "pT":
                    u = UNIT[s[1:]]
                    n = -(-NKEYS[t] // P)
                    filled(act_e, j)
                    if u >= 4:
                        filled(act_e, JOB[("pv", *UNITS[u - 2])])
                    sc.activation(pT[u % 2][:, 0:n * R], bank(j)[:, 0:n * R], ACT.Copy).then_inc(done, 1)
                elif kind == "catT":
                    filled(act_e, j)
                    sc.activation(catT[:, :, tok], group(j)[:, 0:8 * R].rearrange("p (k n) -> p k n", k=KD),
                                  ACT.Copy).then_inc(done, 1)
                elif kind == "y":
                    act_e.wait_ge(x2_made, t + 1)
                    sc.activation(junk[0:R, :], x2b[t % 2][0:R, :], ACT.Square, accum_out=ss[0:R, t:t + 1]).then_inc(x2_sq, 1)
                    act_e.wait_ge(x2_var, t + 1)
                    sc.activation(rr[0:R, t:t + 1], vv[0:R, t:t + 1], ACT.Sqrt).then_inc(x2_sqrt, 1)
                elif kind == "hT":
                    filled(act_e, j)
                    if t >= 1:
                        filled(act_e, JOB[("rt", t - 1)])
                    sc.activation(h2T[:, 0:8 * R], group(j)[:, 0:8 * R], ACT.Copy).then_inc(done, 1)
                elif kind == "rt":
                    act_e.wait_ge(top_ready, t + 1)
                    sc.activation(e4[0:R, :], v8[0:R, 0:4], ACT.Exp, bias=ngate[0:R, :],
                                  accum_out=gs1[0:R, :]).then_inc(gate_exp, 1)
                if kind in ("sc", "scnew") and (kind == "scnew" or t != SAMPLE):
                    u = UNIT[s[1:]]
                    act_e.wait_ge(logits_max, u + 1)
                    n = NKEYS[t]
                    if u >= 4:
                        in_sbuf(act_e, ("pv", *UNITS[u - 4]))
                    sc.activation(prob[u % 3][:, 0:n], prob[u % 3][:, 0:n], ACT.Exp, bias=negm[:, u % 3:u % 3 + 1],
                                  accum_out=ars[:, u % 4:u % 4 + 1]).then_inc(probs_made, 1)

            def expert_act(i):
                for half in range(2):
                    act_e.wait_ge(gate_added, 2 * i + half + 1)
                    sc.activation(es, eg, ACT.Sigmoid, scale=ALPHA).then_inc(gate_sig, 1)
                    act_e.wait_ge(act_turned, 2 * i + half + 1)
                    sc.activation(actT[:, 4 * half:4 * half + 4, :].rearrange("p k n -> p (k n)"), psum[:, 6 + half, :],
                                  ACT.Copy).then_inc(actT_ready, 1)
                act_e.wait_ge(ys_ready, i + 2)
                act_e.dma_start(ys_dram[bass.ds(i * P, P), :], ysb).then_inc(ys_stored, 16)

            act_e.sem_inc(ys_stored, 16)
            with act_e.Fori(0, NE) as i:
                expert_act(i)
            act_e.wait_ge(routed, 1)
            n_over = act_e.value_load(over[0:1, NOV:NOV + 1], min_val=0, max_val=NOV)
            with act_e.If(n_over > 0):
                with act_e.Fori(0, n_over) as j:
                    expert_act(j + NE)
            act_e.wait_ge(ys_stored, (n_over + NE + 1) * 16)
            for t in range(T):
                R = ROWS[t]
                act_e.wait_ge(f_made, t + 1)
                sc.activation(facc[0:R, :], xf[t % 2][0:R, :], ACT.Square, accum_out=ss[0:R, t:t + 1]).then_inc(f_sq, 1)
                act_e.wait_ge(f_var, t + 1)
                sc.activation(rr[0:R, t:t + 1], vv[0:R, t:t + 1], ACT.Sqrt).then_inc(f_sqrt, 1)

        @block.vector
        def _(dve):
            order = Order(dve, dve_s)
            v = nc.vector

            def inv_sqrt(out, root, var, n, rows):
                o, r, x = out[0:rows, n], root[0:rows, n], var[0:rows, n]
                order(v.reciprocal(o, r))
                tmp = r2[0:rows, 0:o.shape[1]]
                order(v.tensor_tensor(tmp, o, o, ALU.mult))
                order(v.tensor_tensor(tmp, tmp, x, ALU.mult))
                order(v.tensor_scalar(tmp, tmp, -0.5, 1.5, ALU.mult, ALU.add))
                order(v.tensor_tensor(o, o, tmp, ALU.mult))

            v.memset(ss, 1.0).then_inc(ss_clear, 1)
            dve.wait_ge(c_sig, 1)
            v.tensor_tensor(cc[0:16, :], cc[0:16, :], csg[0:16, :], ALU.mult).then_inc(c_silu, 1)
            dve.wait_ge(x_sq, 1)
            v.tensor_scalar(vv[:, 0:T], ss[:, 0:T], 1.0 / D, EPS, ALU.mult, ALU.add).then_inc(x_var, 1)
            dve.wait_ge(x_sqrt, 1)
            inv_sqrt(r3, rr, vv, slice(0, T), P)
            for t in range(T):
                v.tensor_scalar(xs5[0:ROWS[t], t, :], xs5[0:ROWS[t], t, :], r3[0:ROWS[t], t:t + 1], None,
                                ALU.mult).then_inc(x_norm, 1)

            def top_k(t):
                R, n = ROWS[t], NKEYS[t]
                k = TOPK_SAMPLE if t == SAMPLE else TOPK_PROMPT
                s_, w = score[t][0:R, :], twork[0:R, 0:n]
                if n <= k:
                    order(v.memset(score[t][:, :], 0.0))
                    v.memset(score[t][0:CHUNK, n - CHUNK:n], MASKED).then_inc(masks_made, 1)
                    return
                for i in range(k // 8):
                    src = s_ if i == 0 else w
                    order(v.max(m8[0:R, :], src))
                    if i < k // 8 - 1:
                        order(v.match_replace(w, m8[0:R, :], src, NEG))
                above, at_, cnt = w, prefix[0:R, 0:n], cgt[0:R, :]
                order(v.tensor_scalar(above, s_, m8[0:R, 7:8], 0.0, ALU.is_gt, ALU.add, accum_out=cnt))
                order(v.tensor_scalar(s_, s_, m8[0:R, 7:8], None, ALU.is_equal))
                order(v.tensor_scalar(cnt, cnt, -1.0, float(k), ALU.mult, ALU.add))
                order(v.tensor_tensor_scan(at_, s_, s_, 0.0, ALU.add, ALU.max))
                order(v.scalar_tensor_tensor(out=s_, in0=at_, scalar=cnt, in1=s_, op0=ALU.is_le, op1=ALU.mult))
                order(v.tensor_tensor(s_, s_, above, ALU.add))
                v.tensor_scalar(s_, s_, -MASKED, MASKED, ALU.mult, ALU.add).then_inc(masks_made, 1)

            def rope(R, t, H, src, dst, tmp):
                x = src.rearrange("p (h d) -> p h d", h=H)
                o = dst.rearrange("p (h d) -> p h d", h=H)
                m = tmp.rearrange("p (h d) -> p h d", h=H)
                order(v.tensor_tensor(o, x, cs[0:R, t, 0:64].unsqueeze(1).to_broadcast([R, H, 64]), ALU.mult))
                for a_, b_ in ((0, 32), (32, 0)):
                    order(v.tensor_tensor(m[:, :, a_:a_ + 32], x[:, :, b_:b_ + 32],
                                          cs[0:R, t, 64 + a_:96 + a_].unsqueeze(1).to_broadcast([R, H, 32]), ALU.mult))
                return v.tensor_tensor(o, o, m, ALU.add)

            kt = 0
            for j, s in enumerate(STEPS):
                kind = s[0]
                done = psum_drained[j % 4]
                t = s[1] if len(s) > 1 else 0
                R = ROWS[t] if t < T else 0
                tok = slice(TOK[t], TOK[t] + R) if t < T else None
                if kind == "c":
                    filled(dve, j)
                    v.tensor_copy(cT, bank(j)[:, 0:16])
                    v.tensor_copy(vT[:, 0:10], bank(j, 1)[:, 0:10]).then_inc(done, 1)
                elif kind == "modT":
                    filled(dve, j)
                    v.tensor_copy(colT[:, 8 * t:8 * t + 8], bank(j)[:, 0:8]).then_inc(done, 1)
                    if t == 3:
                        in_sbuf(dve, ("modT", 3))
                        in_sbuf(dve, ("c",))
                        order(v.tensor_scalar(a1, colT[:, 16:32], 1.0, None, ALU.add))
                        order(v.tensor_tensor(a1.rearrange("p (k c) -> p k c", c=2), a1.rearrange("p (k c) -> p k c", c=2),
                                              vT[:, 0:8].unsqueeze(2).to_broadcast([P, 8, 2]), ALU.mult))
                elif kind == "xT":
                    filled(dve, j)
                    v.tensor_scalar(hT[:, t, 0:SEQ], bank(j), a1[:, 2 * t:2 * t + 1], colT[:, 2 * t:2 * t + 1],
                                    ALU.mult, ALU.add)
                    v.tensor_scalar(hT[:, t, SEQ:NTOK], bank(j, 1)[:, 0:DEC], a1[:, 2 * t + 1:2 * t + 2],
                                    colT[:, 2 * t + 1:2 * t + 2], ALU.mult, ALU.add).then_inc(done, 1)
                elif kind == "qi":
                    i = ORDER.index(t)
                    in_sbuf(dve, s)
                    dve.wait_ge(tabs_in, 64)
                    order(v.tensor_scalar(wis[0:R, t, :], qiraw[i % 2][0:R, 320:324], NIH ** -0.5, None, ALU.mult))
                    rope(R, t, 5, qiraw[i % 2][0:R, 0:320], qro[0:R, t, :], twork[0:R, 0:320]).then_inc(qi_roped, 1)
                elif kind in ("idx", "idxnew"):
                    h = s[2]
                    in_sbuf(dve, s)
                    n0 = 0 if kind == "idx" else 1024
                    n = min(NKEYS[t], 1024) if kind == "idx" else DEC
                    dst, src = score[t][0:R, n0:n0 + n], rel[kt % 2][0:R, 0:n]
                    if h == 0:
                        order(v.tensor_scalar(dst, src, wis[0:R, t, 0:1], None, ALU.mult))
                    else:
                        order(v.scalar_tensor_tensor(out=dst, in0=src, scalar=wis[0:R, t, h:h + 1], in1=dst,
                                                     op0=ALU.mult, op1=ALU.add))
                    kt += 1
                    note(dve, rel_used)
                    if h == NIH - 1 and t not in (0, SAMPLE):
                        order(v.memset(score[t][0:CHUNK, NKEYS[t] - CHUNK:NKEYS[t]], NEG))
                    if s == ("idx", ORDER[-1], NIH - 1):
                        for tt in ORDER:
                            top_k(tt)
                elif kind == "z":
                    filled(dve, j)
                    Z, B = gT2[:, 0:NTOK], bT[:, t, :]
                    dve.wait_ge(out_ki, T * 16)
                    dve.wait_ge(out_kv, 2 * T * 16)
                    for x in mod_stored:
                        dve.wait_ge(x, 16 * 8)
                    order(v.tensor_scalar(Z, group(j)[:, 0:NTOK], vT[:, 8 + t:9 + t], None, ALU.add))
                    note(dve, done)
                    v.scalar_tensor_tensor(out=gT1[1], in0=Z, scalar=-1.0, in1=Z, op0=ALU.mult,
                                           op1=ALU.max).then_inc(gate_z, 1)
                    dve.wait_ge(gate_l, t + 1)
                    order(v.scalar_tensor_tensor(out=Z, in0=Z, scalar=0.0, in1=gT1[1], op0=ALU.min,
                                                 op1=ALU.subtract))
                    order(v.tensor_scalar(Z, Z, 1.0 / 16.0, None, ALU.mult))
                    dve.wait_ge(gate_mask, 1)
                    order(v.tensor_tensor_scan(B, gT1[0], Z, 0.0, ALU.mult, ALU.add))
                    if t == 1:
                        v4 = bT.rearrange("p j (b s) -> p j b s", s=32)
                        c4 = bT[:, :, 0:SEQ].rearrange("p j (c s) -> p j c s", s=CHUNK)
                        for x in range(2):
                            ins = v.tensor_tensor(gqA[:, x].rearrange("p (b s) -> p b s", s=32), v4[:, x],
                                                  v4[:, x, :, 16:17].to_broadcast([P, 17, 32]), ALU.subtract)
                        ins.then_inc(gla_in, 1)
                        for dst, at_ in ((gk0, 16), (gk1, 48), (None, 0), (gkd, 63)):
                            if dst is None:
                                v.tensor_copy(gqe, bT).then_inc(gla_in, 1)
                                continue
                            for x in range(2):
                                ins = v.tensor_tensor(dst[:, x, 0:SEQ].rearrange("p (c s) -> p c s", s=CHUNK),
                                                      c4[:, x, :, at_:at_ + 1].to_broadcast([P, 8, CHUNK]), c4[:, x], ALU.subtract)
                                if dst is not gk1:
                                    a_ = SEQ + min(at_, DEC - 1)
                                    ins = v.tensor_tensor(dst[:, x, SEQ:NTOK], bT[:, x, a_:a_ + 1].to_broadcast([P, DEC]),
                                                          bT[:, x, SEQ:NTOK], ALU.subtract)
                            ins.then_inc(gla_in, 1)
                        v.tensor_copy(eL[:, :, 0:8], c4[:, :, :, 63:64].rearrange("p j c o -> p j (c o)"))
                        v.tensor_copy(eL[:, :, 8:9], bT[:, :, NTOK - 1:NTOK]).then_inc(gla_in, 1)
                        for n, (x, y) in enumerate(((gqA, qgT), (gk0, kgT), (gk1, kgT[:, :, 0:SEQ]), (gqe, qgT), (gkd, kgT))):
                            dve.wait_ge(gla_exp, n + 1)
                            v.tensor_tensor(x, x, y, ALU.mult).then_inc(gla_made, 1)
                        for x in (scT[0], scT[1], states[0].rearrange("p j n -> p (j n)")):
                            v.memset(x, 0.0).then_inc(gla_made, 1)
                elif kind == "gs":
                    filled(dve, j)
                    if t >= 2:
                        filled(dve, JOB[("go", t - 2)])
                    elif t == 0:
                        dve.wait_ge(gla_made, 8)
                    v.copy_predicated(scT[t % 2][0:R, :].rearrange("p (b n) -> p b n", b=2),
                                      gmask[0:R, :].rearrange("p (b n) -> p b n", b=2),
                                      group(j)[0:R, :].rearrange("p (b n) -> p b n", b=2)[:, :, 0:128]).then_inc(done, 1)
                elif kind == "gst":
                    filled(dve, j)
                    c = 2 * t + s[2]
                    if t == SAMPLE:
                        dve.wait_ge(state_in, 16)
                        for x in range(2):
                            ins = v.scalar_tensor_tensor(out=states[5][:, x, :], in0=states[4][:, x, :],
                                                         scalar=eL[:, x, 8:9], in1=bank(j)[:, x * DV:(x + 1) * DV],
                                                         op0=ALU.mult, op1=ALU.add)
                        ins.then_inc(done, 1)
                    elif c == 0:
                        v.tensor_copy(states[1].rearrange("p j n -> p (j n)"), bank(j)[:, 0:256]).then_inc(done, 1)
                    else:
                        prev = JOB[("gst", (c - 1) // 2, (c - 1) % 2)]
                        dve.wait_ge(psum_drained[prev % 4], prev // 4 + 1)
                        for x in range(2):
                            ins = v.scalar_tensor_tensor(out=states[(c + 1) % 4][:, x, :], in0=states[c % 4][:, x, :],
                                                         scalar=eL[:, x, c:c + 1], in1=bank(j)[:, x * DV:(x + 1) * DV],
                                                         op0=ALU.mult, op1=ALU.add)
                        ins.then_inc(done, 1)
                elif kind == "go":
                    filled(dve, j)
                    in_sbuf(dve, ("gi", t))
                    order(v.tensor_tensor(ot[0:R, :], ot[0:R, :], bank(j)[0:R, :], ALU.add))
                    note(dve, done)
                    note(dve, o_sum)
                    dve.wait_ge(o_sq, t + 1)
                    v.tensor_scalar(vv4[0:R, :], ss4[0:R, :], 1.0 / DV, EPS, ALU.mult, ALU.add).then_inc(o_var, 1)
                    dve.wait_ge(o_sqrt, t + 1)
                    inv_sqrt(r3, rr4, vv4, slice(0, 4), R)
                    dve.wait_ge(raw_used, 3 * T)
                    for h in range(NBH):
                        g = rg[0:R, t, h * DV:(h + 1) * DV]
                        ins = v.scalar_tensor_tensor(out=g, in0=ot[0:R, h * DV:(h + 1) * DV],
                                                     scalar=r3[0:R, h:h + 1], in1=g, op0=ALU.mult, op1=ALU.mult)
                    ins.then_inc(o_done, 1)
                elif kind in ("sc", "scnew"):
                    u = UNIT[s[1:]]
                    n0 = 0 if kind == "sc" else 1024
                    n = min(NKEYS[t], 1024) if kind == "sc" else DEC
                    filled(dve, j)
                    if u >= 3:
                        filled(dve, JOB[("pT", *UNITS[u - 3])])
                        if UNITS[u - 3][0] == SAMPLE:
                            filled(dve, JOB[("pTnew", *UNITS[u - 3])])
                    dve.wait_ge(masks_made, T)
                    if t == SAMPLE:
                        dve.wait_ge(mask_spread, 1)
                    mx = amx[:, 2 * (u % 3) + (kind == "scnew"):2 * (u % 3) + (kind == "scnew") + 1]
                    order(v.tensor_tensor_reduce(out=prob[u % 3][:, n0:n0 + n], in0=group(j)[:, 0:n],
                                                 in1=score[t][:, n0:n0 + n], scale=HD ** -0.5, scalar=NEG,
                                                 op0=ALU.add, op1=ALU.max, accum_out=mx))
                    m0 = amx[:, 2 * (u % 3):2 * (u % 3) + 1]
                    note(dve, done)
                    if kind == "scnew":
                        order(v.tensor_tensor(m0, m0, mx, ALU.max))
                    if kind == "scnew" or t != SAMPLE:
                        v.tensor_scalar(negm[:, u % 3:u % 3 + 1], m0, -1.0, None, ALU.mult).then_inc(logits_max, 1)
                elif kind == "pv":
                    h = s[2]
                    u = UNIT[s[1:]]
                    filled(dve, j)
                    dve.wait_ge(probs_made, u + 1)
                    r1 = rinv[:, u % 4:u % 4 + 1]
                    order(v.reciprocal(r1, ars[:, u % 4:u % 4 + 1]))
                    if t == SAMPLE:
                        order(v.tensor_scalar(osum[h], bank(j)[:, h * HD:(h + 1) * HD], r1, None, ALU.mult))
                        for q in range(4):
                            ins = v.tensor_copy(catA[0:R, t, (4 * h + q) * HD:(4 * h + q + 1) * HD],
                                                osum[h][32 * q:32 * q + R, :])
                        ins.then_inc(done, 1)
                        continue
                    g0 = h // 4 * HD
                    v.tensor_scalar(catA[0:R, t, h * HD:(h + 1) * HD], bank(j)[0:R, g0:g0 + HD], r1,
                                    None, ALU.mult).then_inc(done, 1)
                elif kind == "y":
                    row = rowS if t == SAMPLE else rowP
                    if t == 0:
                        dve.wait_ge(rows_in, ROW_DMAS * 16)
                        for x, rws in ((rowP, P), (rowS, DEC)):
                            order(v.scalar_tensor_tensor(out=x[1][0:rws, :], in0=x[1][0:rws, :], scalar=1.0,
                                                         in1=gffn_b[0:rws, :], op0=ALU.add, op1=ALU.mult))
                        for x in (sel, oneh, gates, chosen):
                            order(v.memset(x, 0.0))
                    filled(dve, j)
                    dve.wait_ge(x_again[t % 2], 16 * (t // 2 + 1))
                    if t >= 2:
                        dve.wait_ge(x2_stored[t % 2], 16 * (t // 2))
                        dve.wait_ge(h2_stored[t % 2], 16 * (t // 2))
                        filled(dve, JOB[("hT", t - 2)])
                    x2, h2 = x2b[t % 2][0:R, :], h2b[t % 2][0:R, :]
                    if t == SAMPLE:
                        for q in range(4):
                            x3, r3_ = (z_.rearrange("p (b q n) -> p b q n", b=2, q=4)[:, :, q] for z_ in (x2, row[0][0:R, :]))
                            ins = v.tensor_tensor(x3, psum[32 * q:32 * q + R, 2 * (j % 4):2 * (j % 4) + 2, 0:P], r3_, ALU.mult)
                        order(ins)
                    else:
                        order(v.tensor_tensor(x2, group(j)[0:R, :], row[0][0:R, :], ALU.mult))
                    note(dve, done)
                    order(v.tensor_tensor(x2, x2, xin[t % 2][0:R, :], ALU.add))
                    note(dve, x2_made)
                    dve.wait_ge(x2_sq, t + 1)
                    v.tensor_scalar(vv[0:R, t:t + 1], ss[0:R, t:t + 1], 1.0 / D, EPS, ALU.mult, ALU.add).then_inc(x2_var, 1)
                    dve.wait_ge(x2_sqrt, t + 1)
                    inv_sqrt(r3, rr, vv, slice(t, t + 1), R)
                    order(v.scalar_tensor_tensor(out=h2, in0=x2, scalar=r3[0:R, t:t + 1], in1=row[1][0:R, :],
                                                 op0=ALU.mult, op1=ALU.mult))
                    v.tensor_tensor(h2, h2, row[2][0:R, :], ALU.add).then_inc(h2_made, 1)
                elif kind == "rt":
                    filled(dve, j)
                    lg = rj[0:R, :]
                    order(v.tensor_tensor(lg, bank(j)[0:R, 0:NE], br_b[0:R, :], ALU.add))
                    note(dve, done)
                    order(v.max(v8[0:R, :], lg))
                    order(v.max_index(i8[0:R, :], v8[0:R, :], lg))
                    v.tensor_scalar(ngate[0:R, :], v8[0:R, 0:1], -1.0, None, ALU.mult).then_inc(top_ready, 1)
                    ch = chosen[0:R, 4 * t:4 * t + 4]
                    order(v.tensor_copy(ch, i8[0:R, 0:4]))
                    oh = oneh[0:R, t * 128:(t + 1) * 128].rearrange("p (k e) -> p k e", e=NE)
                    for k in range(TOPE):
                        order(v.tensor_scalar(oh[:, k, :], iota_e[0:R, :], chosen[0:R, 4 * t + k:4 * t + k + 1], None, ALU.is_equal))
                    order(v.tensor_reduce(sel[0:R, t * NE:(t + 1) * NE], oh.rearrange("p k e -> p e k"), AX.X, ALU.add))
                    note(dve, sel_made)
                    dve.wait_ge(gate_exp, t + 1)
                    order(v.reciprocal(gr1[0:R, :], gs1[0:R, :]))
                    order(v.tensor_scalar(gates[0:R, 4 * t:4 * t + 4], e4[0:R, :], gr1[0:R, :], None, ALU.mult))
                elif kind == "rank":
                    filled(dve, j)
                    v.tensor_copy(rank, bank(j)[:, 0:(T + 1) * NE]).then_inc(done, 1)
                    in_sbuf(dve, s)
                    dve.wait_ge(iota_made, 1)
                    cnt = rank[:, T * NE:(T + 1) * NE]
                    order(v.tensor_scalar(xb_, cnt, float(P), None, ALU.is_gt))
                    for m in range(2, 5):
                        order(v.scalar_tensor_tensor(out=xb_, in0=cnt, scalar=float(P * m), in1=xb_, op0=ALU.is_gt, op1=ALU.add))
                    order(v.tensor_tensor_scan(xe_, ones[:, 0:NE], xb_, 0.0, ALU.mult, ALU.add))
                    order(v.tensor_tensor(xst, xe_, xb_, ALU.subtract))
                    oh4 = oneh.rearrange("p (t k e) -> p t k e", k=TOPE, e=NE)
                    picked = pick_t.rearrange("p (t k e) -> p t k e", k=TOPE, e=NE)
                    pick3 = pick_t.rearrange("p (c e) -> p c e", e=NE)
                    rank4 = rank[:, 0:T * NE].rearrange("p (t e) -> p t e", e=NE).unsqueeze(2).to_broadcast([P, T, TOPE, NE])
                    order(v.tensor_tensor(picked, oh4, rank4, ALU.mult))
                    order(v.tensor_reduce(f1, pick3, AX.X, ALU.add))
                    order(v.tensor_tensor(pick3, oneh.rearrange("p (c e) -> p c e", e=NE),
                                          xst.unsqueeze(1).to_broadcast([P, T * TOPE, NE]), ALU.mult))
                    order(v.tensor_reduce(f2, pick3, AX.X, ALU.add))
                    order(v.tensor_scalar(f3, f1, float(P), None, ALU.is_ge))
                    order(v.tensor_copy(f4, f3))
                    for m in range(2, 5):
                        order(v.scalar_tensor_tensor(out=f3, in0=f1, scalar=float(P * m), in1=f3, op0=ALU.is_ge, op1=ALU.add))
                    order(v.scalar_tensor_tensor(out=f5, in0=f3, scalar=-float(P), in1=f1, op0=ALU.mult, op1=ALU.add))
                    order(v.scalar_tensor_tensor(out=f6, in0=f3, scalar=float(NE - 1), in1=f2, op0=ALU.add, op1=ALU.add))
                    order(v.tensor_tensor(f6, f6, chosen, ALU.subtract))
                    order(v.tensor_tensor(f6, f6, f4, ALU.mult))
                    order(v.tensor_tensor(f6, f6, chosen, ALU.add))
                    order(v.scalar_tensor_tensor(out=f7, in0=f5, scalar=float(NBLK), in1=f6, op0=ALU.mult, op1=ALU.add))
                    order(v.tensor_copy(tab_pos, f7))
                    order(v.scalar_tensor_tensor(out=f7, in0=f6, scalar=float(P), in1=f5, op0=ALU.mult, op1=ALU.add))
                    order(v.tensor_copy(ys_row, f7))
                    tn = tmpn[0:1, :].rearrange("p (j e) -> p j e", e=NE)
                    order(v.tensor_tensor(tn, iota_j[0:1, :].rearrange("p (j e) -> p j e", e=NE),
                                          xe_[0:1, :].unsqueeze(1).to_broadcast([1, NOV, NE]), ALU.is_ge))
                    order(v.tensor_reduce(ovf[0:1, 0:NOV], tn, AX.X, ALU.add))
                    order(v.tensor_scalar(ovf[0:1, 0:NOV], ovf[0:1, 0:NOV], float(NE - 1), None, ALU.min))
                    order(v.tensor_copy(ovf[0:1, NOV:NOV + 1], xe_[0:1, NE - 1:NE]))
                    order(v.tensor_copy(over[0:1, :], ovf[0:1, :]))
                    note(dve, routed)

            def take_tokens(i):
                dve.wait_ge(xg_turned, i + 1)
                for x in range(2):
                    ins = v.tensor_copy(xgT[:, 4 * x:4 * x + 4, :].rearrange("p k n -> p (k n)"), psum[:, x, :])
                ins.then_inc(xgT_ready, 1)

            def expert_dve(i):
                for half in range(2):
                    g, u = psum[:, 2 * half, :], psum[:, 2 * half + 1, :]
                    dve.wait_ge(act_ready, i * 2 + half + 1)
                    dve.wait_ge(chunk_done, i * RING + 2 * half + 1)
                    if half == 0:
                        dve.wait_ge(bias_ready, i + 1)
                    local(v.tensor_tensor(eg, g, bias_b[:, half * 512:(half + 1) * 512], ALU.add), 0, half, i)
                    v.tensor_scalar(eg, eg, LIMIT, None, ALU.min).then_inc(gate_added, 1)
                    dve.wait_ge(chunk_done, i * RING + 2 * half + 2)
                    local(v.tensor_tensor(eu, u, bias_b[:, D + half * 512:D + (half + 1) * 512], ALU.add), 1, half, i)
                    local(v.tensor_scalar(eu, eu, LIMIT, -LIMIT, ALU.min, ALU.max), 2, half, i)
                    dve.wait_ge(gate_sig, i * 2 + half + 1)
                    local(v.tensor_tensor(eg, eg, es, ALU.mult), 3, half, i)
                    v.scalar_tensor_tensor(out=act[:, half * 512:(half + 1) * 512], in0=eu, scalar=1.0, in1=eg,
                                           op0=ALU.add, op1=ALU.mult).then_inc(act_ready, 1)
                take_tokens(i + 1)
                dve.wait_ge(chunk_done, i * RING + RING)
                dve.wait_ge(ys_stored, i * 16 + 16)
                for n in range(2):
                    ins = v.tensor_tensor(ysb[:, n * 512:(n + 1) * 512], psum[:, 4 + n, :],
                                          bias_b[:, 2 * D + n * 512:2 * D + (n + 1) * 512], ALU.add)
                ins.then_inc(ys_ready, 1)

            def local(ins, n, half, i):
                ins.then_inc(gu_added, 1)
                dve.wait_ge(gu_added, i * 8 + 4 * half + n + 1)

            note(dve, act_ready)
            note(dve, ys_ready)
            take_tokens(0)
            with dve.Fori(0, NE) as i:
                expert_dve(i)
            n_over = dve.value_load(over[0:1, NOV:NOV + 1], min_val=0, max_val=NOV)
            with dve.If(n_over > 0):
                with dve.Fori(0, n_over) as jj:
                    expert_dve(jj + NE)

            dve.wait_ge(fin_rows, 16 * 7)
            for x, rws in ((fP, P), (fS, DEC)):
                order(v.scalar_tensor_tensor(out=x[2][0:rws, :], in0=x[2][0:rws, :], scalar=1.0, in1=gfin_b[0:rws, :],
                                             op0=ALU.add, op1=ALU.mult))
            for t in range(T):
                R = ROWS[t]
                row = fS if t == SAMPLE else fP
                x2, o, y = xf[t % 2][0:R, :], fo[t % 2][0:R, :], yg[t % 2]
                dve.wait_ge(fin_y[t % 2], 64 * (t // 2 + 1))
                if t >= 2:
                    dve.wait_ge(f_stored[t % 2], 16 * (t // 2))
                order(v.tensor_scalar(o, y[0:R, 0:D], gates[0:R, 4 * t:4 * t + 1], None, ALU.mult))
                for k in range(1, TOPE):
                    order(v.scalar_tensor_tensor(out=o, in0=y[0:R, k * D:(k + 1) * D], scalar=gates[0:R, 4 * t + k:4 * t + k + 1],
                                                 in1=o, op0=ALU.mult, op1=ALU.add))
                order(v.tensor_tensor(o, o, row[0][0:R, :], ALU.mult))
                dve.wait_ge(fin_x[t % 2], 16 * (t // 2 + 1))
                v.tensor_tensor(x2, x2, o, ALU.add).then_inc(f_made, 1)
                dve.wait_ge(f_sq, t + 1)
                v.tensor_scalar(vv[0:R, t:t + 1], ss[0:R, t:t + 1], 1.0 / D, EPS, ALU.mult, ALU.add).then_inc(f_var, 1)
                dve.wait_ge(f_sqrt, t + 1)
                inv_sqrt(r3, rr, vv, slice(t, t + 1), R)
                order(v.scalar_tensor_tensor(out=o, in0=x2, scalar=r3[0:R, t:t + 1], in1=row[2][0:R, :],
                                             op0=ALU.mult, op1=ALU.mult))
                v.tensor_tensor(o, o, row[1][0:R, :], ALU.add).then_inc(f_out, 1)

        @block.gpsimd
        def _(pool):
            order = Order(pool, pool_s)
            g = nc.gpsimd
            order(g.memset(ident, 0.0))
            order(g.affine_select(out=ident, in_=ident, compare_op=ALU.not_equal, fill=1.0, base=0,
                                  pattern=[[-1, P]], channel_multiplier=1))
            order(g.memset(pick2, 0.0))
            order(g.memset(pick2[0:1, :], 1.0))
            for x in bmod:
                order(g.memset(x, 0.0))
            note(pool, bias_clear)
            note(pool, consts)
            order(g.memset(ones, 1.0))
            order(g.affine_select(out=before, in_=ones, compare_op=ALU.is_gt, fill=0.0, base=0,
                                  pattern=[[1, P]], channel_multiplier=-1))
            order(g.iota(gmask, pattern=[[0, NBH], [1, CHUNK]], base=0, channel_multiplier=-1))
            order(g.iota(gmask[CHUNK:P, :], pattern=[[0, NBH], [1, CHUNK]], base=0, channel_multiplier=-1))
            order(g.tensor_scalar(gmask, gmask, 0.0, None, ALU.is_ge))
            order(g.iota(iota_e, pattern=[[1, NE]], base=0, channel_multiplier=0, allow_small_or_imprecise_dtypes=True))
            order(g.iota(tok_id[:, 0:T], pattern=[[P, T]], base=0, channel_multiplier=1))
            order(g.memset(zero_i, 0))
            note(pool, consts)
            pool.dma_start(slot_dram.rearrange("(p b) o -> p (b o)", b=NBLK), zero_i).then_inc(tab_zero, 16)

            def rope(R, t, H, src, dst):
                x = src.rearrange("p (h d) -> p h d", h=H)
                o = dst if len(dst.shape) == 3 else dst.rearrange("p (h d) -> p h d", h=H)
                m = rope_p[0:R, 0:H * 64].rearrange("p (h d) -> p h d", h=H)
                order(g.tensor_tensor(o, x, cs[0:R, t, 0:64].unsqueeze(1).to_broadcast([R, H, 64]), ALU.mult))
                for a_, b_ in ((0, 32), (32, 0)):
                    order(g.tensor_tensor(m[:, :, a_:a_ + 32], x[:, :, b_:b_ + 32],
                                          cs[0:R, t, 64 + a_:96 + a_].unsqueeze(1).to_broadcast([R, H, 32]), ALU.mult))
                return g.tensor_tensor(o, o, m, ALU.add)

            for j, s in enumerate(STEPS):
                kind = s[0]
                t = s[1] if len(s) > 1 else 0
                R = ROWS[t] if t < T else 0
                tok = slice(TOK[t], TOK[t] + R) if t < T else None
                if kind == "kv":
                    i = ORDER.index(t)
                    in_sbuf(pool, s)
                    pool.wait_ge(tabs_in, 64)
                    order(rope(R, t, 2, raw[i % 2][0:R, 0:128], kro[0:R, t, :]))
                    note(pool, raw_used)
                    kd_, vd_ = (k_sample[0, 0], v_sample[0, 0]) if t == SAMPLE else (k_prompt[0, 0, tok], v_prompt[0, 0, tok])
                    pool.dma_start(kd_.rearrange("t g n -> t (g n)"), kro[0:R, t, :]).then_inc(out_kv, 16)
                    pool.dma_start(vd_.rearrange("t g n -> t (g n)"), va[0:R, t, :]).then_inc(out_kv, 16)
                elif kind == "qa":
                    i = ORDER.index(t)
                    in_sbuf(pool, s)
                    for gr in range(2):
                        dst = qaro[0:R, t, :].rearrange("p (r g d) -> p g r d", g=2, r=4)[:, gr]
                        order(rope(R, t, 4, raw[(T + i) % 2][0:R, gr * 256:(gr + 1) * 256], dst))
                    note(pool, raw_used)
                elif kind == "rg":
                    i = ORDER.index(t)
                    in_sbuf(pool, s)
                    r = rg[0:R, t, :]
                    order(g.tensor_tensor(r, r, graw[i % 2][0:R, :], ALU.mult))
                    r4 = r.rearrange("p (h n) -> p h n", h=NBH)
                    order(g.tensor_tensor(r4, r4, gout_b[0:R, :].unsqueeze(1).to_broadcast([R, NBH, DV]), ALU.mult))
                    note(pool, raw_used)
                elif kind == "z" and t == 0:
                    filled(pool, j)
                    order(g.memset(gT1[0], 1.0))
                    order(g.memset(gT1[0].rearrange("p (c s) -> p c s", s=32)[:, 0:17:2, 0:1], 0.0))
                    note(pool, gate_mask)
                    pool.wait_ge(masks_made, T)
                    order(g.memset(twork[:, 0:D], 0.0))
                    pool.dma_start(ys_dram[NE * P:(NE + NOV) * P, :].rearrange("(b p) n -> p b n", p=P),
                                   twork[:, 0:D].unsqueeze(1).to_broadcast([P, NOV, D])).then_inc(ys_cleared, 16)
                    pool.wait_ge(mod_stored[0], 16 * 8)
                    pool.wait_ge(mod_stored[1], 16 * 8)
                    pool.dma_start(states[4], a["state_gla"][0, 0].rearrange("(j h) d n -> (h d) j n", h=2)).then_inc(state_in, 16)
                elif kind == "gst" and (t, s[2]) in ((3, 1), (SAMPLE, 0)):
                    in_sbuf(pool, s)
                    st, dst = (states[5], gla_sample) if t == SAMPLE else (states[0], gla_prompt)
                    pool.dma_start(dst[0, 0].rearrange("(j h) d n -> (h d) j n", h=2), st).then_inc(out_state, 16)
                elif kind == "catT" and t == 0:
                    for tt in range(T):
                        in_sbuf(pool, ("pv", tt, LAST[tt]))
                        pool.wait_ge(o_done, tt + 1)
                    pool.wait_ge(out_state, 32)
                    pool.wait_ge(ys_cleared, 16)
                    pool.wait_ge(out_kv, 2 * T * 16)
                    pool.wait_ge(out_ki, T * 16)
                    pool.wait_ge(mod_stored[0], 16 * 8)
                    pool.wait_ge(mod_stored[1], 16 * 8)
                    for n, m in enumerate((2, 4, 3)):
                        pool.dma_start(rowP[n], mod_dram[0:1, m * D:(m + 1) * D].to_broadcast([P, D])).then_inc(rows_in, 16)
                        pool.dma_start(rowS[n][0:DEC, :], mod_dram[1:2, m * D:(m + 1) * D].to_broadcast([DEC, D])).then_inc(rows_in, 16)
                    pool.dma_start(gffn_b, a["g_ffn"].to_broadcast([P, D])).then_inc(rows_in, 16)
                    pool.dma_start(br_b, a["b_router"].to_broadcast([P, NE])).then_inc(rows_in, 16)
                    pool.dma_start(wr, a["w_router"][0].rearrange("(k p) n -> p k n", p=P)).then_inc(rows_in, 16)
                    order(g.iota(iota_j, pattern=[[1, NOV], [0, NE]], base=0, channel_multiplier=0,
                                 allow_small_or_imprecise_dtypes=True))
                    note(pool, iota_made)
                    for tt in range(2):
                        pool.dma_start(xin[tt], x_rows(tt)).then_inc(x_again[tt], 16)
                elif kind == "y":
                    pool.wait_ge(x2_made, t + 1)
                    pool.dma_start(x2_dram[tok, :], x2b[t % 2][0:R, :]).then_inc(x2_stored[t % 2], 16)
                    pool.wait_ge(h2_made, t + 1)
                    pool.dma_start(h_dram[tok, :], h2b[t % 2][0:R, :]).then_inc(h2_stored[t % 2], 16)
                    if t + 2 < T:
                        pool.dma_start(xin[t % 2][0:ROWS[t + 2], :], x_rows(t + 2)).then_inc(x_again[t % 2], 16)
            pool.wait_ge(routed, 1)
            pool.wait_ge(tab_zero, 16)
            n = 0
            for t in range(T):
                for k in range(TOPE):
                    c = 4 * t + k
                    g.indirect_dma_start(slot_dram, bass.IndirectOffsetOnAxis(tab_pos[0:ROWS[t], c:c + 1], 0),
                                         tok_id[0:ROWS[t], t:t + 1], None).then_inc(tab_written, 16)
                    n += 1
            pool.wait_ge(tab_written, 16 * n)
            pool.dma_start(slot_tok, slot_dram.rearrange("(p b) o -> p (b o)", b=NBLK)).then_inc(tab_in, 16)
            pool.wait_ge(tab_in, 16)
            for x, y in ((x2_stored[0], 3), (x2_stored[1], 2), (h2_stored[0], 3), (h2_stored[1], 2)):
                pool.wait_ge(x, 16 * y)

            def settle():
                pool.sem_inc(pool_settled, 1)

            def gather(i):
                g.tensor_copy(idx_now, slot_tok[:, bass.ds(i, 1)]).then_inc(idx_copied, 1)
                pool.wait_ge(idx_copied, i + 1)
                settle()
                g.indirect_dma_start(xg, None, h_dram, bass.IndirectOffsetOnAxis(idx_now, 0)).then_inc(gathered, 16)

            def expert_pool(i):
                pool.wait_ge(bias_in, (i + 1) * 32)
                pool.wait_ge(act_ready, i * 2 + 1)
                settle()
                g.partition_broadcast(bias_b[:, 0:2 * D], brow[:, 0:2 * D])
                pool.wait_ge(ys_ready, i + 1)
                settle()
                g.partition_broadcast(bias_b[:, 2 * D:3 * D], brow[:, 2 * D:3 * D]).then_inc(bias_ready, 1)
                pool.wait_ge(xg_turned, i + 1)
                gather(i + 1)

            gather(0)
            with pool.Fori(0, NE) as i:
                expert_pool(i)
            n_over = pool.value_load(over[0:1, NOV:NOV + 1], min_val=0, max_val=NOV)
            with pool.If(n_over > 0):
                with pool.Fori(0, n_over) as jj:
                    expert_pool(jj + NE)
            pool.wait_ge(gathered, (n_over + NE + 1) * 16)
            pool.wait_ge(ys_stored, (n_over + NE + 1) * 16)
            settle()
            for t in range(T):
                R = ROWS[t]
                if t >= 2:
                    pool.wait_ge(f_made, t - 1)
                for k in range(TOPE):
                    c = 4 * t + k
                    g.indirect_dma_start(yg[t % 2][0:R, k * D:(k + 1) * D], None, ys_dram,
                                         bass.IndirectOffsetOnAxis(ys_row[0:R, c:c + 1], 0)).then_inc(fin_y[t % 2], 16)

        @block.tensor
        def _(pe):
            mm, tr = nc.tensor.matmul, nc.tensor.transpose

            def sample_product(j, b, xT, w):
                n = SPAN[STEPS[j][0]]
                for k in range(KD):
                    for q in range(4):
                        last = mm(bank(j, b)[32 * q:32 * q + DEC, 0:n], lhsT=xT[:, k, SEQ:NTOK], rhs=w[:, k, q * n:(q + 1) * n],
                                  start=(k == 0), stop=(k == KD - 1))
                return last

            pe.wait_ge(consts, 2)
            pe.wait_ge(c_silu, 1)
            for j, s in enumerate(STEPS):
                kind = s[0]
                t = s[1] if len(s) > 1 else 0
                R = ROWS[t] if t < T else 0
                tok = slice(TOK[t], TOK[t] + R) if t < T else None
                free_group(pe, j)
                if kind == "c":
                    pe.wait_ge(c_in, 64)
                    tr(bank(j)[:, 0:16], cc[0:16, :], ident[0:16, 0:16])
                    last = tr(bank(j, 1)[:, 0:10], vecs[0:10, :], ident[0:10, 0:10])
                elif kind == "mod":
                    chunk_in(pe, s)
                    if t == 0:
                        in_sbuf(pe, ("c",))
                    w = wslot(CH[s] % FRONT_RING)
                    brow_ = (bmod if t < 4 else bmod2)[CH[s] % FRONT_RING]
                    for q in range(4):
                        mm(bank(j)[32 * q:32 * q + 2, 0:P], lhsT=pick2, rhs=brow_[:, q * P:(q + 1) * P], start=True, stop=False)
                    for k in range(KD):
                        for q in range(4):
                            last = mm(bank(j)[32 * q:32 * q + 2, 0:P], lhsT=cT[:, k:16:8], rhs=w[:, k, q * P:(q + 1) * P],
                                      start=False, stop=(k == KD - 1))
                elif kind == "modT":
                    pe.wait_ge(mod_copied, t + 1)
                    for k in range(4):
                        last = tr(bank(j)[:, 2 * k:2 * k + 2], modrow[t % 2][0:2, k * P:(k + 1) * P], ident[0:2, 0:2])
                elif kind == "xT":
                    pe.wait_ge(x_norm, T)
                    for tt in range(T):
                        r = ROWS[tt]
                        dst = bank(j, 1)[:, 0:r] if tt == SAMPLE else bank(j)[:, TOK[tt]:TOK[tt] + r]
                        last = tr(dst, xs5[0:r, tt, t * P:(t + 1) * P], ident[0:r, 0:r])
                elif kind in ("qi", "kv", "qa", "vg", "rg"):
                    chunk_in(pe, (kind, 0))
                    if kind == "qi":
                        in_sbuf(pe, ("xT", KD - 1))
                    n = {"qi": 324, "kv": 256}.get(kind, CW)
                    w = wslot(CH[(kind, 0)] % FRONT_RING)
                    if t == SAMPLE:
                        last = sample_product(j, 0, hT, w)
                    for k in range(KD if t != SAMPLE else 0):
                        last = mm(bank(j)[0:R, 0:n], lhsT=hT[:, k, tok], rhs=w[:, k, 0:n], start=(k == 0), stop=(k == KD - 1))
                elif kind in ("lr", "qkg"):
                    c = ("kv", 0) if kind == "lr" else ("qkg", 0)
                    chunk_in(pe, c)
                    at_, m = (256, 16) if kind == "lr" else (t * P, P)
                    w = wslot(CH[c] % FRONT_RING)
                    for b, lo_, hi_ in ((0, 0, NTOK // 2), (1, NTOK // 2, NTOK)):
                        for k in range(KD):
                            last = mm(bank(j, b)[0:m, 0:hi_ - lo_], lhsT=w[:, k, at_:at_ + m], rhs=hT[:, k, lo_:hi_],
                                      start=(k == 0), stop=(k == KD - 1))
                elif kind == "qiT":
                    pe.wait_ge(qi_roped, ORDER.index(t) + 1)
                    for k in range(2):
                        tr(bank(j)[:, k * R:(k + 1) * R], qro[0:R, t, k * P:(k + 1) * P], ident[0:R, 0:R])
                    for half in range(2):
                        last = mm(bank(j)[64 * half:64 * half + 64, 2 * R:3 * R], lhsT=qro[0:R, t, 256:320],
                                  rhs=ident[0:R, 0:R], start=True, stop=True)
                elif kind == "cacheT":
                    pe.wait_ge(cache_in, 48)
                    for half in range(2):
                        mm(bank(j)[64 * half:64 * half + 64, 0:P], lhsT=ckidx[:, t, :], rhs=ident, start=True, stop=True)
                    last = tr(bank(j, 1)[:, 0:P], ck[:, t, :], ident)
                elif kind in ("idx", "idxnew"):
                    h = s[2]
                    ps = slice(64 * (h % 2), 64 * (h % 2) + 64)
                    keys = kiTs if t == SAMPLE else kiT
                    if h == 0 and kind == "idx":
                        in_sbuf(pe, ("qiT", t))
                        in_sbuf(pe, ("cacheT", 7))
                    spans = [(1024, 1056)] if kind == "idxnew" else \
                        [(x, min(x + 512, min(NKEYS[t], 1024))) for x in range(0, min(NKEYS[t], 1024), 512)]
                    for b, (lo_, hi_) in enumerate(spans):
                        last = mm(bank(j, b)[0:R, 0:hi_ - lo_], lhsT=qiT[ps, h // 2, tok], rhs=keys[ps, lo_:hi_],
                                  start=True, stop=True)
                elif kind == "qaT":
                    pe.wait_ge(raw_used, T + ORDER.index(t) + 1)
                    for k in range(4):
                        tr(bank(j)[:, k * R:(k + 1) * R], qaro[0:R, t, k * P:(k + 1) * P], ident[0:R, 0:R])
                    last = tr(bank(j, 1)[:, 0:R], kro[0:R, t, :], ident[0:R, 0:R])
                elif kind == "z":
                    in_sbuf(pe, ("lr",))
                    pe.wait_ge(tabs_in, 64)
                    for b, lo_, hi_ in ((0, 0, SEQ), (1, SEQ, NTOK)):
                        last = mm(bank(j, b)[:, 0:hi_ - lo_], lhsT=wgate[0:16, t * P:(t + 1) * P], rhs=lrT[0:16, lo_:hi_],
                                  start=True, stop=True)
                elif kind == "kd":
                    pe.wait_ge(gla_made, 8)
                    for x in range(2):
                        last = tr(bank(j)[0:R, x * P:(x + 1) * P], gkd[:, x, tok], ident)
                elif kind == "gs":
                    pe.wait_ge(gla_made, 8)
                    S = min(CHUNK, R)
                    for c in range(R // S):
                        po = slice(c * CHUNK, c * CHUNK + S)
                        kc = slice(TOK[t] + c * CHUNK, TOK[t] + c * CHUNK + S)
                        for h in range(NBH):
                            ps = slice(64 * (h % 2), 64 * (h % 2) + 64)
                            for b in range(S // 32):
                                q0 = TOK[t] + c * CHUNK + 32 * b
                                kk = gk1 if b else gk0
                                col = (h // 2) * 64 + 32 * b
                                last = mm(bank(j, h % 2)[po, col:col + 32], lhsT=kk[ps, h // 2, kc],
                                          rhs=gqA[ps, h // 2, q0:q0 + 32], start=True, stop=True)
                elif kind == "gst":
                    in_sbuf(pe, ("kd", t))
                    S = min(CHUNK, R)
                    ks = slice(s[2] * CHUNK, s[2] * CHUNK + S)
                    for h in range(NBH):
                        last = mm(bank(j)[64 * (h % 2):64 * (h % 2) + 64, (h // 2) * DV:(h // 2 + 1) * DV],
                                  lhsT=kdn[ks, t, h * 64:(h + 1) * 64], rhs=vg[ks, t, h * DV:(h + 1) * DV],
                                  start=True, stop=True)
                elif kind == "gi":
                    if t == SAMPLE:
                        pe.wait_ge(state_in, 16)
                    else:
                        in_sbuf(pe, ("gst", t, 0))
                    S = min(CHUNK, R)
                    for c in range(R // S):
                        po = slice(c * CHUNK, c * CHUNK + S)
                        qc = slice(TOK[t] + c * CHUNK, TOK[t] + c * CHUNK + S)
                        st = states[4] if t == SAMPLE else states[(2 * t + c) % 4]
                        for h in range(NBH):
                            ps = slice(64 * (h % 2), 64 * (h % 2) + 64)
                            last = mm(bank(j, h % 2)[po, (h // 2) * DV:(h // 2 + 1) * DV], lhsT=gqe[ps, h // 2, qc],
                                      rhs=st[ps, h // 2, :], start=True, stop=True)
                elif kind == "go":
                    in_sbuf(pe, ("gs", t))
                    S = min(CHUNK, R)
                    for c in range(R // S):
                        po = slice(c * CHUNK, c * CHUNK + S)
                        for h in range(NBH):
                            col = (h % 2) * 128 + (h // 2) * 64
                            last = mm(bank(j)[po, h * DV:(h + 1) * DV], lhsT=scT[t % 2][po, col:col + S],
                                      rhs=vg[po, t, h * DV:(h + 1) * DV], start=True, stop=True)
                elif kind in ("sc", "scnew"):
                    h = s[2]
                    g0 = 64 * (h if t == SAMPLE else h // 4)
                    ps = slice(g0, g0 + 64)
                    keys, qs = (kTs, qaTs[ps, :]) if t == SAMPLE else (kaT, qaT[ps, h % 4, tok])
                    if h == 0:
                        in_sbuf(pe, ("qaT", t))
                    spans = [(1024, 1056)] if kind == "scnew" else \
                        [(x, min(x + 512, min(NKEYS[t], 1024))) for x in range(0, min(NKEYS[t], 1024), 512)]
                    for b, (lo_, hi_) in enumerate(spans):
                        last = mm(bank(j, b)[:, 0:hi_ - lo_], lhsT=qs, rhs=keys[ps, lo_:hi_],
                                  start=True, stop=True)
                elif kind in ("pT", "pTnew"):
                    u = UNIT[s[1:]]
                    pe.wait_ge(probs_made, u + 1)
                    if kind == "pTnew":
                        last = tr(bank(j)[0:DEC, 0:P], prob[u % 3][:, PAST:PAST + DEC], ident)
                    for x in range(min(NKEYS[t], PAST) // P if kind == "pT" else 0):
                        last = tr(group(j)[:, x * P:(x + 1) * P], prob[u % 3][:, x * P:(x + 1) * P], ident)
                elif kind == "pv":
                    u = UNIT[s[1:]]
                    in_sbuf(pe, ("pT", *s[1:]))
                    nb = min(NKEYS[t], PAST) // P
                    turned_p, val = (pTs[s[2]][0], Vs) if t == SAMPLE else (pT[u % 2], va)
                    for x in range(nb):
                        last = mm(bank(j)[:, 0:P], lhsT=turned_p[:, x * P:(x + 1) * P], rhs=val[:, x, :],
                                  start=(x == 0), stop=(x == nb - 1 and t != SAMPLE))
                    if t == SAMPLE:
                        in_sbuf(pe, ("pTnew", *s[1:]))
                        last = mm(bank(j)[:, 0:P], lhsT=pTs[s[2]][1][0:DEC, :], rhs=Vs[0:DEC, nb, :], start=False, stop=True)
                elif kind == "catT":
                    in_sbuf(pe, ("pv", t, LAST[t]))
                    pe.wait_ge(o_done, t + 1)
                    for k in range(KD):
                        src = catA[0:R, t, k * P:(k + 1) * P] if k < 4 else rg[0:R, t, (k - 4) * P:(k - 3) * P]
                        last = tr(group(j)[:, k * R:(k + 1) * R], src, ident[0:R, 0:R])
                elif kind == "y":
                    in_sbuf(pe, ("catT", t))
                    for n in range(2):
                        chunk_in(pe, ("out", n))
                        w = wslot(CH[("out", n)] % FRONT_RING)
                        if t == SAMPLE:
                            last = sample_product(j, n, catT, w)
                        for k in range(KD if t != SAMPLE else 0):
                            last = mm(bank(j, n)[0:R, :], lhsT=catT[:, k, tok], rhs=w[:, k, :], start=(k == 0), stop=(k == KD - 1))
                elif kind == "hT":
                    pe.wait_ge(h2_made, t + 1)
                    for k in range(KD):
                        last = tr(group(j)[:, k * R:(k + 1) * R], h2b[t % 2][0:R, k * P:(k + 1) * P], ident[0:R, 0:R])
                elif kind == "rt":
                    in_sbuf(pe, ("hT", t))
                    pe.wait_ge(rows_in, ROW_DMAS * 16)
                    for k in range(KD):
                        last = mm(bank(j)[0:R, 0:NE], lhsT=h2T[:, k * R:(k + 1) * R], rhs=wr[:, k, :], start=(k == 0), stop=(k == KD - 1))
                elif kind == "rank":
                    pe.wait_ge(sel_made, T)
                    for tt in range(T + 1):
                        for x in range(min(tt + 1, T)):
                            last = mm(bank(j)[:, tt * NE:(tt + 1) * NE], lhsT=(before if x == tt else ones),
                                      rhs=sel[:, x * NE:(x + 1) * NE], start=(x == 0), stop=(x == min(tt, T - 1)))
                last.then_inc(psum_filled, 1)

            def turn_tokens(i):
                pe.wait_ge(gathered, (i + 1) * 16)
                for k in range(KD):
                    last = tr(psum[:, k // 4, (k % 4) * P:(k % 4 + 1) * P], xg[:, k * P:(k + 1) * P], ident)
                last.then_inc(xg_turned, 1)

            def turn_act(i, half):
                pe.wait_ge(act_ready, i * 2 + half + 2)
                for k in range(4):
                    last = tr(psum[:, 6 + half, k * P:(k + 1) * P], act[:, (4 * half + k) * P:(4 * half + k + 1) * P], ident)
                last.then_inc(act_turned, 1)

            def down(i, half):
                c = 4 + half
                pe.wait_ge(actT_ready, i * 2 + half + 1)
                pe.wait_ge(loaded[c], i * 16 + FRONT_TOTAL[c] + 16)
                w = slot(c).rearrange("p (k n) -> p k n", k=4)
                for n in range(2):
                    for k in range(4):
                        last = mm(psum[:, 4 + n, :], lhsT=actT[:, 4 * half + k, :], rhs=w[:, k, n * 512:(n + 1) * 512],
                                  start=(half == 0 and k == 0), stop=(half == 1 and k == 3))
                last.then_inc(chunk_done, 1)

            def expert_pe(i):
                pe.wait_ge(xgT_ready, i + 1)
                for c in range(4):
                    pe.wait_ge(loaded[c], i * 16 + FRONT_TOTAL[c] + 16)
                    for k in range(KD):
                        last = mm(psum[:, c, :], lhsT=xgT[:, k, :], rhs=wslot(c)[:, k, :], start=(k == 0), stop=(k == KD - 1))
                    last.then_inc(chunk_done, 1)
                    if c == 2:
                        turn_act(i, 0)
                pe.wait_ge(ys_ready, i + 1)
                down(i, 0)
                turn_act(i, 1)
                turn_tokens(i + 1)
                down(i, 1)

            in_sbuf(pe, ("rank",))
            in_sbuf(pe, ("rt", T - 1))
            turn_tokens(0)
            with pe.Fori(0, NE) as i:
                expert_pe(i)
            pe.wait_ge(routed, 1)
            n_over = pe.value_load(over[0:1, NOV:NOV + 1], min_val=0, max_val=NOV)
            with pe.If(n_over > 0):
                with pe.Fori(0, n_over) as jj:
                    expert_pe(jj + NE)


INS = ["x_prompt", "x_sample", "cache_k", "cache_v", "cache_kidx", "state_gla", "c_prompt", "c_sample", "w_mod", "b_mod",
       "g_mix", "g_ffn", "w_in", "gla_w_gate", "gla_b_gate", "gla_g_out", "w_out", "w_router", "b_router", "w_gate_up",
       "b_gate_up", "w_down", "b_down", "w_mod_final", "b_mod_final", "g_final"]
OUTS = [(1, SEQ, D), (1, DEC, D), (1, 1, SEQ, 2, HD), (1, 1, SEQ, 2, HD), (1, 1, SEQ, HD), (1, 1, NBH, HD, DV),
        (1, 1, DEC, 2, HD), (1, 1, DEC, 2, HD), (1, 1, DEC, HD), (1, 1, NBH, HD, DV)]


def rope_table(np):
    half = HD // 2
    inv = (10000.0 ** (-np.arange(half, dtype=np.float64) / half)).astype(np.float32)
    pos = np.concatenate([np.arange(SEQ), PAST + np.arange(DEC)]).astype(np.float32)
    ang = (pos[:, None] * inv[None, :]).astype(np.float64)
    return np.concatenate([np.cos(ang), np.cos(ang), -np.sin(ang), np.sin(ang)], 1).astype(np.float32)


def kernel(**inputs):
    import numpy as np
    import concourse.bacc as bacc
    from concourse.bass_utils import run_bass_kernel_spmd

    nc = bacc.Bacc("TRN2", target_bir_lowering=False, num_devices=1)
    arrays, aps = {}, {}
    for name in INS:
        arrays[f"in_{name}"] = np.ascontiguousarray(inputs[name])
    arrays["in_rope"] = rope_table(np)
    for name, x in arrays.items():
        aps[name[3:]] = nc.dram_tensor(name, x.shape, mybir.dt.from_np(x.dtype), kind="ExternalInput").ap()
    outs = [nc.dram_tensor(f"out_{i}", shape, F32, kind="ExternalOutput").ap() for i, shape in enumerate(OUTS)]
    build(nc, aps, outs)
    r = run_bass_kernel_spmd(nc, [arrays], core_ids=[0])
    return tuple(r.results[0][f"out_{i}"] for i in range(len(OUTS)))
```

```python
from contextlib import ExitStack

import concourse.bass as bass
from concourse import mybir

F32 = mybir.dt.float32
F32R = mybir.dt.float32r
I32 = mybir.dt.int32
U32 = mybir.dt.uint32
ALU = mybir.AluOpType
ACT = mybir.ActivationFunctionType
AX = mybir.AxisListType

P = 128
D = 1024
KD = D // P
SEQ, DEC, PAST = 512, 32, 1024
NTOK = SEQ + DEC
T = 5
ROWS = [P, P, P, P, DEC]
TOK = [0, 128, 256, 384, 512]
SAMPLE = 4
HD = 64
NH, NIH, NBH, DV = 8, 4, 4, 128
NKEYS = [128, 256, 384, 512, PAST + DEC]
TOPK_PROMPT, TOPK_SAMPLE = min(256, SEQ // 4), min(256, (PAST + DEC) // 4)
CHUNK = 64
NE, TOPE = 32, 4
NOV = NTOK * TOPE // P - 1
NBLK = NE + NOV + 1
EPS = 1e-6
NEG = -3.0e38
MASKED = -1.0e30
CW = 512
SLOT = KD * CW
FRONT_RING = 3
RAW, SPLIT = 3, 3
BCH = 6
CHUNK0 = 3
POOL_PART = 512
LIMIT, ALPHA = 7.0, 1.702

QA, KA, VA, QI, KI, WI, QG, KG, VG, LR, RG = 0, 512, 640, 768, 1024, 1088, 1092, 1348, 1604, 2116, 2132
ORDER = [SAMPLE, 0, 1, 2, 3]
UNITS = [(SAMPLE, 0), (SAMPLE, 1)] + [(t, h) for t in range(4) for h in range(NH)]
LAST = [NH - 1] * 4 + [1]
UNIT = {x: u for u, x in enumerate(UNITS)}


def front_chunks():
    c, m = [("mod", n) for n in range(4)], 4
    for x, more in (("qi", 2), ("kv", 3), ("qa", 3), ("qkg", 2), ("vg", 2), ("rg", 0)):
        c += [(x, 0)] + [("mod", m + n) for n in range(more)]
        m += more
    return c + [("out", 0), ("out", 1)]


def steps():
    s = [("c",)]
    for n in range(4):
        s += [("mod", n), ("modT", n)]
    s += [("xT", k) for k in range(KD)]
    s += [("qi", t) for t in ORDER]
    s += [("qiT", t) for t in ORDER]
    s += [("cacheT", i) for i in range(PAST // P)]
    s += [("mod", 4), ("mod", 5)]
    for t in ORDER:
        for h in range(NIH):
            s.append(("idx", t, h))
            if t == SAMPLE:
                s.append(("idxnew", t, h))
    s += [("kv", t) for t in ORDER] + [("lr",), ("mod", 6), ("mod", 7), ("mod", 8)]
    s += [("qa", t) for t in ORDER] + [("mod", 9), ("mod", 10), ("mod", 11)]
    s += [("qaT", t) for t in ORDER]
    s += [("qkg", j) for j in range(4)] + [("mod", 12), ("mod", 13)]
    s += [("vg", t) for t in ORDER] + [("mod", 14), ("mod", 15)]
    s += [("z", j) for j in range(2)]
    s += [("rg", t) for t in ORDER]
    s += [("kd", t) for t in range(T)]
    gla = []
    for t in range(T):
        gla += [("gs", t), ("gst", t, 0)]
        if t != SAMPLE:
            gla += [("gst", t, 1)]
        gla += [("gi", t), ("go", t)]
    for u in range(len(UNITS) + 3):
        if u < len(UNITS):
            s.append(("sc", *UNITS[u]))
            if UNITS[u][0] == SAMPLE:
                s.append(("scnew", *UNITS[u]))
        if 2 <= u < len(UNITS) + 2:
            s.append(("pT", *UNITS[u - 2]))
            if UNITS[u - 2][0] == SAMPLE:
                s.append(("pTnew", *UNITS[u - 2]))
        pace = 2 if u < 4 else 1
        s += gla[:pace]
        gla = gla[pace:]
        if u >= 3:
            s.append(("pv", *UNITS[u - 3]))
    assert not gla
    s += [("catT", t) for t in range(T)]
    s += [("y", 0), ("y", 1), ("hT", 0)]
    for t in range(T):
        if t + 2 < T:
            s.append(("y", t + 2))
        s.append(("rt", t))
        if t + 1 < T:
            s.append(("hT", t + 1))
    s += [("rank",)]
    return s


STEPS = steps()
JOB = {s: j for j, s in enumerate(STEPS)}
NJOBS = len(STEPS)


class Carver:

    def __init__(self, ap, words):
        self.ap, self.at, self.words = ap, 0, words

    def take(self, words):
        assert self.at + words <= self.words, (self.at, words, self.words)
        self.at += words
        return self.ap[:, self.at - words:self.at]


def build(nc, a, outs):
    (y_prompt, y_sample, k_prompt, v_prompt, ki_prompt, gla_prompt, k_sample, v_sample, ki_sample,
     gla_sample) = outs
    ctx = ExitStack()
    with ctx:
        def sem(name):
            return ctx.enter_context(nc.semaphore(name))

        def dram(name, shape, dt=F32):
            return nc.dram_tensor(name, shape, dt, kind="Internal").ap()

        mod_dram = dram("mod_dram", [2, 8 * D])
        x2_dram = dram("x2_dram", [NTOK, D])
        h_dram = dram("h_dram", [NTOK, D])
        slot_dram = dram("slot_dram", [P * NBLK, 1], I32)
        ys_dram = dram("ys_dram", [(1 + NE + NOV) * P, D])

        raw_ring = ctx.enter_context(nc.sbuf_tensor("raw_ring", [P, RAW * SLOT], F32))
        KEEP, WORK = 1362, 27200
        keep_t = ctx.enter_context(nc.sbuf_tensor("keep", [P, KEEP], F32))
        AREA = FRONT_RING * SLOT + WORK
        with ExitStack() as front:
            ring = front.enter_context(nc.sbuf_tensor("front_ring", [P, FRONT_RING * SLOT], F32))
            work_t = front.enter_context(nc.sbuf_tensor("work", [P, WORK], F32))
        with ExitStack() as experts:
            SPLIT_WORDS, EX_WORDS = 2 * SPLIT * SLOT + 4 * D, 9 * D + 3 * CW
            assert SPLIT_WORDS + EX_WORDS <= AREA
            split_t = experts.enter_context(nc.sbuf_tensor("split", [P, SPLIT_WORDS], F32R))
            ex_t = experts.enter_context(nc.sbuf_tensor("expert_work", [P, EX_WORDS], F32))
        NF = 3
        FIN_WORDS = (6 * NF + 8) * D
        with nc.sbuf_tensor("final_work", [P, FIN_WORDS], F32) as fin_t:
            pass
        psum = ctx.enter_context(nc.psum_tensor("psum", [P, 8, 512], F32))

        def wslot(n):
            return ring[:, n * SLOT:(n + 1) * SLOT].rearrange("p (k n) -> p k n", k=KD)

        def raw_slot(c):
            return raw_ring[:, c % RAW * SLOT:(c % RAW + 1) * SLOT]

        def high(c):
            return split_t[:, c % SPLIT * SLOT:(c % SPLIT + 1) * SLOT]

        def low(c):
            return split_t[:, (SPLIT + c % SPLIT) * SLOT:(SPLIT + c % SPLIT + 1) * SLOT]

        keep = Carver(keep_t, KEEP)
        ident = keep.take(P)
        before = keep.take(P)
        ones = keep.take(P)
        gates = keep.take(T * TOPE)
        chosen = keep.take(T * TOPE)
        ys_row = keep.take(T * TOPE).bitcast(I32)
        tab_pos = keep.take(T * TOPE).bitcast(I32)
        tok_id = keep.take(8).bitcast(I32)
        slot_tok = keep.take(NBLK).bitcast(I32)
        over = keep.take(NOV + 1).bitcast(I32)
        small = keep.take(300)
        sel = keep.take(T * NE)
        iota_e = keep.take(NE)
        idx_now = keep.take(1).bitcast(I32)
        pick2 = keep.take(2)
        zero_i = keep.take(NBLK).bitcast(I32)

        hi = Carver(raw_ring, RAW * SLOT)
        lo = Carver(work_t, WORK)
        hT = lo.take(KD * NTOK).rearrange("p (k n) -> p k n", k=KD)
        qiT = lo.take(2 * NTOK).rearrange("p (k n) -> p k n", k=2)
        kiT = lo.take(NTOK)
        qaT = lo.take(4 * NTOK).rearrange("p (k n) -> p k n", k=4)
        kaT = lo.take(NTOK)
        va = lo.take(T * P).rearrange("p (t n) -> p t n", t=T)
        score = [lo.take(n) for n in NKEYS]
        kiTs = lo.take(PAST + DEC)
        kTs = lo.take(PAST + DEC)
        Vs = lo.take(9 * P).rearrange("p (t n) -> p t n", t=9)
        cs = lo.take(T * 128).rearrange("p (t n) -> p t n", t=T)
        gmask = lo.take(256).bitcast(I32)
        gout_b = lo.take(P)
        wgate = lo.take(256)
        vT = lo.take(16)
        cT = lo.take(16)
        colT = lo.take(32)
        a1 = lo.take(16)
        cc = lo.take(P)
        csg = lo.take(P)
        vecs = lo.take(P)
        wis = lo.take(T * 4).rearrange("p (t n) -> p t n", t=T)
        m8 = lo.take(8)
        lrT = lo.take(NTOK)
        gT2 = lo.take(NTOK)
        vg = hi.take(T * 512).rearrange("p (t n) -> p t n", t=T)
        rg = hi.take(T * 512).rearrange("p (t n) -> p t n", t=T)
        xs5 = raw_ring[:, 0:T * D].rearrange("p (t n) -> p t n", t=T)
        catA = hi.take(T * 512).rearrange("p (t n) -> p t n", t=T)
        qaro = catA
        catA_flat = catA.rearrange("p t n -> p (t n)")
        qgT = hi.take(2 * NTOK).rearrange("p (k n) -> p k n", k=2)
        kgT = hi.take(2 * NTOK).rearrange("p (k n) -> p k n", k=2)
        STAGE = 9280
        pr = Carver(lo.take(STAGE), STAGE)
        qro = pr.take(T * 320).rearrange("p (t n) -> p t n", t=T)
        qiraw = [pr.take(324), pr.take(324)]
        raw = [pr.take(512), pr.take(512)]
        kro = pr.take(T * P).rearrange("p (t n) -> p t n", t=T)
        prefix = pr.take(2048)
        rel = [prefix[:, 0:1024], prefix[:, 1024:2048]]
        rope_p = pr.take(512)
        ckidx = pr.take(8 * 64).rearrange("p (t n) -> p t n", t=8)
        ck = pr.take(8 * 128).rearrange("p (t n) -> p t n", t=8)
        modrow = [pr.take(CW), pr.take(CW)]
        cache_flat = pr.ap[:, pr.at - 2 * CW - 1536:pr.at - 2 * CW]
        bmod = [catA_flat[:, n * CW:(n + 1) * CW] for n in range(FRONT_RING)]
        EARLY_MODS = 6
        bmod2 = [cache_flat[:, n * CW:(n + 1) * CW] for n in range(FRONT_RING)]
        twork = hi.take(PAST + DEC)
        gl = Carver(pr.ap, STAGE)
        bT = gl.take(2 * NTOK).rearrange("p (k n) -> p k n", k=2)
        gqA = gl.take(2 * NTOK).rearrange("p (k n) -> p k n", k=2)
        gk0 = gl.take(2 * NTOK).rearrange("p (k n) -> p k n", k=2)
        gk1 = gl.take(2 * SEQ).rearrange("p (k n) -> p k n", k=2)
        gqe = gl.take(2 * NTOK).rearrange("p (k n) -> p k n", k=2)
        gkd = gl.take(2 * NTOK).rearrange("p (k n) -> p k n", k=2)
        kdn = gl.take(T * 256).rearrange("p (t n) -> p t n", t=T)
        states = [gl.take(256).rearrange("p (j n) -> p j n", j=2) for _ in range(6)]
        scT = [hi.take(256), hi.take(256)]
        ot = hi.take(512)
        eL = lo.take(18).rearrange("p (j n) -> p j n", j=2)
        at = Carver(hT.rearrange("p k n -> p (k n)"), KD * NTOK)
        prob = [at.take(PAST + DEC) for _ in range(3)]
        gT1 = [qiT[:, 0, :], qiT[:, 1, :]]
        graw = [kiTs[:, 0:512], kiTs[:, 512:1024]]
        pTs = [(qiT.rearrange("p k n -> p (k n)")[:, 0:1024], kiT[:, 0:P]), (kiTs[:, 0:1024], kiT[:, P:2 * P])]
        qaTs = csg
        osum = [cc[:, 0:64], cc[:, 64:128]]
        pT = [at.take(512), at.take(512)]
        amx = at.take(16)
        ars = at.take(16)
        op = Carver(work_t, WORK)
        catT = op.take(KD * NTOK).rearrange("p (k n) -> p k n", k=KD)
        rowP = [op.take(D) for _ in range(3)]
        rowS = [op.take(D) for _ in range(3)]
        gffn_b = op.take(D)
        xin = [op.take(D), op.take(D)]
        x2b = [op.take(D), op.take(D)]
        h2b = [op.take(D), op.take(D)]
        junk = op.take(D)
        h2T = op.take(D)
        wr = op.take(KD * NE).rearrange("p (k n) -> p k n", k=KD)
        br_b = op.take(NE)
        oneh = op.take(T * TOPE * NE)
        rank = op.take(T * NE + NE)
        tmpn = op.take(NOV * NE)
        iota_j = op.take(NOV * NE)
        xb_, xe_, xst = op.take(NE), op.take(NE), op.take(NE)
        rj = op.take(NE)
        pick_t = op.take(T * TOPE * NE)
        sel_before = op.take((T + 1) * NE)
        turned_parts = Carver(split_t[:, 2 * SPLIT * SLOT:SPLIT_WORDS], 4 * D)
        xgT_hi, xgT_lo, actT_hi, actT_lo = (turned_parts.take(D).rearrange("p (k n) -> p k n", k=KD) for _ in range(4))
        ex = Carver(ex_t, EX_WORDS)
        xg, act = ex.take(D), ex.take(D)
        eg, eu, es = ex.take(512), ex.take(512), ex.take(512)
        ysb = ex.take(D)
        brow = ex.take(3 * D)
        bias_b = ex.take(3 * D)
        fi = Carver(fin_t, FIN_WORDS)
        yg = [fi.take(4 * D) for _ in range(NF)]
        xf = [fi.take(D) for _ in range(NF)]
        fo = [fi.take(D) for _ in range(NF)]
        facc = fi.take(D)
        fP = [fi.take(D) for _ in range(3)]
        fS = [fi.take(D) for _ in range(3)]
        gfin_b = fi.take(D)

        sm = Carver(small, 300)
        ss, vv, rr, r2, r3 = (sm.take(8) for _ in range(5))
        ss4, vv4, rr4 = (sm.take(4) for _ in range(3))
        cgt, thr8, ngate = sm.take(1), sm.take(8), sm.take(1)
        v8 = sm.take(8)
        i8 = sm.take(8).bitcast(U32)
        e4 = sm.take(4)
        gs1, gr1 = sm.take(1), sm.take(1)
        nR = T * TOPE
        f1, f2, f3, f4, f5, f6, f7 = (sm.take(nR) for _ in range(7))
        negm = sm.take(16)
        rinv = sm.take(16)
        table_pull = sm.take(1)
        ovf = sm.take(NOV + 1)

        psum_filled = sem("psum_filled")
        psum_drained = [sem(f"psum_drained{g}") for g in range(4)]
        loaded = [sem(f"loaded{n}") for n in range(FRONT_RING)]
        raw_in = [sem(f"raw_in{n}") for n in range(RAW)]
        high_made, split_dve, split_pool = sem("high_made"), sem("split_dve"), sem("split_pool")
        xgT_high, actT_high = sem("xgT_high"), sem("actT_high")
        consts = sem("consts")
        c_in, x_in, cache_in, tabs_in = sem("c_in"), sem("x_in"), sem("cache_in"), sem("tabs_in")
        c_sig, c_silu = sem("c_sig"), sem("c_silu")
        x_sq, x_var, x_sqrt, x_norm = sem("x_sq"), sem("x_var"), sem("x_sqrt"), sem("x_norm")
        mod_copied, bias_clear = sem("mod_copied"), sem("bias_clear")
        mod_stored = [sem("mod_stored0"), sem("mod_stored1")]
        a1_made = sem("a1_made")
        qi_roped, raw_used = sem("qi_roped"), sem("raw_used")
        rel_used = sem("rel_used")
        masks_made, mask_spread = sem("masks_made"), sem("mask_spread")
        act_s = sem("act_order")
        dve_s = sem("dve_order")
        pool_s = sem("pool_order")
        new_keys = sem("new_keys")
        out_kv, out_ki, out_state = sem("out_kv"), sem("out_ki"), sem("out_state")
        rg_gated = sem("rg_gated")
        gate_z, gate_l = sem("gate_z"), sem("gate_l")
        gla_in, gla_exp, gla_made = sem("gla_in"), sem("gla_exp"), sem("gla_made")
        state_in = sem("state_in")
        o_sum, o_sq, o_var, o_sqrt, o_done = (sem(n) for n in ("o_sum", "o_sq", "o_var", "o_sqrt", "o_done"))
        logits_max, probs_made = sem("logits_max"), sem("probs_made")
        rows_in, x_again = sem("rows_in"), [sem("x_again0"), sem("x_again1")]
        rows_made = sem("rows_made")
        x2_made, x2_sq, x2_var, x2_sqrt, h2_made = (sem(n) for n in ("x2_made", "x2_sq", "x2_var", "x2_sqrt", "h2_made"))
        x2_stored = [sem("x2_stored0"), sem("x2_stored1")]
        h2_stored = [sem("h2_stored0"), sem("h2_stored1")]
        top_ready, gate_exp, sel_made = sem("top_ready"), sem("gate_exp"), sem("sel_made")
        routed, tab_zero, tab_written, tab_in = sem("routed"), sem("tab_zero"), sem("tab_written"), sem("tab_in")
        chunk_done = sem("chunk_done")
        bias_in, bias_ready, bias_gu_used, bias_dn_used = (sem(n) for n in ("bias_in", "bias_ready", "bias_gu_used", "bias_dn_used"))
        gathered, xg_turned, xgT_ready = sem("gathered"), sem("xg_turned"), sem("xgT_ready")
        gate_added, gate_sig, act_ready = sem("gate_added"), sem("gate_sig"), sem("act_ready")
        act_turned, actT_ready = sem("act_turned"), sem("actT_ready")
        ys_ready, ys_stored = sem("ys_ready"), sem("ys_stored")
        gu_added, experts_done = sem("gu_added"), sem("experts_done")
        fin_rows = sem("fin_rows")
        fin_x = [sem(f"fin_x{n}") for n in range(NF)]
        fin_y = [sem(f"fin_y{n}") for n in range(NF)]
        f_made, f_sq, f_var, f_sqrt, f_out = (sem(n) for n in ("f_made", "f_sq", "f_var", "f_sqrt", "f_out"))
        f_stored = [sem(f"f_stored{n}") for n in range(NF)]
        idx_copied = sem("idx_copied")
        ys_cleared = sem("ys_cleared")
        pool_settled = sem("pool_settled")
        ss_clear, gate_mask, iota_made = sem("ss_clear"), sem("gate_mask"), sem("iota_made")

        def note(eng, s):
            eng.sem_inc(s, 1)

        ROW_DMAS = 9

        class Order:

            def __init__(self, eng, s):
                self.eng, self.s, self.n = eng, s, 0

            def __call__(self, ins):
                self.n = self.n + 1
                ins.then_inc(self.s, 1)
                self.eng.wait_ge(self.s, self.n)

        def bank(j, b=0):
            return psum[:, 2 * (j % 4) + b, :]

        def group(j):
            return psum[:, 2 * (j % 4):2 * (j % 4) + 2, :].rearrange("p b n -> p (b n)")

        SPAN = {"qi": 81, "kv": 64, "qa": P, "vg": P, "rg": P, "y": P}

        def halves(ap):
            return ap.rearrange("p (b n) -> p b n", b=2)

        def turned(j):
            return psum[:, 2 * (j % 4):2 * (j % 4) + 2, 0:NTOK // 2]

        def filled(eng, j):
            eng.wait_ge(psum_filled, j + 1)

        def in_sbuf(eng, step):
            j = JOB[step]
            eng.wait_ge(psum_drained[j % 4], j // 4 + 1)

        def free_group(eng, j):
            if j >= 4:
                eng.wait_ge(psum_drained[j % 4], j // 4)

        chunks = front_chunks()
        CH = {c: n for n, c in enumerate(chunks)}
        NCH = len(chunks)
        assert NCH % FRONT_RING == 0
        last_step = {}
        for s in STEPS:
            key = {"mod": ("mod", s[1] if len(s) > 1 else 0), "lr": ("kv", 0), "qi": ("qi", 0), "kv": ("kv", 0),
                   "qa": ("qa", 0), "qkg": ("qkg", 0), "vg": ("vg", 0), "rg": ("rg", 0)}.get(s[0])
            if key:
                last_step[key] = s
            if s[0] == "y":
                last_step[("out", 0)] = last_step[("out", 1)] = s
        parts = [2 if c[0] in ("mod", "kv") else 1 for c in chunks]
        need = []
        tot = [0] * FRONT_RING
        for n in range(NCH):
            tot[n % FRONT_RING] += 16 * parts[n]
            need.append(tot[n % FRONT_RING])

        def chunk_in(eng, c):
            eng.wait_ge(loaded[CH[c] % FRONT_RING], need[CH[c]])

        w_in = a["w_in"][0].rearrange("(k p) n -> p k n", p=P)
        w_mod = a["w_mod"][0].rearrange("(k p) n -> p k n", p=P)
        w_modf = a["w_mod_final"].rearrange("(k p) n -> p k n", p=P)
        w_out = a["w_out"][0].rearrange("(k p) n -> p k n", p=P)
        w_gu = a["w_gate_up"][0].rearrange("e (k p) n -> e p k n", p=P)
        w_dn = a["w_down"][0].rearrange("e (k p) n -> e p k n", p=P)
        x_p, x_s = a["x_prompt"][0], a["x_sample"][0]

        def x_rows(t):
            return x_s if t == SAMPLE else x_p[TOK[t]:TOK[t] + P, :]

        def chunk_cols(c):
            kind, n = c
            if kind == "mod":
                w = w_mod[:, :, n * CW:(n + 1) * CW] if n < 12 else w_modf[:, :, (n - 12) * CW:(n - 11) * CW]
                return [(0, CW, w)]
            if kind == "qi":
                return [(0, 324, w_in[:, :, QI:QI + 324])]
            if kind == "kv":
                return [(0, 256, w_in[:, :, KA:KA + 256]), (256, 16, w_in[:, :, LR:LR + 16])]
            if kind == "out":
                return [(0, CW, w_out[:, :, n * CW:(n + 1) * CW])]
            at_ = {"qa": QA, "qkg": QG, "vg": VG, "rg": RG}[kind]
            return [(0, CW, w_in[:, :, at_:at_ + CW])]

        block = ctx.enter_context(nc.Block())

        @block.sync
        def _(sp):
            for n, c in enumerate(chunks):
                if n >= FRONT_RING:
                    old = chunks[n - FRONT_RING]
                    filled(sp, JOB[last_step[old]])
                s = n % FRONT_RING
                for at_, w, src in chunk_cols(c):
                    sp.dma_start(wslot(s)[:, :, at_:at_ + w], src).then_inc(loaded[s], 16)
                if c[0] == "mod":
                    m = c[1]
                    b = a["b_mod"][0, m * CW:(m + 1) * CW] if m < 12 else a["b_mod_final"][(m - 12) * CW:(m - 11) * CW]
                    if m == 0:
                        sp.wait_ge(bias_clear, 1)
                    if m == EARLY_MODS:
                        filled(sp, JOB[("cacheT", 7)])
                    sp.dma_start((bmod if m < EARLY_MODS else bmod2)[s][0:1, :], b.unsqueeze(0)).then_inc(loaded[s], 16)

            def chunk(i, c, e):
                if not (isinstance(i, int) and i == 0 and c < RAW):
                    sp.wait_ge(split_dve, i * BCH + c + 1)
                    sp.wait_ge(split_pool, i * BCH + c + 1)
                if c < 4:
                    n = (c // 2) + 2 * (c % 2)
                    src = w_gu[bass.ds(e, 1), :, :, n * CW:(n + 1) * CW].rearrange("e p k n -> p (e k) n")
                    dst = raw_slot(c).rearrange("p (k n) -> p k n", k=KD)
                else:
                    src = w_dn[bass.ds(e, 1), :, (c - 4) * 4:(c - 3) * 4, :].rearrange("e p k n -> p (e k) n")
                    dst = raw_slot(c).rearrange("p (k n) -> p k n", k=4)
                sp.dma_start(dst, src).then_inc(raw_in[c % RAW], 16)

            def bias_rows(e):
                sp.dma_start(brow[0:1, 0:2 * D], a["b_gate_up"][0][bass.ds(e, 1), :]).then_inc(bias_in, 16)
                sp.dma_start(brow[0:1, 2 * D:3 * D], a["b_down"][0][bass.ds(e, 1), :]).then_inc(bias_in, 16)

            def expert_weights(i, e, e_next):
                for c in range(RAW, BCH):
                    chunk(i, c, e)
                sp.wait_ge(bias_ready, i + 1)
                bias_rows(e_next)
                for c in range(RAW):
                    chunk(i + 1, c, e_next)

            for t in range(T):
                filled(sp, JOB[("catT", t)])
            sp.wait_ge(rows_in, ROW_DMAS * 16)
            for c in range(RAW):
                chunk(0, c, 0)
            sp.wait_ge(routed, 1)
            bias_rows(0)
            with sp.Fori(0, NE - 1) as e:
                expert_weights(e, e, e + 1)
            expert_weights(NE - 1, NE - 1, sp.value_load(over[0:1, 0:1], min_val=0, max_val=NE - 1))
            n_over = sp.value_load(over[0:1, NOV:NOV + 1], min_val=0, max_val=NOV)
            with sp.If(n_over > 0):
                with sp.Fori(0, n_over) as j:
                    e = sp.value_load(over[0:1, bass.ds(j, 1)], min_val=0, max_val=NE - 1)
                    e_next = sp.value_load(over[0:1, bass.ds(j + 1, 1)], min_val=0, max_val=NE - 1)
                    expert_weights(j + NE, e, e_next)

            sp.wait_ge(experts_done, 1)
            for n, m in enumerate((5, 6, 7)):
                sp.dma_start(fP[n], mod_dram[0:1, m * D:(m + 1) * D].to_broadcast([P, D])).then_inc(fin_rows, 16)
                sp.dma_start(fS[n][0:DEC, :], mod_dram[1:2, m * D:(m + 1) * D].to_broadcast([DEC, D])).then_inc(fin_rows, 16)
            sp.dma_start(gfin_b, a["g_final"].unsqueeze(0).to_broadcast([P, D])).then_inc(fin_rows, 16)

            def load_x2(t):
                sp.dma_start(xf[t % NF][0:ROWS[t], :], x2_dram[TOK[t]:TOK[t] + ROWS[t], :]).then_inc(fin_x[t % NF], 16)

            for t in range(NF):
                load_x2(t)
            for t in range(T):
                R = ROWS[t]
                sp.wait_ge(f_out, t + 1)
                dst = y_sample[0] if t == SAMPLE else y_prompt[0, TOK[t]:TOK[t] + P, :]
                sp.dma_start(dst, fo[t % NF][0:R, :]).then_inc(f_stored[t % NF], 16)
                if t + NF < T:
                    load_x2(t + NF)
            for n in range(NF):
                sp.wait_ge(f_stored[n], 16 * len(range(n, T, NF)))

        @block.scalar
        def _(act_e):
            order = Order(act_e, act_s)
            sc = nc.scalar

            def leave(dst, j, t, lo_, n, fn=ACT.Copy):
                if t != SAMPLE:
                    return sc.activation(dst, bank(j)[0:ROWS[t], lo_:lo_ + n], fn)
                w = SPAN[STEPS[j][0]]
                for q in range(4):
                    x, y = max(lo_, q * w), min(lo_ + n, (q + 1) * w)
                    if x < y:
                        ins = sc.activation(dst[:, x - lo_:y - lo_], bank(j)[32 * q:32 * q + DEC, x - q * w:y - q * w], fn)
                return ins

            act_e.dma_start(cc[0:8, :], a["c_prompt"].rearrange("o (k p) -> (o k) p", p=P)).then_inc(c_in, 16)
            act_e.dma_start(cc[8:16, :], a["c_sample"].rearrange("o (k p) -> (o k) p", p=P)).then_inc(c_in, 16)
            act_e.dma_start(vecs[0:8, :], a["g_mix"].rearrange("o (k p) -> (o k) p", p=P)).then_inc(c_in, 16)
            act_e.dma_start(vecs[8:10, :], a["gla_b_gate"].rearrange("o (k p) -> (o k) p", p=P)).then_inc(c_in, 16)
            for t in range(T):
                act_e.dma_start(xs5[0:ROWS[t], t, :], x_rows(t)).then_inc(x_in, 16)
            act_e.wait_ge(c_in, 64)
            sc.activation(csg[0:16, :], cc[0:16, :], ACT.Sigmoid).then_inc(c_sig, 1)
            def x_squares():
                act_e.wait_ge(x_in, 16 * T)
                act_e.wait_ge(ss_clear, 1)
                for t in range(T):
                    order(sc.activation(rel[0][0:ROWS[t], :], xs5[0:ROWS[t], t, :], ACT.Square,
                                        accum_out=ss[0:ROWS[t], t:t + 1]))
                note(act_e, x_sq)
                act_e.wait_ge(x_var, 1)
                sc.activation(rr[:, 0:T], vv[:, 0:T], ACT.Sqrt).then_inc(x_sqrt, 1)
                act_e.wait_ge(loaded[1], need[1])
                act_e.dma_start(cs[:, 0:4, :], a["rope"][0:SEQ].rearrange("(t p) n -> p t n", p=P)).then_inc(tabs_in, 16)
                act_e.dma_start(cs[0:DEC, 4, :], a["rope"][SEQ:NTOK]).then_inc(tabs_in, 16)
                act_e.dma_start(wgate[0:16, :], a["gla_w_gate"][0]).then_inc(tabs_in, 16)
                act_e.dma_start(gout_b, a["gla_g_out"].to_broadcast([P, DV])).then_inc(tabs_in, 16)
                act_e.dma_start(ckidx, a["cache_kidx"][0, 0].rearrange("(t p) n -> p t n", p=P)).then_inc(cache_in, 16)
                act_e.dma_start(ck, a["cache_k"][0, 0].rearrange("(t p) g n -> p t (g n)", p=P)).then_inc(cache_in, 16)
                act_e.dma_start(Vs[:, 0:8, :], a["cache_v"][0, 0].rearrange("(t p) g n -> p t (g n)", p=P)).then_inc(cache_in, 16)

            kt = 0
            for j, s in enumerate(STEPS):
                kind = s[0]
                done = psum_drained[j % 4]
                t = s[1] if len(s) > 1 else 0
                R = ROWS[t] if t < T else 0
                tok = slice(TOK[t], TOK[t] + R) if t < T else None
                if kind == "mod":
                    filled(act_e, j)
                    if t >= 2:
                        act_e.wait_ge(mod_stored[t % 2], 16 * (t // 2))
                        if t - 2 < 4:
                            filled(act_e, JOB[("modT", t - 2)])
                    for q in range(4):
                        ins = sc.activation(modrow[t % 2][0:2, q * P:(q + 1) * P], bank(j)[32 * q:32 * q + 2, 0:P], ACT.Copy)
                    order(ins)
                    note(act_e, done)
                    note(act_e, mod_copied)
                    act_e.dma_start(mod_dram[:, t * CW:(t + 1) * CW], modrow[t % 2][0:2, :]).then_inc(mod_stored[t % 2], 16)
                    if t == 1:
                        x_squares()
                elif kind == "qi":
                    i = ORDER.index(t)
                    filled(act_e, j)
                    if i >= 2:
                        act_e.wait_ge(qi_roped, i - 1)
                    leave(qiraw[i % 2][0:R, :], j, t, 0, 324).then_inc(done, 1)
                elif kind == "qiT":
                    filled(act_e, j)
                    sc.activation(qiT[:, :, tok], bank(j)[:, 0:2 * R].rearrange("p (k n) -> p k n", k=2), ACT.Copy)
                    dst = ki_sample[0, 0] if t == SAMPLE else ki_prompt[0, 0, tok, :]
                    act_e.dma_start(dst, qro[0:R, t, 256:320]).then_inc(out_ki, 16)
                    if t == SAMPLE:
                        sc.activation(kiTs[:, PAST:PAST + DEC], bank(j)[:, 2 * R:3 * R], ACT.Copy)
                    sc.activation(kiT[:, tok], bank(j)[:, 2 * R:3 * R], ACT.Copy).then_inc(done, 1)
                elif kind == "cacheT":
                    filled(act_e, j)
                    sc.activation(kiTs[:, t * P:(t + 1) * P], bank(j)[:, 0:P], ACT.Copy)
                    sc.activation(kTs[:, t * P:(t + 1) * P], bank(j, 1)[:, 0:P], ACT.Copy).then_inc(done, 1)
                elif kind in ("idx", "idxnew"):
                    filled(act_e, j)
                    if kt >= 2:
                        act_e.wait_ge(rel_used, kt - 1)
                    n = min(NKEYS[t], 1024) if kind == "idx" else DEC
                    sc.activation(rel[kt % 2][0:R, 0:n], group(j)[0:R, 0:n], ACT.Relu).then_inc(done, 1)
                    kt += 1
                elif kind == "kv":
                    i = ORDER.index(t)
                    filled(act_e, j)
                    if i >= 2:
                        act_e.wait_ge(raw_used, i - 1)
                    if t == SAMPLE:
                        act_e.wait_ge(cache_in, 48)
                        leave(Vs[0:R, 8, :], j, t, 128, 128)
                    leave(va[0:R, t, :], j, t, 128, 128)
                    leave(raw[i % 2][0:R, 0:128], j, t, 0, 128).then_inc(done, 1)
                elif kind == "lr":
                    filled(act_e, j)
                    sc.activation(halves(lrT)[0:16], turned(j)[0:16], ACT.Copy).then_inc(done, 1)
                elif kind == "qa":
                    i = ORDER.index(t)
                    filled(act_e, j)
                    act_e.wait_ge(raw_used, T + i - 1)
                    leave(raw[(T + i) % 2][0:R, :], j, t, 0, 512).then_inc(done, 1)
                elif kind == "qaT":
                    filled(act_e, j)
                    if t == SAMPLE:
                        sc.activation(qaTs, bank(j)[:, 0:4 * R], ACT.Copy)
                    else:
                        sc.activation(qaT[:, :, tok], bank(j)[:, 0:4 * R].rearrange("p (k n) -> p k n", k=4), ACT.Copy)
                    if t == SAMPLE:
                        sc.activation(kTs[:, PAST:PAST + DEC], bank(j, 1)[:, 0:R], ACT.Copy)
                    sc.activation(kaT[:, tok], bank(j, 1)[:, 0:R], ACT.Copy).then_inc(done, 1)
                elif kind == "qkg":
                    filled(act_e, j)
                    dst, f = (qgT, HD ** -0.5) if t < 2 else (kgT, 1.0)
                    sc.activation(halves(dst[:, t % 2, :]), turned(j), ACT.Copy, scale=f).then_inc(done, 1)
                elif kind == "vg":
                    filled(act_e, j)
                    leave(vg[0:R, t, :], j, t, 0, 512).then_inc(done, 1)
                elif kind == "rg":
                    i = ORDER.index(t)
                    filled(act_e, j)
                    if i >= 2:
                        act_e.wait_ge(raw_used, 2 * T + i - 1)
                    if t == SAMPLE:
                        act_e.wait_ge(masks_made, 1)
                        for q in range(1, 4):
                            ins = sc.activation(score[t][32 * q:32 * q + DEC, :], score[t][0:DEC, :], ACT.Copy)
                        ins.then_inc(mask_spread, 1)
                    leave(graw[i % 2][0:R, :], j, t, 0, 512, ACT.Sigmoid)
                    leave(rg[0:R, t, :], j, t, 0, 512).then_inc(done, 1)
                    if i == 2:
                        for n, x in enumerate((gqA, gk0, gk1, gqe, gkd, eL)):
                            act_e.wait_ge(gla_in, n + 1)
                            sc.activation(x, x, ACT.Exp).then_inc(gla_exp, 1)
                elif kind == "z":
                    act_e.wait_ge(gate_z, t + 1)
                    order(sc.activation(gT1[1], gT1[1], ACT.Exp, scale=-1.0))
                    sc.activation(gT1[1], gT1[1], ACT.Ln, bias=1.0).then_inc(gate_l, 1)
                elif kind == "kd":
                    filled(act_e, j)
                    sc.activation(kdn[0:R, t, :], bank(j)[0:R, 0:256], ACT.Copy).then_inc(done, 1)
                elif kind == "gi":
                    filled(act_e, j)
                    act_e.wait_ge(o_done, t)
                    sc.activation(ot[0:R, :].rearrange("p (j b n) -> p b j n", b=2, j=2),
                                  group(j)[0:R, :].rearrange("p (b j n) -> p b j n", b=2, j=4)[:, :, 0:2, :],
                                  ACT.Copy).then_inc(done, 1)
                elif kind == "go":
                    act_e.wait_ge(o_sum, t + 1)
                    for h in range(NBH):
                        order(sc.activation(gT2[0:R, 0:DV], ot[0:R, h * DV:(h + 1) * DV], ACT.Square,
                                            accum_out=ss4[0:R, h:h + 1]))
                    note(act_e, o_sq)
                    act_e.wait_ge(o_var, t + 1)
                    sc.activation(rr4[0:R, :], vv4[0:R, :], ACT.Sqrt).then_inc(o_sqrt, 1)
                elif kind in ("pT", "pTnew") and t == SAMPLE:
                    filled(act_e, j)
                    if kind == "pT":
                        act_e.wait_ge(raw_used, 3 * T)
                        sc.activation(pTs[s[2]][0], group(j), ACT.Copy).then_inc(done, 1)
                    else:
                        sc.activation(pTs[s[2]][1][0:DEC, :], bank(j)[0:DEC, 0:P], ACT.Copy).then_inc(done, 1)
                elif kind == "pT":
                    u = UNIT[s[1:]]
                    n = -(-NKEYS[t] // P)
                    filled(act_e, j)
                    if u >= 4:
                        filled(act_e, JOB[("pv", *UNITS[u - 2])])
                    sc.activation(pT[u % 2][:, 0:n * R], bank(j)[:, 0:n * R], ACT.Copy).then_inc(done, 1)
                elif kind == "catT":
                    filled(act_e, j)
                    sc.activation(catT[:, :, tok], group(j)[:, 0:8 * R].rearrange("p (k n) -> p k n", k=KD),
                                  ACT.Copy).then_inc(done, 1)
                elif kind == "y":
                    act_e.wait_ge(x2_made, t + 1)
                    sc.activation(junk[0:R, :], x2b[t % 2][0:R, :], ACT.Square, accum_out=ss[0:R, t:t + 1]).then_inc(x2_sq, 1)
                    act_e.wait_ge(x2_var, t + 1)
                    sc.activation(rr[0:R, t:t + 1], vv[0:R, t:t + 1], ACT.Sqrt).then_inc(x2_sqrt, 1)
                elif kind == "hT":
                    filled(act_e, j)
                    if t >= 1:
                        filled(act_e, JOB[("rt", t - 1)])
                    sc.activation(h2T[:, 0:8 * R], group(j)[:, 0:8 * R], ACT.Copy).then_inc(done, 1)
                elif kind == "rt":
                    act_e.wait_ge(top_ready, t + 1)
                    sc.activation(e4[0:R, :], v8[0:R, 0:4], ACT.Exp, bias=ngate[0:R, :],
                                  accum_out=gs1[0:R, :]).then_inc(gate_exp, 1)
                if kind in ("sc", "scnew") and (kind == "scnew" or t != SAMPLE):
                    u = UNIT[s[1:]]
                    act_e.wait_ge(logits_max, u + 1)
                    n = NKEYS[t]
                    if u >= 4:
                        in_sbuf(act_e, ("pv", *UNITS[u - 4]))
                    sc.activation(prob[u % 3][:, 0:n], prob[u % 3][:, 0:n], ACT.Exp, bias=negm[:, u % 3:u % 3 + 1],
                                  accum_out=ars[:, u % 4:u % 4 + 1]).then_inc(probs_made, 1)

            def high_part(i, c):
                act_e.wait_ge(raw_in[c % RAW], i * 32 + c // RAW * 16 + 16)
                act_e.wait_ge(chunk_done, i * BCH + c + 1)
                for x in range(2):
                    h = slice(x * SLOT // 2, (x + 1) * SLOT // 2)
                    sc.activation(high(c)[:, h], raw_slot(c)[:, h], ACT.Copy).then_inc(high_made, 1)

            def take_tokens(i):
                act_e.wait_ge(xg_turned, i + 1)
                sc.activation(xgT_hi.rearrange("p k n -> p (k n)"), psum[:, 0:2, :].rearrange("p b n -> p (b n)"),
                              ACT.Copy).then_inc(xgT_high, 1)

            def take_act(i, half):
                act_e.wait_ge(act_turned, 2 * i + half + 1)
                sc.activation(actT_hi[:, 4 * half:4 * half + 4, :].rearrange("p k n -> p (k n)"), psum[:, 6 + half, :],
                              ACT.Copy).then_inc(actT_high, 1)

            def gate_sigmoid(i, half):
                act_e.wait_ge(gate_added, 2 * i + half + 1)
                sc.activation(es, eg, ACT.Sigmoid, scale=ALPHA).then_inc(gate_sig, 1)

            def expert_act(i):
                sc.activation(table_pull, table_pull, ACT.Sigmoid)
                high_part(i, 2)
                high_part(i, 3)
                act_e.wait_ge(ys_ready, i + 1)
                act_e.dma_start(ys_dram[bass.ds(i * P, P), :], ysb).then_inc(ys_stored, 16)
                gate_sigmoid(i, 0)
                high_part(i, 4)
                high_part(i, 5)
                take_act(i, 0)
                gate_sigmoid(i, 1)
                high_part(i + 1, 0)
                take_tokens(i + 1)
                take_act(i, 1)
                high_part(i + 1, 1)
            act_e.wait_ge(routed, 1)
            order(sc.activation(table_pull, ones[:, 0:1], ACT.Copy))
            high_part(0, 0)
            high_part(0, 1)
            take_tokens(0)
            with act_e.Fori(0, NE) as i:
                expert_act(i)
            act_e.wait_ge(routed, 1)
            n_over = act_e.value_load(over[0:1, NOV:NOV + 1], min_val=0, max_val=NOV)
            with act_e.If(n_over > 0):
                with act_e.Fori(0, n_over) as j:
                    expert_act(j + NE)
            act_e.wait_ge(ys_ready, n_over + NE + 1)
            act_e.dma_start(ys_dram[bass.ds((n_over + NE) * P, P), :], ysb).then_inc(ys_stored, 16)
            act_e.wait_ge(ys_stored, (n_over + NE + 1) * 16)
            act_e.wait_ge(gathered, (n_over + NE + 1) * 16)
            act_e.wait_ge(bias_in, (n_over + NE + 1) * 32)
            for x in raw_in:
                act_e.wait_ge(x, (n_over + NE) * 32 + 16)
            act_e.wait_ge(split_dve, (n_over + NE) * BCH + 2 + CHUNK0)
            act_e.wait_ge(split_pool, (n_over + NE) * BCH + 2 + CHUNK0)
            act_e.wait_ge(xgT_ready, n_over + NE + 1)
            note(act_e, experts_done)
            for t in range(T):
                R = ROWS[t]
                act_e.wait_ge(f_made, t + 1)
                sc.activation(facc[0:R, :], xf[t % NF][0:R, :], ACT.Square, accum_out=ss[0:R, t:t + 1]).then_inc(f_sq, 1)
                act_e.wait_ge(f_var, t + 1)
                sc.activation(rr[0:R, t:t + 1], vv[0:R, t:t + 1], ACT.Sqrt).then_inc(f_sqrt, 1)

        @block.vector
        def _(dve):
            order = Order(dve, dve_s)
            v = nc.vector

            def inv_sqrt(out, root, var, n, rows):
                o, r, x = out[0:rows, n], root[0:rows, n], var[0:rows, n]
                order(v.reciprocal(o, r))
                tmp = r2[0:rows, 0:o.shape[1]]
                order(v.tensor_tensor(tmp, o, o, ALU.mult))
                order(v.tensor_tensor(tmp, tmp, x, ALU.mult))
                order(v.tensor_scalar(tmp, tmp, -0.5, 1.5, ALU.mult, ALU.add))
                order(v.tensor_tensor(o, o, tmp, ALU.mult))

            v.memset(ss, 1.0).then_inc(ss_clear, 1)
            dve.wait_ge(c_sig, 1)
            v.tensor_tensor(cc[0:16, :], cc[0:16, :], csg[0:16, :], ALU.mult).then_inc(c_silu, 1)
            def x_scaled():
                dve.wait_ge(x_sq, 1)
                v.tensor_scalar(vv[:, 0:T], ss[:, 0:T], 1.0 / D, EPS, ALU.mult, ALU.add).then_inc(x_var, 1)
                dve.wait_ge(x_sqrt, 1)
                inv_sqrt(r3, rr, vv, slice(0, T), P)
                for t in range(T):
                    v.tensor_scalar(xs5[0:ROWS[t], t, :], xs5[0:ROWS[t], t, :], r3[0:ROWS[t], t:t + 1], None,
                                    ALU.mult).then_inc(x_norm, 1)

            def top_k(t):
                R, n = ROWS[t], NKEYS[t]
                k = TOPK_SAMPLE if t == SAMPLE else TOPK_PROMPT
                s_, w = score[t][0:R, :], twork[0:R, 0:n]
                if n <= k:
                    order(v.memset(score[t][:, :], 0.0))
                    v.memset(score[t][0:CHUNK, n - CHUNK:n], MASKED).then_inc(masks_made, 1)
                    return
                for i in range(k // 8):
                    src = s_ if i == 0 else w
                    order(v.max(m8[0:R, :], src))
                    if i < k // 8 - 1:
                        order(v.match_replace(w, m8[0:R, :], src, NEG))
                above, at_, cnt = w, prefix[0:R, 0:n], cgt[0:R, :]
                order(v.tensor_scalar(above, s_, m8[0:R, 7:8], 0.0, ALU.is_gt, ALU.add, accum_out=cnt))
                order(v.tensor_scalar(s_, s_, m8[0:R, 7:8], None, ALU.is_equal))
                order(v.tensor_scalar(cnt, cnt, -1.0, float(k), ALU.mult, ALU.add))
                order(v.tensor_tensor_scan(at_, s_, s_, 0.0, ALU.add, ALU.max))
                order(v.scalar_tensor_tensor(out=s_, in0=at_, scalar=cnt, in1=s_, op0=ALU.is_le, op1=ALU.mult))
                order(v.tensor_tensor(s_, s_, above, ALU.add))
                v.tensor_scalar(s_, s_, -MASKED, MASKED, ALU.mult, ALU.add).then_inc(masks_made, 1)

            def rope(R, t, H, src, dst, tmp):
                x = src.rearrange("p (h d) -> p h d", h=H)
                o = dst.rearrange("p (h d) -> p h d", h=H)
                m = tmp.rearrange("p (h d) -> p h d", h=H)
                order(v.tensor_tensor(o, x, cs[0:R, t, 0:64].unsqueeze(1).to_broadcast([R, H, 64]), ALU.mult))
                for a_, b_ in ((0, 32), (32, 0)):
                    order(v.tensor_tensor(m[:, :, a_:a_ + 32], x[:, :, b_:b_ + 32],
                                          cs[0:R, t, 64 + a_:96 + a_].unsqueeze(1).to_broadcast([R, H, 32]), ALU.mult))
                return v.tensor_tensor(o, o, m, ALU.add)

            kt = 0
            for j, s in enumerate(STEPS):
                kind = s[0]
                done = psum_drained[j % 4]
                t = s[1] if len(s) > 1 else 0
                R = ROWS[t] if t < T else 0
                tok = slice(TOK[t], TOK[t] + R) if t < T else None
                if kind == "c":
                    filled(dve, j)
                    v.tensor_copy(cT, bank(j)[:, 0:16])
                    v.tensor_copy(vT[:, 0:10], bank(j, 1)[:, 0:10]).then_inc(done, 1)
                elif kind == "modT":
                    filled(dve, j)
                    v.tensor_copy(colT[:, 8 * t:8 * t + 8], bank(j)[:, 0:8]).then_inc(done, 1)
                    if t == 1:
                        x_scaled()
                    if t == 3:
                        in_sbuf(dve, ("modT", 3))
                        in_sbuf(dve, ("c",))
                        order(v.tensor_scalar(a1, colT[:, 16:32], 1.0, None, ALU.add))
                        order(v.tensor_tensor(a1.rearrange("p (k c) -> p k c", c=2), a1.rearrange("p (k c) -> p k c", c=2),
                                              vT[:, 0:8].unsqueeze(2).to_broadcast([P, 8, 2]), ALU.mult))
                elif kind == "xT":
                    filled(dve, j)
                    v.tensor_scalar(hT[:, t, 0:SEQ], bank(j), a1[:, 2 * t:2 * t + 1], colT[:, 2 * t:2 * t + 1],
                                    ALU.mult, ALU.add)
                    v.tensor_scalar(hT[:, t, SEQ:NTOK], bank(j, 1)[:, 0:DEC], a1[:, 2 * t + 1:2 * t + 2],
                                    colT[:, 2 * t + 1:2 * t + 2], ALU.mult, ALU.add).then_inc(done, 1)
                elif kind == "qi":
                    i = ORDER.index(t)
                    in_sbuf(dve, s)
                    dve.wait_ge(tabs_in, 64)
                    order(v.tensor_scalar(wis[0:R, t, :], qiraw[i % 2][0:R, 320:324], NIH ** -0.5, None, ALU.mult))
                    rope(R, t, 5, qiraw[i % 2][0:R, 0:320], qro[0:R, t, :], twork[0:R, 0:320]).then_inc(qi_roped, 1)
                elif kind in ("idx", "idxnew"):
                    h = s[2]
                    in_sbuf(dve, s)
                    n0 = 0 if kind == "idx" else 1024
                    n = min(NKEYS[t], 1024) if kind == "idx" else DEC
                    dst, src = score[t][0:R, n0:n0 + n], rel[kt % 2][0:R, 0:n]
                    if h == 0:
                        order(v.tensor_scalar(dst, src, wis[0:R, t, 0:1], None, ALU.mult))
                    else:
                        order(v.scalar_tensor_tensor(out=dst, in0=src, scalar=wis[0:R, t, h:h + 1], in1=dst,
                                                     op0=ALU.mult, op1=ALU.add))
                    kt += 1
                    note(dve, rel_used)
                    if h == NIH - 1 and t not in (0, SAMPLE):
                        order(v.memset(score[t][0:CHUNK, NKEYS[t] - CHUNK:NKEYS[t]], NEG))
                    if s == ("idx", ORDER[-1], NIH - 1):
                        for tt in ORDER:
                            top_k(tt)
                elif kind == "z":
                    filled(dve, j)
                    Z, B = gT2[:, 0:NTOK], bT[:, t, :]
                    dve.wait_ge(out_ki, T * 16)
                    dve.wait_ge(out_kv, 2 * T * 16)
                    for x in mod_stored:
                        dve.wait_ge(x, 16 * 8)
                    order(v.tensor_scalar(Z, group(j)[:, 0:NTOK], vT[:, 8 + t:9 + t], None, ALU.add))
                    note(dve, done)
                    v.scalar_tensor_tensor(out=gT1[1], in0=Z, scalar=-1.0, in1=Z, op0=ALU.mult,
                                           op1=ALU.max).then_inc(gate_z, 1)
                    dve.wait_ge(gate_l, t + 1)
                    order(v.scalar_tensor_tensor(out=Z, in0=Z, scalar=0.0, in1=gT1[1], op0=ALU.min,
                                                 op1=ALU.subtract))
                    order(v.tensor_scalar(Z, Z, 1.0 / 16.0, None, ALU.mult))
                    dve.wait_ge(gate_mask, 1)
                    order(v.tensor_tensor_scan(B, gT1[0], Z, 0.0, ALU.mult, ALU.add))
                    if t == 1:
                        v4 = bT.rearrange("p j (b s) -> p j b s", s=32)
                        c4 = bT[:, :, 0:SEQ].rearrange("p j (c s) -> p j c s", s=CHUNK)
                        for x in range(2):
                            ins = v.tensor_tensor(gqA[:, x].rearrange("p (b s) -> p b s", s=32), v4[:, x],
                                                  v4[:, x, :, 16:17].to_broadcast([P, 17, 32]), ALU.subtract)
                        ins.then_inc(gla_in, 1)
                        for dst, at_ in ((gk0, 16), (gk1, 48), (None, 0), (gkd, 63)):
                            if dst is None:
                                v.tensor_copy(gqe, bT).then_inc(gla_in, 1)
                                continue
                            for x in range(2):
                                ins = v.tensor_tensor(dst[:, x, 0:SEQ].rearrange("p (c s) -> p c s", s=CHUNK),
                                                      c4[:, x, :, at_:at_ + 1].to_broadcast([P, 8, CHUNK]), c4[:, x], ALU.subtract)
                                if dst is not gk1:
                                    a_ = SEQ + min(at_, DEC - 1)
                                    ins = v.tensor_tensor(dst[:, x, SEQ:NTOK], bT[:, x, a_:a_ + 1].to_broadcast([P, DEC]),
                                                          bT[:, x, SEQ:NTOK], ALU.subtract)
                            ins.then_inc(gla_in, 1)
                        v.tensor_copy(eL[:, :, 0:8], c4[:, :, :, 63:64].rearrange("p j c o -> p j (c o)"))
                        v.tensor_copy(eL[:, :, 8:9], bT[:, :, NTOK - 1:NTOK]).then_inc(gla_in, 1)
                        for n, (x, y) in enumerate(((gqA, qgT), (gk0, kgT), (gk1, kgT[:, :, 0:SEQ]), (gqe, qgT), (gkd, kgT))):
                            dve.wait_ge(gla_exp, n + 1)
                            v.tensor_tensor(x, x, y, ALU.mult).then_inc(gla_made, 1)
                        for x in (scT[0], scT[1], states[0].rearrange("p j n -> p (j n)")):
                            v.memset(x, 0.0).then_inc(gla_made, 1)
                elif kind == "gs":
                    filled(dve, j)
                    if t >= 2:
                        filled(dve, JOB[("go", t - 2)])
                    elif t == 0:
                        dve.wait_ge(gla_made, 8)
                    v.copy_predicated(scT[t % 2][0:R, :].rearrange("p (b n) -> p b n", b=2),
                                      gmask[0:R, :].rearrange("p (b n) -> p b n", b=2),
                                      group(j)[0:R, :].rearrange("p (b n) -> p b n", b=2)[:, :, 0:128]).then_inc(done, 1)
                elif kind == "gst":
                    filled(dve, j)
                    c = 2 * t + s[2]
                    if t == SAMPLE:
                        dve.wait_ge(state_in, 16)
                        for x in range(2):
                            ins = v.scalar_tensor_tensor(out=states[5][:, x, :], in0=states[4][:, x, :],
                                                         scalar=eL[:, x, 8:9], in1=bank(j)[:, x * DV:(x + 1) * DV],
                                                         op0=ALU.mult, op1=ALU.add)
                        ins.then_inc(done, 1)
                    elif c == 0:
                        v.tensor_copy(states[1].rearrange("p j n -> p (j n)"), bank(j)[:, 0:256]).then_inc(done, 1)
                    else:
                        prev = JOB[("gst", (c - 1) // 2, (c - 1) % 2)]
                        dve.wait_ge(psum_drained[prev % 4], prev // 4 + 1)
                        for x in range(2):
                            ins = v.scalar_tensor_tensor(out=states[(c + 1) % 4][:, x, :], in0=states[c % 4][:, x, :],
                                                         scalar=eL[:, x, c:c + 1], in1=bank(j)[:, x * DV:(x + 1) * DV],
                                                         op0=ALU.mult, op1=ALU.add)
                        ins.then_inc(done, 1)
                elif kind == "go":
                    filled(dve, j)
                    in_sbuf(dve, ("gi", t))
                    order(v.tensor_tensor(ot[0:R, :], ot[0:R, :], bank(j)[0:R, :], ALU.add))
                    note(dve, done)
                    note(dve, o_sum)
                    dve.wait_ge(o_sq, t + 1)
                    v.tensor_scalar(vv4[0:R, :], ss4[0:R, :], 1.0 / DV, EPS, ALU.mult, ALU.add).then_inc(o_var, 1)
                    dve.wait_ge(o_sqrt, t + 1)
                    inv_sqrt(r3, rr4, vv4, slice(0, 4), R)
                    dve.wait_ge(raw_used, 3 * T)
                    for h in range(NBH):
                        g = rg[0:R, t, h * DV:(h + 1) * DV]
                        ins = v.scalar_tensor_tensor(out=g, in0=ot[0:R, h * DV:(h + 1) * DV],
                                                     scalar=r3[0:R, h:h + 1], in1=g, op0=ALU.mult, op1=ALU.mult)
                    ins.then_inc(o_done, 1)
                elif kind in ("sc", "scnew"):
                    u = UNIT[s[1:]]
                    n0 = 0 if kind == "sc" else 1024
                    n = min(NKEYS[t], 1024) if kind == "sc" else DEC
                    filled(dve, j)
                    if u >= 3:
                        filled(dve, JOB[("pT", *UNITS[u - 3])])
                        if UNITS[u - 3][0] == SAMPLE:
                            filled(dve, JOB[("pTnew", *UNITS[u - 3])])
                    dve.wait_ge(masks_made, T)
                    if t == SAMPLE:
                        dve.wait_ge(mask_spread, 1)
                    mx = amx[:, 2 * (u % 3) + (kind == "scnew"):2 * (u % 3) + (kind == "scnew") + 1]
                    order(v.tensor_tensor_reduce(out=prob[u % 3][:, n0:n0 + n], in0=group(j)[:, 0:n],
                                                 in1=score[t][:, n0:n0 + n], scale=HD ** -0.5, scalar=NEG,
                                                 op0=ALU.add, op1=ALU.max, accum_out=mx))
                    m0 = amx[:, 2 * (u % 3):2 * (u % 3) + 1]
                    note(dve, done)
                    if kind == "scnew":
                        order(v.tensor_tensor(m0, m0, mx, ALU.max))
                    if kind == "scnew" or t != SAMPLE:
                        v.tensor_scalar(negm[:, u % 3:u % 3 + 1], m0, -1.0, None, ALU.mult).then_inc(logits_max, 1)
                elif kind == "pv":
                    h = s[2]
                    u = UNIT[s[1:]]
                    filled(dve, j)
                    dve.wait_ge(probs_made, u + 1)
                    r1 = rinv[:, u % 4:u % 4 + 1]
                    order(v.reciprocal(r1, ars[:, u % 4:u % 4 + 1]))
                    if t == SAMPLE:
                        order(v.tensor_scalar(osum[h], bank(j)[:, h * HD:(h + 1) * HD], r1, None, ALU.mult))
                        for q in range(4):
                            ins = v.tensor_copy(catA[0:R, t, (4 * h + q) * HD:(4 * h + q + 1) * HD],
                                                osum[h][32 * q:32 * q + R, :])
                        ins.then_inc(done, 1)
                        continue
                    g0 = h // 4 * HD
                    v.tensor_scalar(catA[0:R, t, h * HD:(h + 1) * HD], bank(j)[0:R, g0:g0 + HD], r1,
                                    None, ALU.mult).then_inc(done, 1)
                elif kind == "y":
                    row = rowS if t == SAMPLE else rowP
                    if t == 0:
                        dve.wait_ge(rows_in, ROW_DMAS * 16)
                        for x, rws in ((rowP, P), (rowS, DEC)):
                            order(v.scalar_tensor_tensor(out=x[1][0:rws, :], in0=x[1][0:rws, :], scalar=1.0,
                                                         in1=gffn_b[0:rws, :], op0=ALU.add, op1=ALU.mult))
                        for x in (sel, oneh, gates, chosen, sel_before[:, 0:NE]):
                            order(v.memset(x, 0.0))
                    filled(dve, j)
                    dve.wait_ge(x_again[t % 2], 16 * (t // 2 + 1))
                    if t >= 2:
                        dve.wait_ge(x2_stored[t % 2], 16 * (t // 2))
                        dve.wait_ge(h2_stored[t % 2], 16 * (t // 2))
                        filled(dve, JOB[("hT", t - 2)])
                    x2, h2 = x2b[t % 2][0:R, :], h2b[t % 2][0:R, :]
                    if t == SAMPLE:
                        for q in range(4):
                            x3, r3_ = (z_.rearrange("p (b q n) -> p b q n", b=2, q=4)[:, :, q] for z_ in (x2, row[0][0:R, :]))
                            ins = v.tensor_tensor(x3, psum[32 * q:32 * q + R, 2 * (j % 4):2 * (j % 4) + 2, 0:P], r3_, ALU.mult)
                        order(ins)
                    else:
                        order(v.tensor_tensor(x2, group(j)[0:R, :], row[0][0:R, :], ALU.mult))
                    note(dve, done)
                    order(v.tensor_tensor(x2, x2, xin[t % 2][0:R, :], ALU.add))
                    note(dve, x2_made)
                    dve.wait_ge(x2_sq, t + 1)
                    v.tensor_scalar(vv[0:R, t:t + 1], ss[0:R, t:t + 1], 1.0 / D, EPS, ALU.mult, ALU.add).then_inc(x2_var, 1)
                    dve.wait_ge(x2_sqrt, t + 1)
                    inv_sqrt(r3, rr, vv, slice(t, t + 1), R)
                    order(v.scalar_tensor_tensor(out=h2, in0=x2, scalar=r3[0:R, t:t + 1], in1=row[1][0:R, :],
                                                 op0=ALU.mult, op1=ALU.mult))
                    v.tensor_tensor(h2, h2, row[2][0:R, :], ALU.add).then_inc(h2_made, 1)
                elif kind == "rt":
                    filled(dve, j)
                    lg = rj[0:R, :]
                    order(v.tensor_tensor(lg, bank(j)[0:R, 0:NE], br_b[0:R, :], ALU.add))
                    note(dve, done)
                    order(v.max(v8[0:R, :], lg))
                    order(v.max_index(i8[0:R, :], v8[0:R, :], lg))
                    v.tensor_scalar(ngate[0:R, :], v8[0:R, 0:1], -1.0, None, ALU.mult).then_inc(top_ready, 1)
                    ch = chosen[0:R, 4 * t:4 * t + 4]
                    order(v.tensor_copy(ch, i8[0:R, 0:4]))
                    oh = oneh[0:R, t * 128:(t + 1) * 128].rearrange("p (k e) -> p k e", e=NE)
                    for k in range(TOPE):
                        order(v.tensor_scalar(oh[:, k, :], iota_e[0:R, :], chosen[0:R, 4 * t + k:4 * t + k + 1], None, ALU.is_equal))
                    order(v.tensor_reduce(sel[0:R, t * NE:(t + 1) * NE], oh.rearrange("p k e -> p e k"), AX.X, ALU.add))
                    order(v.tensor_tensor(sel_before[:, (t + 1) * NE:(t + 2) * NE], sel_before[:, t * NE:(t + 1) * NE],
                                          sel[:, t * NE:(t + 1) * NE], ALU.add))
                    note(dve, sel_made)
                    dve.wait_ge(gate_exp, t + 1)
                    order(v.reciprocal(gr1[0:R, :], gs1[0:R, :]))
                    order(v.tensor_scalar(gates[0:R, 4 * t:4 * t + 4], e4[0:R, :], gr1[0:R, :], None, ALU.mult))
                elif kind == "rank":
                    filled(dve, j)
                    v.tensor_copy(rank, bank(j)[:, 0:(T + 1) * NE]).then_inc(done, 1)
                    in_sbuf(dve, s)
                    dve.wait_ge(iota_made, 1)
                    cnt = rank[:, T * NE:(T + 1) * NE]
                    order(v.tensor_scalar(xb_, cnt, float(P), None, ALU.is_gt))
                    for m in range(2, 5):
                        order(v.scalar_tensor_tensor(out=xb_, in0=cnt, scalar=float(P * m), in1=xb_, op0=ALU.is_gt, op1=ALU.add))
                    order(v.tensor_tensor_scan(xe_, ones[:, 0:NE], xb_, 0.0, ALU.mult, ALU.add))
                    order(v.tensor_tensor(xst, xe_, xb_, ALU.subtract))
                    oh4 = oneh.rearrange("p (t k e) -> p t k e", k=TOPE, e=NE)
                    picked = pick_t.rearrange("p (t k e) -> p t k e", k=TOPE, e=NE)
                    pick3 = pick_t.rearrange("p (c e) -> p c e", e=NE)
                    rank4 = rank[:, 0:T * NE].rearrange("p (t e) -> p t e", e=NE).unsqueeze(2).to_broadcast([P, T, TOPE, NE])
                    order(v.tensor_tensor(picked, oh4, rank4, ALU.mult))
                    order(v.tensor_reduce(f1, pick3, AX.X, ALU.add))
                    order(v.tensor_tensor(pick3, oneh.rearrange("p (c e) -> p c e", e=NE),
                                          xst.unsqueeze(1).to_broadcast([P, T * TOPE, NE]), ALU.mult))
                    order(v.tensor_reduce(f2, pick3, AX.X, ALU.add))
                    order(v.tensor_scalar(f3, f1, float(P), None, ALU.is_ge))
                    order(v.tensor_copy(f4, f3))
                    for m in range(2, 5):
                        order(v.scalar_tensor_tensor(out=f3, in0=f1, scalar=float(P * m), in1=f3, op0=ALU.is_ge, op1=ALU.add))
                    order(v.scalar_tensor_tensor(out=f5, in0=f3, scalar=-float(P), in1=f1, op0=ALU.mult, op1=ALU.add))
                    order(v.scalar_tensor_tensor(out=f6, in0=f3, scalar=float(NE - 1), in1=f2, op0=ALU.add, op1=ALU.add))
                    order(v.tensor_tensor(f6, f6, chosen, ALU.subtract))
                    order(v.tensor_tensor(f6, f6, f4, ALU.mult))
                    order(v.tensor_tensor(f6, f6, chosen, ALU.add))
                    order(v.scalar_tensor_tensor(out=f7, in0=f5, scalar=float(NBLK), in1=f6, op0=ALU.mult, op1=ALU.add))
                    order(v.tensor_copy(tab_pos, f7))
                    order(v.scalar_tensor_tensor(out=f7, in0=f6, scalar=float(P), in1=f5, op0=ALU.mult, op1=ALU.add))
                    order(v.tensor_scalar(f7, f7, float(P), None, ALU.add))
                    order(v.tensor_copy(ys_row, f7))
                    tn = tmpn[0:1, :].rearrange("p (j e) -> p j e", e=NE)
                    order(v.tensor_tensor(tn, iota_j[0:1, :].rearrange("p (j e) -> p j e", e=NE),
                                          xe_[0:1, :].unsqueeze(1).to_broadcast([1, NOV, NE]), ALU.is_ge))
                    order(v.tensor_reduce(ovf[0:1, 0:NOV], tn, AX.X, ALU.add))
                    order(v.tensor_scalar(ovf[0:1, 0:NOV], ovf[0:1, 0:NOV], float(NE - 1), None, ALU.min))
                    order(v.tensor_copy(ovf[0:1, NOV:NOV + 1], xe_[0:1, NE - 1:NE]))
                    order(v.tensor_copy(over[0:1, :], ovf[0:1, :]))
                    note(dve, routed)

            def low_part(i, c):
                for x, (lo_, hi_) in enumerate(((0, SLOT // 2), (SLOT // 2, SLOT - POOL_PART))):
                    dve.wait_ge(high_made, 2 * (i * BCH + c) + x + 1)
                    ins = v.tensor_tensor(low(c)[:, lo_:hi_], raw_slot(c)[:, lo_:hi_], high(c)[:, lo_:hi_].bitcast(F32), ALU.subtract)
                ins.then_inc(split_dve, 1)

            def take_tokens(i):
                dve.wait_ge(xgT_high, i + 1)
                v.tensor_tensor(xgT_lo.rearrange("p k n -> p (k n)"), psum[:, 0:2, :].rearrange("p b n -> p (b n)"),
                                xgT_hi.rearrange("p k n -> p (k n)").bitcast(F32), ALU.subtract).then_inc(xgT_ready, 1)

            def take_act(i, half):
                dve.wait_ge(actT_high, 2 * i + half + 1)
                k = slice(4 * half, 4 * half + 4)
                v.tensor_tensor(actT_lo[:, k, :].rearrange("p k n -> p (k n)"), psum[:, 6 + half, :],
                                actT_hi[:, k, :].rearrange("p k n -> p (k n)").bitcast(F32), ALU.subtract).then_inc(actT_ready, 1)

            def gate_half(i, half):
                dve.wait_ge(act_ready, i * 2 + half + 1)
                dve.wait_ge(chunk_done, i * BCH + 2 * half + 1 + CHUNK0)
                if half == 0:
                    dve.wait_ge(bias_ready, i + 1)
                local(v.tensor_tensor(eg, psum[:, 2 * half, :], bias_b[:, half * 512:(half + 1) * 512], ALU.add), 0, half, i)
                v.tensor_scalar(eg, eg, LIMIT, None, ALU.min).then_inc(gate_added, 1)

            def up_half(i, half):
                dve.wait_ge(chunk_done, i * BCH + 2 * half + 2 + CHUNK0)
                local(v.tensor_tensor(eu, psum[:, 2 * half + 1, :], bias_b[:, D + half * 512:D + (half + 1) * 512], ALU.add), 1, half, i)
                local(v.tensor_scalar(eu, eu, LIMIT, -LIMIT, ALU.min, ALU.max), 2, half, i)
                dve.wait_ge(gate_sig, i * 2 + half + 1)
                local(v.tensor_tensor(eg, eg, es, ALU.mult), 3, half, i)
                v.scalar_tensor_tensor(out=act[:, half * 512:(half + 1) * 512], in0=eu, scalar=1.0, in1=eg,
                                       op0=ALU.add, op1=ALU.mult).then_inc(act_ready, 1)

            def expert_dve(i):
                low_part(i, 2)
                gate_half(i, 0)
                low_part(i, 3)
                up_half(i, 0)
                low_part(i, 4)
                gate_half(i, 1)
                low_part(i, 5)
                take_act(i, 0)
                up_half(i, 1)
                low_part(i + 1, 0)
                take_tokens(i + 1)
                take_act(i, 1)
                low_part(i + 1, 1)
                dve.wait_ge(chunk_done, i * BCH + BCH + CHUNK0)
                dve.wait_ge(ys_stored, i * 16 + 16)
                v.tensor_tensor(ysb, psum[:, 4:6, :].rearrange("p b n -> p (b n)"), bias_b[:, 2 * D:3 * D],
                                ALU.add).then_inc(ys_ready, 1)

            def local(ins, n, half, i):
                ins.then_inc(gu_added, 1)
                dve.wait_ge(gu_added, i * 8 + 4 * half + n + 1)

            order(v.memset(ysb, 0.0))
            note(dve, act_ready)
            note(dve, ys_ready)
            dve.sem_inc(split_dve, CHUNK0)
            low_part(0, 0)
            low_part(0, 1)
            take_tokens(0)
            with dve.Fori(0, NE) as i:
                expert_dve(i)
            n_over = dve.value_load(over[0:1, NOV:NOV + 1], min_val=0, max_val=NOV)
            with dve.If(n_over > 0):
                with dve.Fori(0, n_over) as jj:
                    expert_dve(jj + NE)

            dve.wait_ge(fin_rows, 16 * 7)
            for x, rws in ((fP, P), (fS, DEC)):
                order(v.scalar_tensor_tensor(out=x[2][0:rws, :], in0=x[2][0:rws, :], scalar=1.0, in1=gfin_b[0:rws, :],
                                             op0=ALU.add, op1=ALU.mult))

            def combine(t):
                R = ROWS[t]
                row = fS if t == SAMPLE else fP
                x2, o, y = xf[t % NF][0:R, :], fo[t % NF][0:R, :], yg[t % NF]
                dve.wait_ge(fin_y[t % NF], 64 * (t // NF + 1))
                if t >= NF:
                    dve.wait_ge(f_stored[t % NF], 16 * (t // NF))
                order(v.tensor_scalar(o, y[0:R, 0:D], gates[0:R, 4 * t:4 * t + 1], None, ALU.mult))
                for k in range(1, TOPE):
                    order(v.scalar_tensor_tensor(out=o, in0=y[0:R, k * D:(k + 1) * D], scalar=gates[0:R, 4 * t + k:4 * t + k + 1],
                                                 in1=o, op0=ALU.mult, op1=ALU.add))
                order(v.tensor_tensor(o, o, row[0][0:R, :], ALU.mult))
                dve.wait_ge(fin_x[t % NF], 16 * (t // NF + 1))
                v.tensor_tensor(x2, x2, o, ALU.add).then_inc(f_made, 1)

            def last_norm(t):
                R = ROWS[t]
                row = fS if t == SAMPLE else fP
                x2, o = xf[t % NF][0:R, :], fo[t % NF][0:R, :]
                dve.wait_ge(f_sq, t + 1)
                v.tensor_scalar(vv[0:R, t:t + 1], ss[0:R, t:t + 1], 1.0 / D, EPS, ALU.mult, ALU.add).then_inc(f_var, 1)
                dve.wait_ge(f_sqrt, t + 1)
                inv_sqrt(r3, rr, vv, slice(t, t + 1), R)
                order(v.scalar_tensor_tensor(out=o, in0=x2, scalar=r3[0:R, t:t + 1], in1=row[2][0:R, :],
                                             op0=ALU.mult, op1=ALU.mult))
                v.tensor_tensor(o, o, row[1][0:R, :], ALU.add).then_inc(f_out, 1)

            combine(0)
            for t in range(T):
                if t + 1 < T:
                    combine(t + 1)
                last_norm(t)

        @block.gpsimd
        def _(pool):
            order = Order(pool, pool_s)
            g = nc.gpsimd
            order(g.memset(ident, 0.0))
            order(g.affine_select(out=ident, in_=ident, compare_op=ALU.not_equal, fill=1.0, base=0,
                                  pattern=[[-1, P]], channel_multiplier=1))
            order(g.memset(pick2, 0.0))
            order(g.memset(pick2[0:1, :], 1.0))
            for x in bmod:
                order(g.memset(x, 0.0))
            note(pool, bias_clear)
            note(pool, consts)
            order(g.memset(ones, 1.0))
            order(g.affine_select(out=before, in_=ones, compare_op=ALU.is_gt, fill=0.0, base=0,
                                  pattern=[[1, P]], channel_multiplier=-1))
            order(g.iota(gmask, pattern=[[0, NBH], [1, CHUNK]], base=0, channel_multiplier=-1))
            order(g.iota(gmask[CHUNK:P, :], pattern=[[0, NBH], [1, CHUNK]], base=0, channel_multiplier=-1))
            order(g.tensor_scalar(gmask, gmask, 0.0, None, ALU.is_ge))
            order(g.iota(iota_e, pattern=[[1, NE]], base=0, channel_multiplier=0, allow_small_or_imprecise_dtypes=True))
            order(g.iota(tok_id[:, 0:T], pattern=[[P, T]], base=0, channel_multiplier=1))
            order(g.memset(zero_i, 0))
            note(pool, consts)
            pool.dma_start(slot_dram.rearrange("(p b) o -> p (b o)", b=NBLK), zero_i).then_inc(tab_zero, 16)

            def rope(R, t, H, src, dst):
                x = src.rearrange("p (h d) -> p h d", h=H)
                o = dst if len(dst.shape) == 3 else dst.rearrange("p (h d) -> p h d", h=H)
                m = rope_p[0:R, 0:H * 64].rearrange("p (h d) -> p h d", h=H)
                order(g.tensor_tensor(o, x, cs[0:R, t, 0:64].unsqueeze(1).to_broadcast([R, H, 64]), ALU.mult))
                for a_, b_ in ((0, 32), (32, 0)):
                    order(g.tensor_tensor(m[:, :, a_:a_ + 32], x[:, :, b_:b_ + 32],
                                          cs[0:R, t, 64 + a_:96 + a_].unsqueeze(1).to_broadcast([R, H, 32]), ALU.mult))
                return g.tensor_tensor(o, o, m, ALU.add)

            for j, s in enumerate(STEPS):
                kind = s[0]
                t = s[1] if len(s) > 1 else 0
                R = ROWS[t] if t < T else 0
                tok = slice(TOK[t], TOK[t] + R) if t < T else None
                if kind == "kv":
                    i = ORDER.index(t)
                    in_sbuf(pool, s)
                    pool.wait_ge(tabs_in, 64)
                    order(rope(R, t, 2, raw[i % 2][0:R, 0:128], kro[0:R, t, :]))
                    note(pool, raw_used)
                    kd_, vd_ = (k_sample[0, 0], v_sample[0, 0]) if t == SAMPLE else (k_prompt[0, 0, tok], v_prompt[0, 0, tok])
                    pool.dma_start(kd_.rearrange("t g n -> t (g n)"), kro[0:R, t, :]).then_inc(out_kv, 16)
                    pool.dma_start(vd_.rearrange("t g n -> t (g n)"), va[0:R, t, :]).then_inc(out_kv, 16)
                elif kind == "qa":
                    i = ORDER.index(t)
                    in_sbuf(pool, s)
                    for gr in range(2):
                        dst = qaro[0:R, t, :].rearrange("p (r g d) -> p g r d", g=2, r=4)[:, gr]
                        order(rope(R, t, 4, raw[(T + i) % 2][0:R, gr * 256:(gr + 1) * 256], dst))
                    note(pool, raw_used)
                elif kind == "rg":
                    i = ORDER.index(t)
                    in_sbuf(pool, s)
                    r = rg[0:R, t, :]
                    order(g.tensor_tensor(r, r, graw[i % 2][0:R, :], ALU.mult))
                    r4 = r.rearrange("p (h n) -> p h n", h=NBH)
                    order(g.tensor_tensor(r4, r4, gout_b[0:R, :].unsqueeze(1).to_broadcast([R, NBH, DV]), ALU.mult))
                    note(pool, raw_used)
                elif kind == "z" and t == 0:
                    filled(pool, j)
                    order(g.memset(gT1[0], 1.0))
                    order(g.memset(gT1[0].rearrange("p (c s) -> p c s", s=32)[:, 0:17:2, 0:1], 0.0))
                    note(pool, gate_mask)
                    pool.wait_ge(masks_made, T)
                    order(g.memset(twork[:, 0:D], 0.0))
                    pool.dma_start(ys_dram[(1 + NE) * P:(1 + NE + NOV) * P, :].rearrange("(b p) n -> p b n", p=P),
                                   twork[:, 0:D].unsqueeze(1).to_broadcast([P, NOV, D])).then_inc(ys_cleared, 16)
                    pool.wait_ge(mod_stored[0], 16 * 8)
                    pool.wait_ge(mod_stored[1], 16 * 8)
                    pool.dma_start(states[4], a["state_gla"][0, 0].rearrange("(j h) d n -> (h d) j n", h=2)).then_inc(state_in, 16)
                elif kind == "gst" and (t, s[2]) in ((3, 1), (SAMPLE, 0)):
                    in_sbuf(pool, s)
                    st, dst = (states[5], gla_sample) if t == SAMPLE else (states[0], gla_prompt)
                    pool.dma_start(dst[0, 0].rearrange("(j h) d n -> (h d) j n", h=2), st).then_inc(out_state, 16)
                elif kind == "catT" and t == 0:
                    for tt in range(T):
                        in_sbuf(pool, ("pv", tt, LAST[tt]))
                        pool.wait_ge(o_done, tt + 1)
                    pool.wait_ge(out_state, 32)
                    pool.wait_ge(ys_cleared, 16)
                    pool.wait_ge(out_kv, 2 * T * 16)
                    pool.wait_ge(out_ki, T * 16)
                    pool.wait_ge(mod_stored[0], 16 * 8)
                    pool.wait_ge(mod_stored[1], 16 * 8)
                    for n, m in enumerate((2, 4, 3)):
                        pool.dma_start(rowP[n], mod_dram[0:1, m * D:(m + 1) * D].to_broadcast([P, D])).then_inc(rows_in, 16)
                        pool.dma_start(rowS[n][0:DEC, :], mod_dram[1:2, m * D:(m + 1) * D].to_broadcast([DEC, D])).then_inc(rows_in, 16)
                    pool.dma_start(gffn_b, a["g_ffn"].to_broadcast([P, D])).then_inc(rows_in, 16)
                    pool.dma_start(br_b, a["b_router"].to_broadcast([P, NE])).then_inc(rows_in, 16)
                    pool.dma_start(wr, a["w_router"][0].rearrange("(k p) n -> p k n", p=P)).then_inc(rows_in, 16)
                    order(g.iota(iota_j, pattern=[[1, NOV], [0, NE]], base=0, channel_multiplier=0,
                                 allow_small_or_imprecise_dtypes=True))
                    note(pool, iota_made)
                    for tt in range(2):
                        pool.dma_start(xin[tt], x_rows(tt)).then_inc(x_again[tt], 16)
                elif kind == "y":
                    pool.wait_ge(x2_made, t + 1)
                    pool.dma_start(x2_dram[tok, :], x2b[t % 2][0:R, :]).then_inc(x2_stored[t % 2], 16)
                    pool.wait_ge(h2_made, t + 1)
                    pool.dma_start(h_dram[tok, :], h2b[t % 2][0:R, :]).then_inc(h2_stored[t % 2], 16)
                    if t + 2 < T:
                        pool.dma_start(xin[t % 2][0:ROWS[t + 2], :], x_rows(t + 2)).then_inc(x_again[t % 2], 16)
            pool.wait_ge(routed, 1)
            pool.wait_ge(tab_zero, 16)
            n = 0
            for t in range(T):
                for k in range(TOPE):
                    c = 4 * t + k
                    g.indirect_dma_start(slot_dram, bass.IndirectOffsetOnAxis(tab_pos[0:ROWS[t], c:c + 1], 0),
                                         tok_id[0:ROWS[t], t:t + 1], None).then_inc(tab_written, 16)
                    n += 1
            pool.wait_ge(tab_written, 16 * n)
            pool.dma_start(slot_tok, slot_dram.rearrange("(p b) o -> p (b o)", b=NBLK)).then_inc(tab_in, 16)
            pool.wait_ge(tab_in, 16)
            for x, y in ((x2_stored[0], 3), (x2_stored[1], 2), (h2_stored[0], 3), (h2_stored[1], 2)):
                pool.wait_ge(x, 16 * y)

            def settle():
                pool.sem_inc(pool_settled, 1)

            def gather(i):
                g.tensor_copy(idx_now, slot_tok[:, bass.ds(i, 1)]).then_inc(idx_copied, 1)
                pool.wait_ge(idx_copied, i + 1)
                settle()
                g.indirect_dma_start(xg, None, h_dram, bass.IndirectOffsetOnAxis(idx_now, 0)).then_inc(gathered, 16)

            def low_part(i, c):
                pool.wait_ge(high_made, 2 * (i * BCH + c) + 2)
                h = slice(SLOT - POOL_PART, SLOT)
                g.tensor_tensor(low(c)[:, h], raw_slot(c)[:, h], high(c)[:, h].bitcast(F32), ALU.subtract).then_inc(split_pool, 1)

            def expert_pool(i):
                pool.wait_ge(bias_in, (i + 1) * 32)
                pool.wait_ge(act_ready, i * 2 + 1)
                settle()
                g.partition_broadcast(bias_b[:, 0:2 * D], brow[:, 0:2 * D])
                pool.wait_ge(ys_ready, i + 1)
                settle()
                g.partition_broadcast(bias_b[:, 2 * D:3 * D], brow[:, 2 * D:3 * D]).then_inc(bias_ready, 1)
                pool.wait_ge(xg_turned, i + 1)
                gather(i + 1)
                for c in range(2, BCH):
                    low_part(i, c)
                for c in range(2):
                    low_part(i + 1, c)

            pool.sem_inc(split_pool, CHUNK0)
            gather(0)
            low_part(0, 0)
            low_part(0, 1)
            with pool.Fori(0, NE) as i:
                expert_pool(i)
            n_over = pool.value_load(over[0:1, NOV:NOV + 1], min_val=0, max_val=NOV)
            with pool.If(n_over > 0):
                with pool.Fori(0, n_over) as jj:
                    expert_pool(jj + NE)
            pool.wait_ge(experts_done, 1)
            for t in range(T):
                R = ROWS[t]
                if t >= NF:
                    pool.wait_ge(f_made, t - NF + 1)
                for k in range(TOPE):
                    c = 4 * t + k
                    g.indirect_dma_start(yg[t % NF][0:R, k * D:(k + 1) * D], None, ys_dram,
                                         bass.IndirectOffsetOnAxis(ys_row[0:R, c:c + 1], 0)).then_inc(fin_y[t % NF], 16)

        @block.tensor
        def _(pe):
            mm, tr = nc.tensor.matmul, nc.tensor.transpose

            def sample_product(j, b, xT, w):
                n = SPAN[STEPS[j][0]]
                for k in range(KD):
                    for q in range(4):
                        last = mm(bank(j, b)[32 * q:32 * q + DEC, 0:n], lhsT=xT[:, k, SEQ:NTOK], rhs=w[:, k, q * n:(q + 1) * n],
                                  start=(k == 0), stop=(k == KD - 1))
                return last

            pe.wait_ge(consts, 2)
            pe.wait_ge(c_silu, 1)
            for j, s in enumerate(STEPS):
                kind = s[0]
                t = s[1] if len(s) > 1 else 0
                R = ROWS[t] if t < T else 0
                tok = slice(TOK[t], TOK[t] + R) if t < T else None
                free_group(pe, j)
                if kind == "c":
                    pe.wait_ge(c_in, 64)
                    tr(bank(j)[:, 0:16], cc[0:16, :], ident[0:16, 0:16])
                    last = tr(bank(j, 1)[:, 0:10], vecs[0:10, :], ident[0:10, 0:10])
                elif kind == "mod":
                    chunk_in(pe, s)
                    if t == 0:
                        in_sbuf(pe, ("c",))
                    w = wslot(CH[s] % FRONT_RING)
                    brow_ = (bmod if t < EARLY_MODS else bmod2)[CH[s] % FRONT_RING]
                    for q in range(4):
                        mm(bank(j)[32 * q:32 * q + 2, 0:P], lhsT=pick2, rhs=brow_[:, q * P:(q + 1) * P], start=True, stop=False)
                    for k in range(KD):
                        for q in range(4):
                            last = mm(bank(j)[32 * q:32 * q + 2, 0:P], lhsT=cT[:, k:16:8], rhs=w[:, k, q * P:(q + 1) * P],
                                      start=False, stop=(k == KD - 1))
                elif kind == "modT":
                    pe.wait_ge(mod_copied, t + 1)
                    for k in range(4):
                        last = tr(bank(j)[:, 2 * k:2 * k + 2], modrow[t % 2][0:2, k * P:(k + 1) * P], ident[0:2, 0:2])
                elif kind == "xT":
                    pe.wait_ge(x_norm, T)
                    for tt in range(T):
                        r = ROWS[tt]
                        dst = bank(j, 1)[:, 0:r] if tt == SAMPLE else bank(j)[:, TOK[tt]:TOK[tt] + r]
                        last = tr(dst, xs5[0:r, tt, t * P:(t + 1) * P], ident[0:r, 0:r])
                elif kind in ("qi", "kv", "qa", "vg", "rg"):
                    chunk_in(pe, (kind, 0))
                    if kind == "qi":
                        in_sbuf(pe, ("xT", KD - 1))
                    n = {"qi": 324, "kv": 256}.get(kind, CW)
                    w = wslot(CH[(kind, 0)] % FRONT_RING)
                    if t == SAMPLE:
                        last = sample_product(j, 0, hT, w)
                    for k in range(KD if t != SAMPLE else 0):
                        last = mm(bank(j)[0:R, 0:n], lhsT=hT[:, k, tok], rhs=w[:, k, 0:n], start=(k == 0), stop=(k == KD - 1))
                elif kind in ("lr", "qkg"):
                    c = ("kv", 0) if kind == "lr" else ("qkg", 0)
                    chunk_in(pe, c)
                    at_, m = (256, 16) if kind == "lr" else (t * P, P)
                    w = wslot(CH[c] % FRONT_RING)
                    for b, lo_, hi_ in ((0, 0, NTOK // 2), (1, NTOK // 2, NTOK)):
                        for k in range(KD):
                            last = mm(bank(j, b)[0:m, 0:hi_ - lo_], lhsT=w[:, k, at_:at_ + m], rhs=hT[:, k, lo_:hi_],
                                      start=(k == 0), stop=(k == KD - 1))
                elif kind == "qiT":
                    pe.wait_ge(qi_roped, ORDER.index(t) + 1)
                    for k in range(2):
                        tr(bank(j)[:, k * R:(k + 1) * R], qro[0:R, t, k * P:(k + 1) * P], ident[0:R, 0:R])
                    for half in range(2):
                        last = mm(bank(j)[64 * half:64 * half + 64, 2 * R:3 * R], lhsT=qro[0:R, t, 256:320],
                                  rhs=ident[0:R, 0:R], start=True, stop=True)
                elif kind == "cacheT":
                    pe.wait_ge(cache_in, 48)
                    for half in range(2):
                        mm(bank(j)[64 * half:64 * half + 64, 0:P], lhsT=ckidx[:, t, :], rhs=ident, start=True, stop=True)
                    last = tr(bank(j, 1)[:, 0:P], ck[:, t, :], ident)
                elif kind in ("idx", "idxnew"):
                    h = s[2]
                    ps = slice(64 * (h % 2), 64 * (h % 2) + 64)
                    keys = kiTs if t == SAMPLE else kiT
                    if h == 0 and kind == "idx":
                        in_sbuf(pe, ("qiT", t))
                        in_sbuf(pe, ("cacheT", 7))
                    spans = [(1024, 1056)] if kind == "idxnew" else \
                        [(x, min(x + 512, min(NKEYS[t], 1024))) for x in range(0, min(NKEYS[t], 1024), 512)]
                    for b, (lo_, hi_) in enumerate(spans):
                        last = mm(bank(j, b)[0:R, 0:hi_ - lo_], lhsT=qiT[ps, h // 2, tok], rhs=keys[ps, lo_:hi_],
                                  start=True, stop=True)
                elif kind == "qaT":
                    pe.wait_ge(raw_used, T + ORDER.index(t) + 1)
                    for k in range(4):
                        tr(bank(j)[:, k * R:(k + 1) * R], qaro[0:R, t, k * P:(k + 1) * P], ident[0:R, 0:R])
                    last = tr(bank(j, 1)[:, 0:R], kro[0:R, t, :], ident[0:R, 0:R])
                elif kind == "z":
                    in_sbuf(pe, ("lr",))
                    pe.wait_ge(tabs_in, 64)
                    for b, lo_, hi_ in ((0, 0, SEQ), (1, SEQ, NTOK)):
                        last = mm(bank(j, b)[:, 0:hi_ - lo_], lhsT=wgate[0:16, t * P:(t + 1) * P], rhs=lrT[0:16, lo_:hi_],
                                  start=True, stop=True)
                elif kind == "kd":
                    pe.wait_ge(gla_made, 8)
                    for x in range(2):
                        last = tr(bank(j)[0:R, x * P:(x + 1) * P], gkd[:, x, tok], ident)
                elif kind == "gs":
                    pe.wait_ge(gla_made, 8)
                    S = min(CHUNK, R)
                    for c in range(R // S):
                        po = slice(c * CHUNK, c * CHUNK + S)
                        kc = slice(TOK[t] + c * CHUNK, TOK[t] + c * CHUNK + S)
                        for h in range(NBH):
                            ps = slice(64 * (h % 2), 64 * (h % 2) + 64)
                            for b in range(S // 32):
                                q0 = TOK[t] + c * CHUNK + 32 * b
                                kk = gk1 if b else gk0
                                col = (h // 2) * 64 + 32 * b
                                last = mm(bank(j, h % 2)[po, col:col + 32], lhsT=kk[ps, h // 2, kc],
                                          rhs=gqA[ps, h // 2, q0:q0 + 32], start=True, stop=True)
                elif kind == "gst":
                    in_sbuf(pe, ("kd", t))
                    S = min(CHUNK, R)
                    ks = slice(s[2] * CHUNK, s[2] * CHUNK + S)
                    for h in range(NBH):
                        last = mm(bank(j)[64 * (h % 2):64 * (h % 2) + 64, (h // 2) * DV:(h // 2 + 1) * DV],
                                  lhsT=kdn[ks, t, h * 64:(h + 1) * 64], rhs=vg[ks, t, h * DV:(h + 1) * DV],
                                  start=True, stop=True)
                elif kind == "gi":
                    if t == SAMPLE:
                        pe.wait_ge(state_in, 16)
                    else:
                        in_sbuf(pe, ("gst", t, 0))
                    S = min(CHUNK, R)
                    for c in range(R // S):
                        po = slice(c * CHUNK, c * CHUNK + S)
                        qc = slice(TOK[t] + c * CHUNK, TOK[t] + c * CHUNK + S)
                        st = states[4] if t == SAMPLE else states[(2 * t + c) % 4]
                        for h in range(NBH):
                            ps = slice(64 * (h % 2), 64 * (h % 2) + 64)
                            last = mm(bank(j, h % 2)[po, (h // 2) * DV:(h // 2 + 1) * DV], lhsT=gqe[ps, h // 2, qc],
                                      rhs=st[ps, h // 2, :], start=True, stop=True)
                elif kind == "go":
                    in_sbuf(pe, ("gs", t))
                    S = min(CHUNK, R)
                    for c in range(R // S):
                        po = slice(c * CHUNK, c * CHUNK + S)
                        for h in range(NBH):
                            col = (h % 2) * 128 + (h // 2) * 64
                            last = mm(bank(j)[po, h * DV:(h + 1) * DV], lhsT=scT[t % 2][po, col:col + S],
                                      rhs=vg[po, t, h * DV:(h + 1) * DV], start=True, stop=True)
                elif kind in ("sc", "scnew"):
                    h = s[2]
                    g0 = 64 * (h if t == SAMPLE else h // 4)
                    ps = slice(g0, g0 + 64)
                    keys, qs = (kTs, qaTs[ps, :]) if t == SAMPLE else (kaT, qaT[ps, h % 4, tok])
                    if h == 0:
                        in_sbuf(pe, ("qaT", t))
                    spans = [(1024, 1056)] if kind == "scnew" else \
                        [(x, min(x + 512, min(NKEYS[t], 1024))) for x in range(0, min(NKEYS[t], 1024), 512)]
                    for b, (lo_, hi_) in enumerate(spans):
                        last = mm(bank(j, b)[:, 0:hi_ - lo_], lhsT=qs, rhs=keys[ps, lo_:hi_],
                                  start=True, stop=True)
                elif kind in ("pT", "pTnew"):
                    u = UNIT[s[1:]]
                    pe.wait_ge(probs_made, u + 1)
                    if kind == "pTnew":
                        last = tr(bank(j)[0:DEC, 0:P], prob[u % 3][:, PAST:PAST + DEC], ident)
                    for x in range(min(NKEYS[t], PAST) // P if kind == "pT" else 0):
                        last = tr(group(j)[:, x * P:(x + 1) * P], prob[u % 3][:, x * P:(x + 1) * P], ident)
                elif kind == "pv":
                    u = UNIT[s[1:]]
                    in_sbuf(pe, ("pT", *s[1:]))
                    nb = min(NKEYS[t], PAST) // P
                    turned_p, val = (pTs[s[2]][0], Vs) if t == SAMPLE else (pT[u % 2], va)
                    for x in range(nb):
                        last = mm(bank(j)[:, 0:P], lhsT=turned_p[:, x * P:(x + 1) * P], rhs=val[:, x, :],
                                  start=(x == 0), stop=(x == nb - 1 and t != SAMPLE))
                    if t == SAMPLE:
                        in_sbuf(pe, ("pTnew", *s[1:]))
                        last = mm(bank(j)[:, 0:P], lhsT=pTs[s[2]][1][0:DEC, :], rhs=Vs[0:DEC, nb, :], start=False, stop=True)
                elif kind == "catT":
                    in_sbuf(pe, ("pv", t, LAST[t]))
                    pe.wait_ge(o_done, t + 1)
                    for k in range(KD):
                        src = catA[0:R, t, k * P:(k + 1) * P] if k < 4 else rg[0:R, t, (k - 4) * P:(k - 3) * P]
                        last = tr(group(j)[:, k * R:(k + 1) * R], src, ident[0:R, 0:R])
                elif kind == "y":
                    in_sbuf(pe, ("catT", t))
                    for n in range(2):
                        chunk_in(pe, ("out", n))
                        w = wslot(CH[("out", n)] % FRONT_RING)
                        if t == SAMPLE:
                            last = sample_product(j, n, catT, w)
                        for k in range(KD if t != SAMPLE else 0):
                            last = mm(bank(j, n)[0:R, :], lhsT=catT[:, k, tok], rhs=w[:, k, :], start=(k == 0), stop=(k == KD - 1))
                elif kind == "hT":
                    pe.wait_ge(h2_made, t + 1)
                    for k in range(KD):
                        last = tr(group(j)[:, k * R:(k + 1) * R], h2b[t % 2][0:R, k * P:(k + 1) * P], ident[0:R, 0:R])
                elif kind == "rt":
                    in_sbuf(pe, ("hT", t))
                    pe.wait_ge(rows_in, ROW_DMAS * 16)
                    for k in range(KD):
                        last = mm(bank(j)[0:R, 0:NE], lhsT=h2T[:, k * R:(k + 1) * R], rhs=wr[:, k, :], start=(k == 0), stop=(k == KD - 1))
                elif kind == "rank":
                    pe.wait_ge(sel_made, T)
                    mm(bank(j)[:, 0:T * NE], lhsT=before, rhs=sel, start=True, stop=False)
                    mm(bank(j)[:, 0:T * NE], lhsT=ones, rhs=sel_before[:, 0:T * NE], start=False, stop=True)
                    last = mm(bank(j)[:, T * NE:(T + 1) * NE], lhsT=ones, rhs=sel_before[:, T * NE:(T + 1) * NE],
                              start=True, stop=True)
                last.then_inc(psum_filled, 1)

            def turn_tokens(i):
                pe.wait_ge(gathered, (i + 1) * 16)
                for k in range(KD):
                    last = tr(psum[:, k // 4, (k % 4) * P:(k % 4 + 1) * P], xg[:, k * P:(k + 1) * P], ident)
                last.then_inc(xg_turned, 1)

            def turn_act(i, half):
                pe.wait_ge(act_ready, i * 2 + half + 2)
                for k in range(4):
                    last = tr(psum[:, 6 + half, k * P:(k + 1) * P], act[:, (4 * half + k) * P:(4 * half + k + 1) * P], ident)
                last.then_inc(act_turned, 1)

            def split_in(i, c):
                pe.wait_ge(split_dve, i * BCH + c + 1 + CHUNK0)
                pe.wait_ge(split_pool, i * BCH + c + 1 + CHUNK0)

            def product(out, x_hi, x_lo, w_hi, w_lo, start, stop):
                mm(out, lhsT=x_hi, rhs=w_hi, start=start, stop=False)
                mm(out, lhsT=x_hi, rhs=w_lo, start=False, stop=False)
                return mm(out, lhsT=x_lo, rhs=w_hi, start=False, stop=stop)

            def down(i, half):
                c = 4 + half
                pe.wait_ge(actT_ready, i * 2 + half + 1)
                split_in(i, c)
                w_hi, w_lo = (x.rearrange("p (k n) -> p k n", k=4) for x in (high(c), low(c)))
                for n in range(2):
                    ns = slice(n * 512, (n + 1) * 512)
                    for k in range(4):
                        last = product(psum[:, 4 + n, :], actT_hi[:, 4 * half + k, :], actT_lo[:, 4 * half + k, :],
                                       w_hi[:, k, ns], w_lo[:, k, ns], half == 0 and k == 0, half == 1 and k == 3)
                last.then_inc(chunk_done, 1)

            def expert_pe(i):
                pe.wait_ge(xgT_ready, i + 1)
                for c in range(4):
                    split_in(i, c)
                    w_hi, w_lo = (x.rearrange("p (k n) -> p k n", k=KD) for x in (high(c), low(c)))
                    for k in range(KD):
                        last = product(psum[:, c, :], xgT_hi[:, k, :], xgT_lo[:, k, :], w_hi[:, k, :], w_lo[:, k, :],
                                       k == 0, k == KD - 1)
                    last.then_inc(chunk_done, 1)
                    if c == 2:
                        turn_act(i, 0)
                turn_tokens(i + 1)
                pe.wait_ge(ys_ready, i + 1)
                down(i, 0)
                turn_act(i, 1)
                down(i, 1)

            in_sbuf(pe, ("rank",))
            in_sbuf(pe, ("rt", T - 1))
            pe.sem_inc(chunk_done, CHUNK0)
            turn_tokens(0)
            with pe.Fori(0, NE) as i:
                expert_pe(i)
            pe.wait_ge(routed, 1)
            n_over = pe.value_load(over[0:1, NOV:NOV + 1], min_val=0, max_val=NOV)
            with pe.If(n_over > 0):
                with pe.Fori(0, n_over) as jj:
                    expert_pe(jj + NE)


INS = ["x_prompt", "x_sample", "cache_k", "cache_v", "cache_kidx", "state_gla", "c_prompt", "c_sample", "w_mod", "b_mod",
       "g_mix", "g_ffn", "w_in", "gla_w_gate", "gla_b_gate", "gla_g_out", "w_out", "w_router", "b_router", "w_gate_up",
       "b_gate_up", "w_down", "b_down", "w_mod_final", "b_mod_final", "g_final"]
OUTS = [(1, SEQ, D), (1, DEC, D), (1, 1, SEQ, 2, HD), (1, 1, SEQ, 2, HD), (1, 1, SEQ, HD), (1, 1, NBH, HD, DV),
        (1, 1, DEC, 2, HD), (1, 1, DEC, 2, HD), (1, 1, DEC, HD), (1, 1, NBH, HD, DV)]


def rope_table(np):
    half = HD // 2
    inv = (10000.0 ** (-np.arange(half, dtype=np.float64) / half)).astype(np.float32)
    pos = np.concatenate([np.arange(SEQ), PAST + np.arange(DEC)]).astype(np.float32)
    ang = (pos[:, None] * inv[None, :]).astype(np.float64)
    return np.concatenate([np.cos(ang), np.cos(ang), -np.sin(ang), np.sin(ang)], 1).astype(np.float32)


def kernel(**inputs):
    import numpy as np
    import concourse.bacc as bacc
    from concourse.bass_utils import run_bass_kernel_spmd

    nc = bacc.Bacc("TRN2", target_bir_lowering=False, num_devices=1)
    arrays, aps = {}, {}
    for name in INS:
        arrays[f"in_{name}"] = np.ascontiguousarray(inputs[name])
    arrays["in_rope"] = rope_table(np)
    for name, x in arrays.items():
        aps[name[3:]] = nc.dram_tensor(name, x.shape, mybir.dt.from_np(x.dtype), kind="ExternalInput").ap()
    outs = [nc.dram_tensor(f"out_{i}", shape, F32, kind="ExternalOutput").ap() for i, shape in enumerate(OUTS)]
    build(nc, aps, outs)
    r = run_bass_kernel_spmd(nc, [arrays], core_ids=[0])
    return tuple(r.results[0][f"out_{i}"] for i in range(len(OUTS)))
```
